# Optimizing a Trainium2 kernel written in Bass

```python
import jax, jax.numpy as jnp
from jax import lax
import numpy as np

D_MODEL = 1024
BATCH = 1
SEQ = 512
DEPTH = 1

MEM_LEN = 256
CONV_WIDTH = D_MODEL // 2
CONV_K = 3
ATT_HEADS = 8
HEAD_DIM = 64
ATT_WIDTH = ATT_HEADS * HEAD_DIM
KV_GROUPS = 2
Q_PER_KV = ATT_HEADS // KV_GROUPS
KV_WIDTH = KV_GROUPS * HEAD_DIM
MIX_WIDTH = CONV_WIDTH + ATT_WIDTH
CMP_BLOCK = 32
CMP_STRIDE = 16
CMP_HIDDEN = 256
SLC_BLOCK = 64
N_SELECT = 16
WINDOW = 512
Q_BLOCK = 128
ROPE_THETA = 10000.0
X_HEADS = 4
X_HEAD_DIM = D_MODEL // X_HEADS
D_FF = -(-8 * D_MODEL // (3 * 256)) * 256
EPS = 1e-6
FORCE = 1e4
W_IN_COLS = 3 * CONV_WIDTH + ATT_WIDTH + 6 * KV_WIDTH + 3 * ATT_HEADS


def rmsnorm(x, g):
    xf = x.astype(jnp.float32)
    y = xf * lax.rsqrt(jnp.mean(xf * xf, axis=-1, keepdims=True) + EPS)
    return (y * g.astype(jnp.float32)).astype(x.dtype)

def rope(x, pos):
    half = HEAD_DIM // 2
    inv = ROPE_THETA ** (-jnp.arange(half, dtype=jnp.float32) / half)
    ang = pos.astype(jnp.float32)[..., None] * inv
    cos = jnp.cos(ang)[:, :, None, :]
    sin = jnp.sin(ang)[:, :, None, :]
    xf = x.astype(jnp.float32)
    x1, x2 = xf[..., :half], xf[..., half:]
    return jnp.concatenate([x1 * cos - x2 * sin, x2 * cos + x1 * sin], axis=-1).astype(x.dtype)

def masked_softmax(s, mask):
    s = jnp.where(mask, s.astype(jnp.float32), -1e30)
    e = jnp.exp(s - jnp.max(s, axis=-1, keepdims=True)) * mask
    return e / jnp.maximum(jnp.sum(e, axis=-1, keepdims=True), 1e-30)

def compress(k, pe, w1, w2, n_cmp):
    b = k.shape[0]
    idx = np.arange(n_cmp)[:, None] * CMP_STRIDE + np.arange(CMP_BLOCK)[None, :]
    blocks = k[:, idx] + pe[None, None, :, None, :]
    flat = blocks.transpose(0, 1, 3, 2, 4).reshape(b, n_cmp, KV_GROUPS, CMP_BLOCK * HEAD_DIM)
    return jax.nn.silu(flat @ w1) @ w2

def short_conv_mixer(bg, cg, xin, conv_w):
    z = cg * xin
    zc = lax.conv_general_dilated(z, conv_w[:, None, :].astype(z.dtype), window_strides=(1,),
                                  padding=((CONV_K - 1, 0),), dimension_numbers=("NWC", "WIO", "NWC"),
                                  feature_group_count=CONV_WIDTH)
    return bg * zc

def nsa_mixer(q, k_cmp_raw, v_cmp_raw, k_slc, v_slc, k_win, v_win, gates, positions,
              pe_kc, w1_kc, w2_kc, pe_vc, w1_vc, w2_vc):
    b, s = q.shape[0], q.shape[1]
    n_cmp = (s - CMP_BLOCK) // CMP_STRIDE + 1
    n_slc = s // SLC_BLOCK
    n_sel = min(N_SELECT, n_slc)
    scale = HEAD_DIM ** -0.5

    q = rope(q, positions)
    cmp_end_np = np.arange(n_cmp) * CMP_STRIDE + CMP_BLOCK - 1
    cmp_end = jnp.asarray(cmp_end_np, dtype=jnp.int32)
    k_cmp = rope(compress(k_cmp_raw, pe_kc, w1_kc, w2_kc, n_cmp), positions[:, cmp_end_np])
    v_cmp = compress(v_cmp_raw, pe_vc, w1_vc, w2_vc, n_cmp)

    ci = np.arange(n_cmp)[:, None] * CMP_STRIDE
    sj = np.arange(n_slc)[None, :] * SLC_BLOCK
    ov = np.clip(np.minimum(ci + CMP_BLOCK, sj + SLC_BLOCK) - np.maximum(ci, sj), 0, None)
    slc_map = jnp.asarray(ov / CMP_BLOCK, dtype=jnp.float32)

    k_blocks = rope(k_slc, positions).reshape(b, n_slc, SLC_BLOCK, KV_GROUPS, HEAD_DIM).transpose(0, 3, 1, 2, 4)
    v_blocks = v_slc.reshape(b, n_slc, SLC_BLOCK, KV_GROUPS, HEAD_DIM).transpose(0, 3, 1, 2, 4)
    pad = ((0, 0), (WINDOW, 0), (0, 0), (0, 0))
    k_win_pad = jnp.pad(rope(k_win, positions), pad)
    v_win_pad = jnp.pad(v_win, pad)
    bi = jnp.arange(b)[:, None, None, None]
    gi = jnp.arange(KV_GROUPS)[None, :, None, None]
    blk = jnp.arange(n_slc)

    def block(i):
        s0 = i * Q_BLOCK
        t = s0 + jnp.arange(Q_BLOCK)
        qb = lax.dynamic_slice_in_dim(q, s0, Q_BLOCK, axis=1).reshape(b, Q_BLOCK, KV_GROUPS, Q_PER_KV, HEAD_DIM)
        gb = lax.dynamic_slice_in_dim(gates, s0, Q_BLOCK, axis=1).reshape(b, Q_BLOCK, KV_GROUPS, Q_PER_KV, 3)

        s_c = jnp.einsum("bqgrd,bkgd->bgrqk", qb, k_cmp) * scale
        p_c = masked_softmax(s_c, cmp_end[None, :] <= t[:, None])
        o_c = jnp.einsum("bgrqk,bkgd->bqgrd", p_c, v_cmp)

        imp = jnp.einsum("bgrqk,ks->bgqs", p_c, slc_map)
        cur = t // SLC_BLOCK
        forced = (blk[None, :] == 0) | (blk[None, :] == cur[:, None]) | (blk[None, :] == cur[:, None] - 1)
        future = blk[None, :] * SLC_BLOCK > t[:, None]
        imp = jnp.where(forced, FORCE, jnp.where(future, -FORCE, imp))
        _, sel = lax.top_k(imp, n_sel)
        ks = k_blocks[bi, gi, sel].reshape(b, KV_GROUPS, Q_BLOCK, n_sel * SLC_BLOCK, HEAD_DIM)
        vs = v_blocks[bi, gi, sel].reshape(b, KV_GROUPS, Q_BLOCK, n_sel * SLC_BLOCK, HEAD_DIM)
        kpos = (sel[..., None] * SLC_BLOCK + jnp.arange(SLC_BLOCK)).reshape(b, KV_GROUPS, Q_BLOCK, n_sel * SLC_BLOCK)
        s_s = jnp.einsum("bqgrd,bgqkd->bgrqk", qb, ks) * scale
        p_s = masked_softmax(s_s, (kpos <= t[None, None, :, None])[:, :, None])
        o_s = jnp.einsum("bgrqk,bgqkd->bqgrd", p_s, vs)

        kw = lax.dynamic_slice_in_dim(k_win_pad, s0, Q_BLOCK + WINDOW, axis=1)
        vw = lax.dynamic_slice_in_dim(v_win_pad, s0, Q_BLOCK + WINDOW, axis=1)
        wpos = s0 - WINDOW + jnp.arange(Q_BLOCK + WINDOW)
        mask_w = (wpos[None, :] <= t[:, None]) & (wpos[None, :] > t[:, None] - WINDOW) & (wpos[None, :] >= 0)
        s_w = jnp.einsum("bqgrd,bkgd->bgrqk", qb, kw) * scale
        p_w = masked_softmax(s_w, mask_w)
        o_w = jnp.einsum("bgrqk,bkgd->bqgrd", p_w, vw)

        o = gb[..., 0:1] * o_c + gb[..., 1:2] * o_s + gb[..., 2:3] * o_w
        return o.reshape(b, Q_BLOCK, ATT_WIDTH).astype(q.dtype)

    out = lax.map(block, jnp.arange(s // Q_BLOCK))
    return out.transpose(1, 0, 2, 3).reshape(b, s, ATT_WIDTH)

def first_inputs(seed: int = 0) -> dict:
    key = jax.random.key(seed)
    ks = jax.random.split(key, 32)

    def w(k, shape, fan_in):
        return jax.random.normal(k, shape, jnp.float32) * fan_in ** -0.5

    def gain(k, n):
        return 1.0 + 0.05 * jax.random.normal(k, (n,), jnp.float32)

    offs = jax.random.randint(ks[2], (BATCH, 1), 0, 2048, dtype=jnp.int32)
    return {
        "x": jax.random.normal(ks[0], (BATCH, SEQ, D_MODEL), jnp.float32),
        "mem": jax.random.normal(ks[1], (BATCH, MEM_LEN, D_MODEL), jnp.float32),
        "positions": jnp.arange(SEQ, dtype=jnp.int32)[None, :] + offs,
        "norm_mix_pre": gain(ks[3], D_MODEL),
        "w_in": w(ks[4], (D_MODEL, W_IN_COLS), D_MODEL),
        "conv_w": w(ks[5], (CONV_K, CONV_WIDTH), CONV_K),
        "pe_kc": 0.1 * jax.random.normal(ks[6], (CMP_BLOCK, HEAD_DIM), jnp.float32),
        "w1_kc": w(ks[7], (CMP_BLOCK * HEAD_DIM, CMP_HIDDEN), CMP_BLOCK * HEAD_DIM),
        "w2_kc": w(ks[8], (CMP_HIDDEN, HEAD_DIM), CMP_HIDDEN),
        "pe_vc": 0.1 * jax.random.normal(ks[9], (CMP_BLOCK, HEAD_DIM), jnp.float32),
        "w1_vc": w(ks[10], (CMP_BLOCK * HEAD_DIM, CMP_HIDDEN), CMP_BLOCK * HEAD_DIM),
        "w2_vc": w(ks[11], (CMP_HIDDEN, HEAD_DIM), CMP_HIDDEN),
        "norm_conv_out": gain(ks[12], CONV_WIDTH),
        "norm_attn_out": gain(ks[13], ATT_WIDTH),
        "w_out": w(ks[14], (MIX_WIDTH, D_MODEL), MIX_WIDTH),
        "norm_mix_post": gain(ks[15], D_MODEL),
        "norm_x_pre": gain(ks[16], D_MODEL),
        "norm_mem": gain(ks[17], D_MODEL),
        "w_q_x": w(ks[18], (D_MODEL, D_MODEL), D_MODEL),
        "w_kv_x": w(ks[19], (D_MODEL, 2 * D_MODEL), D_MODEL),
        "w_o_x": w(ks[20], (D_MODEL, D_MODEL), D_MODEL),
        "norm_x_post": gain(ks[21], D_MODEL),
        "norm_ffn_pre": gain(ks[22], D_MODEL),
        "w_gate_up": w(ks[23], (D_MODEL, 2 * D_FF), D_MODEL),
        "w_down": w(ks[24], (D_FF, D_MODEL), D_FF),
        "norm_ffn_post": gain(ks[25], D_MODEL),
    }

def first_block(x, mem, positions, norm_mix_pre, w_in, conv_w, pe_kc, w1_kc, w2_kc, pe_vc, w1_vc, w2_vc,
              norm_conv_out, norm_attn_out, w_out, norm_mix_post, norm_x_pre, norm_mem, w_q_x, w_kv_x,
              w_o_x, norm_x_post, norm_ffn_pre, w_gate_up, w_down, norm_ffn_post):
    b, s, _ = x.shape
    h = x
    for _layer in range(DEPTH):
        u = rmsnorm(h, norm_mix_pre)
        proj = u @ w_in
        cuts = np.cumsum([CONV_WIDTH, CONV_WIDTH, CONV_WIDTH, ATT_WIDTH] + [KV_WIDTH] * 6)
        bg, cg, xin, q, kc, vc, ksl, vsl, kw, vw, gl = jnp.split(proj, cuts, axis=-1)
        kv_shape = (b, s, KV_GROUPS, HEAD_DIM)
        y_conv = short_conv_mixer(bg, cg, xin, conv_w)
        y_att = nsa_mixer(q.reshape(b, s, ATT_HEADS, HEAD_DIM), kc.reshape(kv_shape), vc.reshape(kv_shape),
                          ksl.reshape(kv_shape), vsl.reshape(kv_shape), kw.reshape(kv_shape), vw.reshape(kv_shape),
                          jax.nn.sigmoid(gl).reshape(b, s, ATT_HEADS, 3), positions,
                          pe_kc, w1_kc, w2_kc, pe_vc, w1_vc, w2_vc)
        mixed = jnp.concatenate([rmsnorm(y_conv, norm_conv_out), rmsnorm(y_att, norm_attn_out)], axis=-1)
        h = h + rmsnorm(mixed @ w_out, norm_mix_post)

        hn = rmsnorm(h, norm_x_pre)
        mn = rmsnorm(mem, norm_mem)
        qx = (hn @ w_q_x).reshape(b, s, X_HEADS, X_HEAD_DIM)
        kx, vx = jnp.split(mn @ w_kv_x, 2, axis=-1)
        kx = kx.reshape(b, MEM_LEN, X_HEADS, X_HEAD_DIM)
        vx = vx.reshape(b, MEM_LEN, X_HEADS, X_HEAD_DIM)
        sx = jnp.einsum("bshd,bmhd->bhsm", qx, kx).astype(jnp.float32) * X_HEAD_DIM ** -0.5
        px = jax.nn.softmax(sx, axis=-1)
        ox = jnp.einsum("bhsm,bmhd->bshd", px, vx).astype(h.dtype).reshape(b, s, D_MODEL)
        h = h + rmsnorm(ox @ w_o_x, norm_x_post)

        hn = rmsnorm(h, norm_ffn_pre)
        g, up = jnp.split(hn @ w_gate_up, 2, axis=-1)
        h = h + rmsnorm((jax.nn.silu(g) * up) @ w_down, norm_ffn_post)
    return h


GRID_W = 64
MEM_TOKENS = 256
MLSTM_HEADS = 4
MLSTM_QK_DIM = 64
MLSTM_V_DIM = 128
MLSTM_CHUNK = 64
MLSTM_CONV = 5
NA_HEADS = 8
NA_HEAD_DIM = 32
NA_WIN_ROWS = 8
NA_WIN_COLS = 16
MEM_HEADS = 4
MEM_HEAD_DIM = 64
N_BRANCH = 3
D_FF_2 = 4 * D_MODEL

MLSTM_QK_W = MLSTM_HEADS * MLSTM_QK_DIM
MLSTM_V_W = MLSTM_HEADS * MLSTM_V_DIM
NA_W = NA_HEADS * NA_HEAD_DIM
MEM_W = MEM_HEADS * MEM_HEAD_DIM
IN_SPLITS = (2 * MLSTM_QK_W, MLSTM_V_W, MLSTM_V_W, 2 * MLSTM_HEADS, 2 * MLSTM_HEADS,
             3 * NA_W, MEM_W, N_BRANCH * D_MODEL)
D_IN = sum(IN_SPLITS)


def rmsnorm_2(x, g):
    xf = x.astype(jnp.float32)
    y = xf * lax.rsqrt(jnp.mean(xf * xf, axis=-1, keepdims=True) + EPS)
    return (y * g.astype(jnp.float32)).astype(x.dtype)

def short_conv(x, w, b):
    c = x.shape[-1]
    y = lax.conv_general_dilated(
        x, w[:, None, :].astype(x.dtype), window_strides=(1,),
        padding=[(MLSTM_CONV // 2, MLSTM_CONV // 2)],
        dimension_numbers=('NWC', 'WIO', 'NWC'), feature_group_count=c)
    return y + b.astype(x.dtype)

def _mlstm_chunk_step(carry, inp):
    c_st, n_st, m_st = carry
    q, k, v, ig, lf = inp
    L = q.shape[-2]
    tril = jnp.tril(jnp.ones((L, L), dtype=bool))
    b = jnp.cumsum(lf, axis=-1)
    d_log = jnp.where(tril, b[..., :, None] - b[..., None, :] + ig[..., None, :], -jnp.inf)
    inter = b + m_st[..., None]
    m_t = jnp.maximum(inter, jnp.max(d_log, axis=-1))
    s = jnp.einsum('bhtd,bhsd->bhts', q, k) * jnp.exp(d_log - m_t[..., None])
    w_inter = jnp.exp(inter - m_t)
    num = (jnp.einsum('bhts,bhsv->bhtv', s, v)
           + w_inter[..., None] * jnp.einsum('bhvd,bhtd->bhtv', c_st, q))
    den = jnp.sum(s, axis=-1) + w_inter * jnp.einsum('bhd,bhtd->bht', n_st, q)
    h = num / jnp.maximum(jnp.abs(den), jnp.exp(-m_t))[..., None]
    b_last = b[..., -1]
    w_log = b_last[..., None] - b + ig
    m_new = jnp.maximum(b_last + m_st, jnp.max(w_log, axis=-1))
    decay = jnp.exp(b_last + m_st - m_new)
    ws = jnp.exp(w_log - m_new[..., None])
    c_new = decay[..., None, None] * c_st + jnp.einsum('bhs,bhsv,bhsd->bhvd', ws, v, k)
    n_new = decay[..., None] * n_st + jnp.einsum('bhs,bhsd->bhd', ws, k)
    return (c_new, n_new, m_new), h

def mlstm_chunkwise(q, k, v, ig, lf):
    bsz, s, nh, dk = q.shape
    dv = v.shape[-1]
    nc = s // MLSTM_CHUNK

    def chunks(a):
        a = a.reshape((bsz, nc, MLSTM_CHUNK, nh) + a.shape[3:])
        return jnp.swapaxes(jnp.moveaxis(a, 1, 0), 2, 3)

    init = (jnp.zeros((bsz, nh, dv, dk), jnp.float32),
            jnp.zeros((bsz, nh, dk), jnp.float32),
            jnp.full((bsz, nh), -jnp.inf, jnp.float32))
    _, hs = lax.scan(_mlstm_chunk_step, init,
                     (chunks(q), chunks(k), chunks(v), chunks(ig), chunks(lf)))
    return jnp.swapaxes(jnp.moveaxis(hs, 0, 1), 2, 3).reshape(bsz, s, nh, dv)

def neighbourhood_attention(q, k, v, rpb):
    bsz, s, nh, dh = q.shape
    rows = s // GRID_W
    win_r = min(NA_WIN_ROWS, rows)
    grid = lambda a: a.reshape(bsz, rows, GRID_W, nh, dh)
    qg, kg, vg = grid(q), grid(k), grid(v)
    row_start = jnp.clip(jnp.arange(rows) - win_r // 2, 0, rows - win_r)
    cols = jnp.arange(GRID_W)
    col_idx = (jnp.clip(cols - NA_WIN_COLS // 2, 0, GRID_W - NA_WIN_COLS)[:, None]
               + jnp.arange(NA_WIN_COLS))
    col_off = col_idx - cols[:, None] + (NA_WIN_COLS - 1)

    def one_row(r):
        rs = row_start[r]
        q_row = lax.dynamic_index_in_dim(qg, r, axis=1, keepdims=False)
        k_win = lax.dynamic_slice_in_dim(kg, rs, win_r, axis=1)[:, :, col_idx]
        v_win = lax.dynamic_slice_in_dim(vg, rs, win_r, axis=1)[:, :, col_idx]
        row_off = rs + jnp.arange(win_r) - r + (NA_WIN_ROWS - 1)
        bias = rpb[:, row_off[None, :, None], col_off[:, None, :]]
        sc = (jnp.einsum('bchd,bicjhd->bhcij', q_row, k_win).astype(jnp.float32)
              + bias.astype(jnp.float32)[None])
        p = jax.nn.softmax(sc.reshape(bsz, nh, GRID_W, win_r * NA_WIN_COLS), axis=-1)
        p = p.reshape(sc.shape).astype(v.dtype)
        return jnp.einsum('bhcij,bicjhd->bchd', p, v_win)

    out = lax.map(one_row, jnp.arange(rows))
    return jnp.moveaxis(out, 0, 1).reshape(bsz, s, nh * dh)

def memory_cross_attention(q, mem_n, w_mem_kv, g_mem_q, g_mem_k):
    bsz, s, _ = q.shape
    m = mem_n.shape[1]
    k, v = jnp.split(mem_n @ w_mem_kv, 2, axis=-1)
    q = rmsnorm_2(q.reshape(bsz, s, MEM_HEADS, MEM_HEAD_DIM), g_mem_q) * (MEM_HEAD_DIM ** -0.5)
    k = rmsnorm_2(k.reshape(bsz, m, MEM_HEADS, MEM_HEAD_DIM), g_mem_k)
    v = v.reshape(bsz, m, MEM_HEADS, MEM_HEAD_DIM)
    sc = jnp.einsum('bshd,bmhd->bhsm', q, k).astype(jnp.float32)
    p = jax.nn.softmax(sc, axis=-1).astype(v.dtype)
    return jnp.einsum('bhsm,bmhd->bshd', p, v).reshape(bsz, s, MEM_W)

def hybrid_layer(x, mem, g_mix, w_in, conv_w, conv_b, b_igate, b_fgate, g_mlstm, w_proj_mlstm,
                 g_na_q, g_na_k, rpb, w_proj_na, g_mem, w_mem_kv, g_mem_q, g_mem_k,
                 w_proj_mem, w_out, g_ffn, w_up, w_down):
    bsz, s, _ = x.shape
    h = rmsnorm_2(x, g_mix)
    z = h @ w_in
    split_idx = np.cumsum(np.array(IN_SPLITS))[:-1]
    qk_m, v_m, o_m, i_pre, f_pre, qkv_na, q_mem, gate_pre = jnp.split(z, split_idx, axis=-1)

    qk_m = jax.nn.silu(short_conv(qk_m, conv_w, conv_b))
    q_m, k_m = jnp.split(qk_m, 2, axis=-1)
    q_m = q_m.reshape(bsz, s, MLSTM_HEADS, MLSTM_QK_DIM).astype(jnp.float32) * (MLSTM_QK_DIM ** -0.5)
    k_m = k_m.reshape(bsz, s, MLSTM_HEADS, MLSTM_QK_DIM).astype(jnp.float32)
    vv = v_m.reshape(bsz, s, MLSTM_HEADS, MLSTM_V_DIM).astype(jnp.float32)
    i_log = i_pre.reshape(bsz, s, 2, MLSTM_HEADS).astype(jnp.float32) + b_igate.astype(jnp.float32)
    f_log = jax.nn.log_sigmoid(f_pre.reshape(bsz, s, 2, MLSTM_HEADS).astype(jnp.float32)
                               + b_fgate.astype(jnp.float32))
    flip = lambda a: jnp.flip(a, axis=1)
    h_fwd = mlstm_chunkwise(q_m, k_m, vv, i_log[:, :, 0], f_log[:, :, 0])
    h_bwd = flip(mlstm_chunkwise(flip(q_m), flip(k_m), flip(vv),
                                 flip(i_log[:, :, 1]), flip(f_log[:, :, 1])))
    h_m = rmsnorm_2(h_fwd + h_bwd, g_mlstm.reshape(MLSTM_HEADS, MLSTM_V_DIM))
    h_m = (h_m.reshape(bsz, s, MLSTM_V_W) * jax.nn.sigmoid(o_m.astype(jnp.float32))).astype(x.dtype)

    q_na, k_na, v_na = jnp.split(qkv_na.reshape(bsz, s, 3, NA_HEADS, NA_HEAD_DIM), 3, axis=2)
    q_na = rmsnorm_2(q_na[:, :, 0], g_na_q) * (NA_HEAD_DIM ** -0.5)
    k_na = rmsnorm_2(k_na[:, :, 0], g_na_k)
    h_na = neighbourhood_attention(q_na, k_na, v_na[:, :, 0], rpb)

    h_mem = memory_cross_attention(q_mem, rmsnorm_2(mem, g_mem), w_mem_kv, g_mem_q, g_mem_k)

    gates = jax.nn.sigmoid(gate_pre).reshape(bsz, s, N_BRANCH, D_MODEL)
    y = (gates[:, :, 0] * (h_m @ w_proj_mlstm)
         + gates[:, :, 1] * (h_na @ w_proj_na)
         + gates[:, :, 2] * (h_mem @ w_proj_mem))
    x = x + y @ w_out

    u = rmsnorm_2(x, g_ffn) @ w_up
    return x + jnp.square(jax.nn.relu(u)) @ w_down

def second_inputs(seed: int = 0) -> dict:
    key = jax.random.key(seed)
    ks = jax.random.split(key, 24)
    nrm = lambda k, shape, scale: jax.random.normal(k, shape, jnp.float32) * scale
    gain = lambda k, shape: 1.0 + 0.1 * jax.random.normal(k, shape, jnp.float32)
    L = DEPTH
    f_bias = (jnp.linspace(3.0, 6.0, MLSTM_HEADS, dtype=jnp.float32)[None, None, :]
              + nrm(ks[8], (L, 2, MLSTM_HEADS), 0.1))
    return {
        'x': nrm(ks[0], (BATCH, SEQ, D_MODEL), 1.0),
        'mem': nrm(ks[1], (BATCH, MEM_TOKENS, D_MODEL), 1.0),
        'g_mix': gain(ks[2], (L, D_MODEL)),
        'w_in': nrm(ks[3], (L, D_MODEL, D_IN), D_MODEL ** -0.5),
        'conv_w': nrm(ks[4], (L, MLSTM_CONV, 2 * MLSTM_QK_W), MLSTM_CONV ** -0.5),
        'conv_b': nrm(ks[5], (L, 2 * MLSTM_QK_W), 0.02),
        'b_igate': nrm(ks[6], (L, 2, MLSTM_HEADS), 0.1),
        'b_fgate': f_bias,
        'g_mlstm': gain(ks[7], (L, MLSTM_V_W)),
        'w_proj_mlstm': nrm(ks[9], (L, MLSTM_V_W, D_MODEL), MLSTM_V_W ** -0.5),
        'g_na_q': gain(ks[10], (L, NA_HEAD_DIM)),
        'g_na_k': gain(ks[11], (L, NA_HEAD_DIM)),
        'rpb': nrm(ks[12], (L, NA_HEADS, 2 * NA_WIN_ROWS - 1, 2 * NA_WIN_COLS - 1), 0.1),
        'w_proj_na': nrm(ks[13], (L, NA_W, D_MODEL), NA_W ** -0.5),
        'g_mem': gain(ks[14], (L, D_MODEL)),
        'w_mem_kv': nrm(ks[15], (L, D_MODEL, 2 * MEM_W), D_MODEL ** -0.5),
        'g_mem_q': gain(ks[16], (L, MEM_HEAD_DIM)),
        'g_mem_k': gain(ks[17], (L, MEM_HEAD_DIM)),
        'w_proj_mem': nrm(ks[18], (L, MEM_W, D_MODEL), MEM_W ** -0.5),
        'w_out': nrm(ks[19], (L, D_MODEL, D_MODEL), D_MODEL ** -0.5),
        'g_ffn': gain(ks[20], (L, D_MODEL)),
        'w_up': nrm(ks[21], (L, D_MODEL, D_FF_2), D_MODEL ** -0.5),
        'w_down': nrm(ks[22], (L, D_FF_2, D_MODEL), D_FF_2 ** -0.5),
    }

def second_block(x, mem, g_mix, w_in, conv_w, conv_b, b_igate, b_fgate, g_mlstm, w_proj_mlstm,
              g_na_q, g_na_k, rpb, w_proj_na, g_mem, w_mem_kv, g_mem_q, g_mem_k,
              w_proj_mem, w_out, g_ffn, w_up, w_down):
    for l in range(DEPTH):
        x = hybrid_layer(x, mem, g_mix[l], w_in[l], conv_w[l], conv_b[l], b_igate[l], b_fgate[l],
                         g_mlstm[l], w_proj_mlstm[l], g_na_q[l], g_na_k[l], rpb[l], w_proj_na[l],
                         g_mem[l], w_mem_kv[l], g_mem_q[l], g_mem_k[l], w_proj_mem[l], w_out[l],
                         g_ffn[l], w_up[l], w_down[l])
    return x


def setup_inputs(seed=0):
    out = dict(first_inputs(seed))
    for name, value in second_inputs(seed + 1).items():
        if name != "x":
            out[name + "_2"] = value
    return out


def reference(
    x, mem, positions, norm_mix_pre, w_in, conv_w, pe_kc, w1_kc, w2_kc, pe_vc, w1_vc, w2_vc,
    norm_conv_out, norm_attn_out, w_out, norm_mix_post, norm_x_pre, norm_mem, w_q_x, w_kv_x,
    w_o_x, norm_x_post, norm_ffn_pre, w_gate_up, w_down, norm_ffn_post, mem_2, g_mix_2, w_in_2,
    conv_w_2, conv_b_2, b_igate_2, b_fgate_2, g_mlstm_2, w_proj_mlstm_2, g_na_q_2, g_na_k_2,
    rpb_2, w_proj_na_2, g_mem_2, w_mem_kv_2, g_mem_q_2, g_mem_k_2, w_proj_mem_2, w_out_2,
    g_ffn_2, w_up_2, w_down_2,
):
    x = first_block(
        x, mem, positions, norm_mix_pre, w_in, conv_w, pe_kc, w1_kc, w2_kc, pe_vc, w1_vc, w2_vc,
        norm_conv_out, norm_attn_out, w_out, norm_mix_post, norm_x_pre, norm_mem, w_q_x, w_kv_x,
        w_o_x, norm_x_post, norm_ffn_pre, w_gate_up, w_down, norm_ffn_post,
    )
    return second_block(
        x, mem_2, g_mix_2, w_in_2, conv_w_2, conv_b_2, b_igate_2, b_fgate_2, g_mlstm_2,
        w_proj_mlstm_2, g_na_q_2, g_na_k_2, rpb_2, w_proj_na_2, g_mem_2, w_mem_kv_2, g_mem_q_2,
        g_mem_k_2, w_proj_mem_2, w_out_2, g_ffn_2, w_up_2, w_down_2,
    )


_drawn_inputs = setup_inputs


def setup_inputs(seed=0):
    import zlib

    import numpy as np

    out = dict(_drawn_inputs(seed))
    spreads = {}
    factors = {'pe_kc': 4.69,
     'conv_b_2': 8.0,
     'b_igate_2': 40.398,
     'g_mlstm_2': 3.849,
     'g_na_q_2': 8.0,
     'g_na_k_2': 8.0,
     'rpb_2': 48.682,
     'g_mem_2': 8.0,
     'g_mem_q_2': 8.0,
     'g_mem_k_2': 8.0}
    for name, (base, spread) in spreads.items():
        noise = np.random.default_rng([zlib.crc32(name.encode()), seed]).standard_normal(out[name].shape)
        drawn = base * np.exp(spread * noise) if base else spread * noise
        out[name] = __import__('jax').numpy.asarray(drawn.astype(out[name].dtype))
    for name, factor in factors.items():
        out[name] = (out[name] * factor).astype(out[name].dtype)
    return out
```

```python
from contextlib import ExitStack

import numpy as np

import concourse.bass as bass
from concourse import mybir

F32 = mybir.dt.float32
F32R = mybir.dt.float32r
I32 = mybir.dt.int32
ALU = mybir.AluOpType
ACT = mybir.ActivationFunctionType
X = mybir.AxisListType.X

P = 128
D, S, MEM = 1024, 512, 256
KT, ST, MT = D // P, S // P, MEM // P
EPS = 1e-6
HD = 64
GROUPS, PER_GROUP = 2, 4
CMP, CSTRIDE = 32, 16
NCMP = (S - CMP) // CSTRIDE + 1
CHID = 256
XH, XD = 4, 256
FF1, FF2 = 2816, 4096
THETA = 10000.0
NEG = -1e30
MAGIC = 12582912.0
TWO_PI = (6.28125, 0.0019340515136718750, 0.00000125566500146)
CW = 2048
RAW, HL = 3, 2
NH, ND = 8, 32
GW = 64
NWIN = 16
ROFF, COFF = 15, 31
LH, LQ, LV = 4, 64, 128
MH, MD = 4, 64

VECS = [("norm_mix_pre", 8), ("norm_x_pre", 8), ("norm_mem", 8), ("norm_ffn_pre", 8), ("g_mix_2", 8),
        ("g_mem_2", 8), ("g_ffn_2", 8), ("norm_conv_out", 4), ("norm_attn_out", 4), ("g_mlstm_2", 4),
        ("conv_w", 12), ("conv_w_2", 20), ("conv_b_2", 4)]
COL = {}
_n = 0
for _name, _rows in VECS:
    COL[_name] = _n
    _n += _rows
NCOL = _n


class Chunk:

    def __init__(self, group, srcs, kts, cols, split=True):
        self.group, self.srcs, self.kts, self.cols, self.split = group, srcs, kts, cols, split
        self.tiles = []


class Group:

    def __init__(self, name, mode, readers):
        self.name, self.mode, self.readers = name, mode, readers
        self.chunks, self.tiles = [], []


class Plan:

    def __init__(self):
        self.groups, self.chunks, self.tiles = {}, [], []
        self.bank_owner = {}
        self.rank = {"A": 0, "V": 0, "H": 0}

    def tile(self, g):
        n = len(self.tiles)
        bank = n % 4
        before = self.bank_owner.get(bank)
        ranks = {}
        for r in g.readers:
            self.rank[r] += 1
            ranks[r] = self.rank[r]
        self.tiles.append((bank, before, ranks))
        self.bank_owner[bank] = n
        g.tiles.append(n)
        return n

    def chunk(self, g, c):
        c.n = len(self.chunks)
        self.chunks.append(c)
        g.chunks.append(c)

    def group(self, name, mode, readers):
        g = self.groups[name] = Group(name, mode, readers)
        return g

    def columns(self, name, w, cols, readers="A"):
        g = self.group(name, "T", readers)
        for c0 in cols:
            c = Chunk(g, [(0, 8, 0, 256, w[:, c0:c0 + 256])], list(range(8)), 256)
            for m in range(2):
                c.tiles.append((self.tile(g), True, True, m, list(range(8))))
            self.chunk(g, c)

    def rows(self, name, w, c0, halves, ntok, readers="A", k0=0, kts=8):
        g = self.group(name, "N", readers)
        for half in range(halves):
            tiles = [self.tile(g) for _ in range(ntok)]
            ks = list(range(kts))
            parts = [ks[i:i + 4] for i in range(0, kts, 4)]
            for i, part in enumerate(parts):
                r0 = (k0 + part[0]) * P
                src = w[r0:r0 + len(part) * P, c0 + 512 * half:c0 + 512 * half + 512]
                c = Chunk(g, [(0, len(part), 0, 512, src)], part, 512)
                for j, n in enumerate(tiles):
                    c.tiles.append((n, i == 0, i == len(parts) - 1, j, part))
                self.chunk(g, c)


def make_plan(a):
    p = Plan()
    w_in = a["w_in"]
    p.rows("q", w_in, 1536, 1, 4)
    p.rows("kv", w_in, 2304, 1, 4)
    p.columns("kcvc", w_in, [2048], readers="V")
    g = p.group("gates", "G", "A")
    c = Chunk(g, [(0, 8, 0, 24, w_in[:, 2816:2840])], list(range(8)), 24)
    c.tiles.append((p.tile(g), True, True, 0, list(range(8))))
    p.chunk(g, c)
    p.columns("bg", w_in, [0, 256])
    p.columns("cg", w_in, [512, 768])
    p.columns("xin", w_in, [1024, 1280], readers="V")
    for name in ("kc", "vc"):
        g = p.group("cmp_" + name, "C", "A")
        tiles = [p.tile(g), p.tile(g)]
        for i in range(4):
            src = a["w1_" + name][i * 512:(i + 1) * 512, :].rearrange("(i d) n -> d i n", d=HD)
            c = Chunk(g, [src], list(range(8)), 256, split=False)
            for m, n in enumerate(tiles):
                c.tiles.append((n, i == 0, i == 3, m, [8 * i + k for k in range(8)]))
            p.chunk(g, c)
    p.rows("out", a["w_out"], 0, 2, 4)
    p.columns("kx", a["w_kv_x"], [0, 256, 512, 768])
    p.rows("vx", a["w_kv_x"], 1024, 2, 2)
    p.columns("qx", a["w_q_x"], [0, 256, 512, 768])
    p.rows("ox", a["w_o_x"], 0, 2, 4)
    for s, (k0, n) in enumerate(((0, 8), (8, 8), (16, 6))):
        g = p.group(f"gu{s}", "T", "A")
        for k in range(k0, k0 + n):
            c = Chunk(g, [(0, 8, 0, 128, a["w_gate_up"][:, k * P:(k + 1) * P]),
                          (0, 8, 128, 256, a["w_gate_up"][:, FF1 + k * P:FF1 + (k + 1) * P])],
                      list(range(8)), 256)
            g.readers = "A"
            c.tiles.append((p.tile(g), True, True, 0, list(range(8))))
            g.readers = "H"
            c.tiles.append((p.tile(g), True, True, 1, list(range(8))))
            p.chunk(g, c)
        p.rows(f"down{s}", a["w_down"], 0, 2, 4, k0=k0, kts=n, readers="A" if s == 0 else "V")
    w2 = a["w_in_2"]
    g = p.group("if", "I", "A")
    c = Chunk(g, [(0, 8, 0, 16, w2[:, 1536:1552])], list(range(8)), 128)
    c.tiles.append((p.tile(g), True, True, 0, list(range(8))))
    p.chunk(g, c)
    p.columns("qk2", w2, [0, 256])
    p.rows("memkv", a["w_mem_kv_2"], 0, 1, 2)
    p.rows("v2", w2, 512, 1, 4)
    p.rows("o2", w2, 1024, 1, 4)
    p.rows("naqk", w2, 1552, 1, 4)
    p.rows("navq", w2, 2064, 1, 4)
    for cp in range(4):
        g = p.group(f"gate2_{cp}", "T", "A")
        for b in range(3):
            c0 = 2576 + b * D + cp * 256
            c = Chunk(g, [(0, 8, 0, 256, w2[:, c0:c0 + 256])], list(range(8)), 256)
            for m in range(2):
                c.tiles.append((p.tile(g), True, True, m, list(range(8))))
            p.chunk(g, c)
        g = p.group(f"proj2_{cp}", "T", "V")
        cs = slice(cp * 256, cp * 256 + 256)
        c = Chunk(g, [(0, 4, 0, 256, a["w_proj_mlstm_2"][:, cs]), (4, 6, 0, 256, a["w_proj_na_2"][:, cs]),
                      (6, 8, 0, 256, a["w_proj_mem_2"][:, cs])], list(range(8)), 256)
        for m in range(2):
            for ks in ([0, 1, 2, 3], [4, 5], [6, 7]):
                c.tiles.append((p.tile(g), True, True, m, ks))
        p.chunk(g, c)
    p.rows("out2", a["w_out_2"], 0, 2, 4, readers="V")
    for s in range(4):
        p.columns(f"up{s}", a["w_up_2"], [s * 1024 + 256 * i for i in range(4)])
        p.rows(f"dn{s}", a["w_down_2"], 0, 2, 4, k0=8 * s, readers="V")
    rank = 0
    for c in p.chunks:
        c.ends = c.tiles[-1][2]
        if not c.ends:
            rank += 1
            c.rank = rank
    return p


class Own:

    def __init__(self, eng, chain):
        self.eng, self.chain, self.count = eng, chain, {}

    def tell(self, ins, sem):
        self.count[sem.name] = self.count.get(sem.name, 0) + 1
        ins.then_inc(sem, 1)
        self.eng.wait_ge(sem, self.count[sem.name])

    def link(self, ins):
        self.tell(ins, self.chain)


def norm_tiles():
    out, base = [], 0
    for phase, ntok, banks, kt0, gain in (
            ("x", ST, 2, 0, COL["norm_mix_pre"]), ("mem", MT, 2, 0, COL["norm_mem"]),
            ("att", ST, 1, 4, COL["norm_attn_out"]), ("hx", ST, 2, 0, COL["norm_x_pre"]),
            ("hf", ST, 2, 0, COL["norm_ffn_pre"]), ("h2", ST, 2, 0, COL["g_mix_2"]),
            ("mem2", MT, 2, 0, COL["g_mem_2"]), ("hm", ST, 1, 0, COL["g_mlstm_2"]),
            ("hna", ST, 1, 4, None), ("h4", ST, 2, 0, COL["g_ffn_2"])):
        for j in range(ntok):
            out.append((phase, j, banks, base, kt0, gain))
            base += banks
    return out


def program(nc, a, out):
    plan = make_plan(a)
    G = plan.groups
    NT = norm_tiles()
    ntile = {(t[0], t[1]): i for i, t in enumerate(NT)}
    splits = [c for c in plan.chunks if c.split]
    split_rank = {c.n: i + 1 for i, c in enumerate(splits)}

    with ExitStack() as ctx:
        def sb(name, shape, dt=F32):
            return ctx.enter_context(nc.sbuf_tensor(name, shape, dt))

        def sem(name):
            return ctx.enter_context(nc.semaphore(name))

        h = sb("h", [P, ST, D])
        xTh, xTl = sb("xT_high", [P, KT, S], F32R), sb("xT_low", [P, KT, S], F32R)
        raw = sb("raw", [P, RAW, CW])
        wh, wl = sb("w_high", [P, HL, CW], F32R), sb("w_low", [P, HL, CW], F32R)
        stage = sb("stage", [P, 2, D])
        qbuf = sb("qbuf", [P, 2, S])
        junk = sb("junk", [P, D], mybir.dt.bfloat16)
        ident = sb("ident", [P, P])
        ones = sb("ones", [P, P])
        antident = sb("antident", [P, P])
        gcol = sb("gcol", [P, NCOL])
        rms = sb("rms", [P, 64])
        gates = sb("gates", [P, ST, 24])
        cmask = sb("cmask", [P, ST, NCMP])
        small = sb("small", [P, 96])
        share = sb("share", [P, 512])
        share2 = sb("share2", [P, D])
        eps_col = sb("eps_col", [P, 1])

        rpb_zero = sb("rpb_zero", [1, 64])
        acol = sb("acol", [P, 2, ST, 36])
        arena_bytes = 77888
        arena_at = nc.sbuf_base
        sb("arena", [P, arena_bytes // 4])

        def at(name, off, shape, dt=F32):
            size = 4
            for n in shape[1:]:
                size *= n
            assert off + size <= arena_bytes, name
            return nc.alloc_sbuf_tensor_at(name, shape, dt, offset=arena_at + off)

        zT = at("zT", 0, [P, 4, S + 2])
        bgT = at("bgT", 8256, [P, 4, S])
        memTh, memTl = at("memT_high", 0, [P, KT, MEM], F32R), at("memT_low", 8192, [P, KT, MEM], F32R)
        fk, fv = at("blocks_k", 16448, [HD, CMP, GROUPS * NCMP]), at("blocks_v", 24448, [HD, CMP, GROUPS * NCMP])
        prob = at("prob", 16448, [P, 2, 2, S])
        probT = at("probT", 24640, [P, 2, 2, ST, P])
        kxT, vx = at("kxT", 16448, [P, KT, MEM]), at("vx", 24640, [P, MT, D])
        qT = at("qT", 32832, [P, PER_GROUP, S])
        kT = at("kT", 41024, [P, 2, S])
        kvn = at("kvn", 45120, [P, ST, S])
        ynat = at("ynat", 32832, [P, ST, D])
        qxT = at("qxT", 32832, [P, KT, S])
        yatt = at("yatt", 53312, [P, ST, S])
        qn = at("qn", 53312, [P, 2, S])
        qrot = at("qrot", 57408, [P, 2, S])
        mem_nat = at("mem_nat", 53312, [P, MT, D])
        xprob, xprobT = at("xprob", 53312, [P, 2, MEM]), at("xprobT", 55360, [P, MT, S])
        silu = at("silu", 53312, [P, 2, S])
        o = 61504
        hidk = at("hidk", o, [P, 2, GROUPS * NCMP])
        hidv = at("hidv", o + 512, [P, 2, GROUPS, 4, 32])
        vbd = at("vbd", o + 2560, [P, GROUPS, 4, HD])
        scb = at("scb", o + 4608, [P, 8, NCMP])
        pc = at("pc", o + 5632, [P, 2, 8, 32])
        pcT = at("pcT", o + 7680, [P, 2, P])
        kcn, kcr = at("kcn", o + 8704, [32, P]), at("kcr", o + 9216, [32, P])
        kcT = at("kcT", o + 9728, [P, 32])
        cosT, sinT = at("cosT", o + 9856, [P, 5, HD]), at("sinT", o + 11136, [P, 5, HD])
        w2k, w2v = at("w2k", o + 12416, [P, 2, HD]), at("w2v", o + 12928, [P, 2, HD])
        peT = at("peT", o + 13440, [P, 2, CMP])
        posf = at("posf", o + 13696, [P, 5])
        posi = at("posi", o + 13728, [P, 5], I32)
        invf = at("invf", o + 13760, [P, 32])
        ang = at("ang", 24640, [P, 5, 32])
        angk = at("angk", 25280, [P, 5, 32])
        rows_in = at("rows_in", 25920, [NCOL, P])
        pe_in = at("pe_in", 26560, [CMP, 2, 2, HD])
        rtmp = at("rtmp", o, [P, 2, S])
        hidh, hidl = at("hid_high", 0, [P, 8, S], F32R), at("hid_low", 16384, [P, 8, S], F32R)
        vext = at("vext", 0, [P, ST, LH, LV + 1])
        og = at("og", 8256, [P, ST, S])
        navq = at("navq", 16448, [P, ST, S])
        naT = at("naT", 24640, [P, 4, S])
        qmT, kmT = at("qmT", 32832, [P, 2, S]), at("kmT", 36928, [P, 2, MEM])
        memkv = at("memkv", 38976, [P, MT, S])
        hsum = at("hsum", 43072, [P, ST, S])
        hna = at("hna", 51264, [P, ST, NH * ND])
        gate_rows = at("gate_rows", 43072, [36, 6, S])
        mem_nat2 = at("mem_nat2", 55360, [P, MT, D])
        qkT = at("qkT", 55360, [P, 4, S])
        qkc = at("qkc", 63552, [P, 4, S + 4])
        mem2Th, mem2Tl = at("mem2T_high", 0, [P, KT, MEM], F32R), at("mem2T_low", 8192, [P, KT, MEM], F32R)
        decay = at("decay", 63552, [P, 2, 1280])
        maxb = at("maxb", 73792, [P, 2, S])
        bias2 = at("bias2", 0, [P, 2, 16, GW])
        nprob, nprobT = at("nprob", 63552, [P, 2, S]), at("nprobT", 67648, [P, 2, ST, P])
        mprob, mprobT = at("mprob", 63552, [P, 2, MEM]), at("mprobT", 65600, [P, MT, S])
        hmTh, hmTl = at("hmT_high", 0, [P, KT, S], F32R), at("hmT_low", 16448, [P, KT, S], F32R)
        yTh, yTl = at("yT_high", 32832, [P, KT, S], F32R), at("yT_low", 49216, [P, KT, S], F32R)
        sg = at("sg", 65600, [P, 3, 2, S])

        causal = share
        na_gain = share[:, :].rearrange("p (h d) -> p h d", d=ND)
        gpost = share2
        mem_gain = share2[:, 0:512].rearrange("p (h d) -> p h d", d=MD)
        neg_max = share2[0:36, 512:1024]

        bank = [ctx.enter_context(nc.psum_tensor(f"bank{i}", [P, S], F32)) for i in range(8)]
        TB, SB = (bank[4], bank[5]), (bank[6], bank[7])

        rpb_pad = nc.dram_tensor("rpb_pad", [1, 64 + NH * ROFF * COFF + 64], F32, kind="Internal").ap()

        raw_in = [sem(f"raw_in{i}") for i in range(RAW)]
        wh_done, wl_done, chunk_used = sem("wh_done"), sem("wl_done"), sem("chunk_used")
        dense_done, dense_a, dense_v = sem("dense_done"), sem("dense_evac_act"), sem("dense_evac_dve")
        act_chain, dve_chain, pool_chain = sem("act_chain"), sem("dve_chain"), sem("pool_chain")
        x_in, rows_in_s, pe_in_s, pos_in = sem("x_in"), sem("vectors_in"), sem("pe_in_done"), sem("pos_in")
        w2_in, gpost_in, mem_in, mem2_in = sem("w2_in"), sem("gpost_in"), sem("mem_in"), sem("mem2_in")
        bias_in = [sem("bias_in0"), sem("bias_in1")]
        pad_in, gain2_in, ifb_in = sem("pad_in"), sem("gain2_in"), sem("gate_bias_in")
        pad_zero, const_ready, b2_const = sem("pad_zero"), sem("const_ready"), sem("b2_const")
        rms_done, xn_ready, tr_done = sem("rms_done"), sem("xn_ready"), sem("tr_done")
        q_ready, hi_done, lo_done, h_ready = sem("q_ready"), sem("hi_done"), sem("lo_done"), sem("h_ready")
        vec_tr, vec_col = sem("vec_transposed"), sem("vec_columns")
        qn_in, rot_ready, rot_tr, qkT_ready = sem("qn_in"), sem("rot_ready"), sem("rot_transposed"), sem("qkT_ready")
        rope_ang, rope_sin, rope_ready = sem("rope_angle"), sem("rope_sine"), sem("rope_ready")
        conv_y, conv_sq, conv_ss, conv_rms, conv_q, conv_hi, conv_lo = (
            sem("conv_y"), sem("conv_square"), sem("conv_sum"), sem("conv_rms"), sem("conv_q"),
            sem("conv_hi"), sem("conv_lo"))
        blocks_ready, hid_zero, cmp_kv, cmp_kv_in, kc_rot, kc_tr, kcT_ready = (
            sem("blocks_ready"), sem("hid_zero"), sem("cmp_kv"), sem("cmp_kv_in"), sem("kc_rot"), sem("kc_tr"),
            sem("kcT_ready"))
        c_scores, c_shift, c_exp, c_tr, c_trin, c_out, c_used = (
            sem("c_scores"), sem("c_shifted"), sem("c_exp"), sem("c_tr"), sem("c_tr_in"), sem("c_out"), sem("c_used"))
        s_done, s_taken, s_max, s_exp, pt_done, pt_a, pt_v, pv_done, o_taken = (
            sem("s_done"), sem("s_taken"), sem("s_max"), sem("s_exp"), sem("pt_done"), sem("pt_act"), sem("pt_dve"),
            sem("pv_done"), sem("o_taken"))
        x_scores, x_max, x_exp, x_norm, x_tr, x_pta, x_ptv, x_out, x_hi, x_lo = (
            sem("x_scores"), sem("x_max"), sem("x_exp"), sem("x_norm"), sem("x_tr"), sem("x_pt_act"),
            sem("x_pt_dve"), sem("x_out"), sem("x_hi"), sem("x_lo"))
        hid_q, hid_hi, hid_lo = sem("hid_q"), sem("hid_hi"), sem("hid_lo")
        spread_zero = sem("spread_zero")
        n_raw, n_norm, n_tr, n_in, n_copied = sem("n_raw"), sem("n_norm"), sem("n_tr"), sem("n_ready"), sem("n_copied")
        qk_conv, qk_ready = sem("qk_conv"), sem("qk_ready")
        gr_lin, gr_exp, gr_ln, gr_max, gr_em, gr_tr, gr_col, gr_neg = (
            sem("gr_lin"), sem("gr_exp"), sem("gr_ln"), sem("gr_max"), sem("gr_em"), sem("gr_tr"), sem("gr_col"),
            sem("gr_neg"))
        l_bc, l_bcin, l_scores, l_shift, l_exp, l_mul, l_mask, l_out, l_used = (
            sem("l_bc"), sem("l_bc_in"), sem("l_scores"), sem("l_shift"), sem("l_exp"), sem("l_mul"),
            sem("l_mask"), sem("l_out"), sem("l_used"))
        b_masked, a_scores, a_taken, a_max, a_exp, a_tr, a_pta, a_ptv, a_out = (
            sem("b_masked"), sem("a_scores"), sem("a_taken"), sem("a_max"), sem("a_exp"), sem("a_tr"),
            sem("a_pt_act"), sem("a_pt_dve"), sem("a_out"))
        a_den = sem("a_den")
        m_scores, m_max, m_exp, m_norm, m_tr, m_pta, m_ptv, m_out, m_hi, m_lo = (
            sem("m_scores"), sem("m_max"), sem("m_exp"), sem("m_norm"), sem("m_tr"), sem("m_pt_act"),
            sem("m_pt_dve"), sem("m_out"), sem("m_hi"), sem("m_lo"))
        y_q, y_hi, y_lo, out_done = sem("y_q"), sem("y_hi"), sem("y_lo"), sem("out_done")

        block = ctx.enter_context(nc.Block())

        def evacuated(eng, n):
            for r, rank in plan.tiles[n][2].items():
                eng.wait_ge({"A": dense_a, "V": dense_v, "H": hid_q}[r], rank)

        def tile_bank(n):
            return bank[plan.tiles[n][0]]

        def used(eng, c):
            if c.ends:
                eng.wait_ge(dense_done, c.tiles[-1][0] + 1)
            else:
                eng.wait_ge(chunk_used, c.rank)

        def group_used(eng, name):
            used(eng, G[name].chunks[-1])

        def bc(ap, shape):
            return ap.broadcast_to(shape)

        @block.sync
        def _(sp):
            xv = a["x"].rearrange("(j p) d -> p j d", p=P)
            sp.dma_start(h[:, :, :], xv).then_inc(x_in, 16)
            r = 0
            for name, n in VECS:
                src = a[name]
                src = src.rearrange("(r q) -> r q", q=P) if len(src.shape) == 1 else \
                    src.rearrange("k (r q) -> (k r) q", q=P)
                sp.dma_start(rows_in[r:r + n, :], src).then_inc(rows_in_s, 16)
                r += n
            sp.wait_ge(pad_zero, 1)
            for o in (0, 64 + NH * ROFF * COFF):
                sp.dma_start(rpb_pad[0:1, o:o + 64], rpb_zero[0:1, :]).then_inc(pad_in, 16)
            sp.dma_start(rpb_pad[0:1, 64:64 + NH * ROFF * COFF],
                         a["rpb_2"].rearrange("h r c -> (h r c)").rearrange("(o n) -> o n", o=1)).then_inc(pad_in, 16)
            ps = a["positions"]
            sp.wait_ge(const_ready, 1)
            for j in range(ST):
                sp.dma_start(posi[:, j:j + 1], bass.AP(ps.tensor, j * P, [[1, P], [1, 1]])).then_inc(pos_in, 16)
            sp.dma_start(posi[0:NCMP, 4:5], bass.AP(ps.tensor, CMP - 1, [[CSTRIDE, NCMP], [1, 1]]),
                         allow_slow_non_contiguous=True).then_inc(pos_in, 16)
            for i, n in enumerate(("pe_kc", "pe_vc")):
                for g in range(2):
                    sp.dma_start(pe_in[:, i, g, :], a[n]).then_inc(pe_in_s, 16)
            for t, n in ((w2k, "w2_kc"), (w2v, "w2_vc")):
                sp.dma_start(t[:, :, :], a[n].rearrange("(m p) d -> p m d", p=P)).then_inc(w2_in, 16)

            before = {
                "cmp_kc": lambda: late_mem(),
                "kx": lambda: post_gain("norm_mix_post", None),
                "ox": lambda: post_gain("norm_x_post", ("h", 4)),
                "gu2": lambda: post_gain("norm_ffn_post", ("h", 8)),
                "qk2": lambda: second_block_loads(),
                "proj2_0": lambda: window_bias(),
            }

            def late_mem():
                sp.wait_ge(qkT_ready, 8)
                sp.dma_start(mem_nat[:, :, :], a["mem"].rearrange("(j p) d -> p j d", p=P)).then_inc(mem_in, 16)

            def post_gain(name, after):
                if after:
                    sp.wait_ge(h_ready, after[1])
                sp.dma_start(gpost[:, :], a[name].rearrange("(o d) -> o d", o=1).broadcast_to([P, D]))\
                    .then_inc(gpost_in, 16)

            def second_block_loads():
                sp.wait_ge(h_ready, 12)
                sp.dma_start(mem_nat2[:, :, :], a["mem_2"].rearrange("(j p) d -> p j d", p=P)).then_inc(mem2_in, 16)
                gq = a["g_na_q_2"].rearrange("(o d) -> o d", o=1)
                gk = a["g_na_k_2"].rearrange("(o d) -> o d", o=1)
                for i, g in enumerate((gq, gk)):
                    sp.dma_start(na_gain[:, 8 * i:8 * i + 8, :], bass.AP(g.tensor, 0, [[0, P], [0, 8], [1, ND]]))\
                        .then_inc(gain2_in, 16)
                for i, n in enumerate(("g_mem_q_2", "g_mem_k_2")):
                    sp.dma_start(mem_gain[:, 4 * i:4 * i + 4, :], bass.AP(a[n].tensor, 0, [[0, P], [0, 4], [1, MD]]))\
                        .then_inc(gain2_in, 16)
                for i, n in enumerate(("b_igate_2", "b_fgate_2")):
                    for d in range(2):
                        sp.dma_start(small[32 * d:32 * d + 4, 88 + i:89 + i], a[n][d, :].rearrange("(h o) -> h o", o=1))\
                            .then_inc(ifb_in, 16)

            def window_bias():
                sp.wait_ge(pad_in, 48)
                sp.wait_ge(l_used, 2 * LH)
                for hd in range(NH):
                    if hd >= 2:
                        sp.wait_ge(a_taken, ST * (hd - 1))
                    src = bass.AP(rpb_pad.tensor, 64 + hd * ROFF * COFF + NWIN - GW, [[1, GW], [COFF, ROFF], [1, GW]])
                    for rr in range(2):
                        sp.dma_start(bias2[64 - 64 * rr:P - 64 * rr, hd % 2, rr:rr + ROFF, :], src)\
                            .then_inc(bias_in[hd % 2], 16)

            for c in plan.chunks:
                if c is c.group.chunks[0] and c.group.name in before:
                    before[c.group.name]()
                if c.n >= RAW:
                    old = plan.chunks[c.n - RAW]
                    if old.split:
                        sp.wait_ge(wh_done, split_rank[old.n])
                        sp.wait_ge(wl_done, split_rank[old.n])
                    else:
                        used(sp, old)
                slot = raw[:, c.n % RAW, :]
                if not c.split:
                    sp.dma_start(slot[0:HD, :].rearrange("d (i n) -> d i n", n=CHID), c.srcs[0])\
                        .then_inc(raw_in[c.n % RAW], 16)
                    continue
                for k0, k1, c0, c1, src in c.srcs:
                    width = c.cols if c.group.mode != "I" else 16
                    dst = slot[:, 0:len(c.kts) * width].rearrange("p (k n) -> p k n", n=width)
                    sp.dma_start(dst[:, k0:k1, c0:c1], src.rearrange("(k p) n -> p k n", p=P))\
                        .then_inc(raw_in[c.n % RAW], 16)
            ov = out.rearrange("(j p) d -> p j d", p=P)
            for half in range(2):
                for j in range(ST):
                    evacuated(sp, G["dn3"].tiles[4 * half + j])
                    cs = slice(512 * half, 512 * half + 512)
                    sp.dma_start(ov[:, j, cs], h[:, j, cs]).then_inc(out_done, 16)
            sp.wait_ge(out_done, 16 * 8)

        loaded = {}
        count = [0] * RAW
        for c in plan.chunks:
            count[c.n % RAW] += 16 * len(c.srcs)
            loaded[c.n] = count[c.n % RAW]

        def split_slot(c, t):
            if t is raw:
                slot = raw[:, c.n % RAW, :]
                if c.group.mode == "I":
                    return slot[:, 0:P].rearrange("p (k q e) -> p k q e", q=4, e=4)
            else:
                slot = t[:, (split_rank[c.n] - 1) % HL, :]
                if c.group.mode == "I":
                    return slot[:, 0:8 * P].rearrange("p (k q e) -> p k q e", q=4, e=32)[:, :, :, 0:4]
            return slot[:, 0:len(c.kts) * c.cols]

        @block.gpsimd
        def _(pool):
            own = Own(pool, pool_chain)
            own.link(pool.memset(posi[:, :], 0))
            own.link(pool.memset(small[:, :], 0.0))
            own.tell(pool.memset(eps_col[:, :], EPS), const_ready)
            own.link(pool.memset(ident[:, :], 0.0))
            own.tell(pool.affine_select(out=ident[:, :], in_=ident[:, :], compare_op=ALU.not_equal, fill=1.0,
                                        base=0, pattern=[[-1, P]], channel_multiplier=1), const_ready)
            own.link(pool.memset(ones[:, :], 1.0))
            own.link(pool.memset(antident[:, :], 0.0))
            own.link(pool.affine_select(out=antident[:, :], in_=antident[:, :], compare_op=ALU.not_equal, fill=1.0,
                                        base=1 - P, pattern=[[1, P]], channel_multiplier=1))
            own.link(pool.memset(causal[:, :], 0.0))
            own.link(pool.affine_select(out=causal[:, 384:512], in_=causal[:, 384:512], compare_op=ALU.is_ge,
                                        fill=NEG, base=0, pattern=[[-1, P]], channel_multiplier=1))
            own.link(pool.memset(cmask[:, :, :], 0.0))
            own.link(pool.affine_select(out=cmask[:, :, :], in_=cmask[:, :, :], compare_op=ALU.is_ge, fill=NEG,
                                        base=-(CMP - 1), pattern=[[P, ST], [-CSTRIDE, NCMP]], channel_multiplier=1))
            own.link(pool.memset(small[:, 95:96], 1.0))
            own.link(pool.affine_select(out=small[:, 95:96], in_=small[:, 95:96], compare_op=ALU.is_ge, fill=0.0,
                                        base=-(CMP - 1), pattern=[[0, 1]], channel_multiplier=1))
            for j in range(32):
                own.link(pool.memset(invf[:, j:j + 1], float(np.float32(THETA ** (-j / 32.0)))))
            own.link(pool.memset(zT[:, :, 0:2], 0.0))
            own.tell(pool.memset(pc[:, :, :, :], 0.0), const_ready)
            own.tell(pool.memset(rpb_zero[:, :], 0.0), pad_zero)

            done = [0]

            def low_parts(upto):
                while done[0] < len(splits) and splits[done[0]].n <= upto:
                    c = splits[done[0]]
                    done[0] += 1
                    if c.group.mode == "I":
                        r = (split_rank[c.n] - 1) % HL
                        used(pool, splits[done[0] - 1 - HL])
                        own.link(pool.tensor_copy(wh[:, r, 0:8 * P], bc(small[:, 94:95], [P, 8 * P])))
                        own.tell(pool.tensor_copy(wl[:, r, 0:8 * P], bc(small[:, 94:95], [P, 8 * P])), spread_zero)
                    pool.wait_ge(wh_done, split_rank[c.n])
                    own.tell(pool.tensor_tensor(split_slot(c, wl), split_slot(c, raw), split_slot(c, wh).bitcast(F32),
                                                ALU.subtract), wl_done)

            low_parts(G["xin"].chunks[-1].n)
            pool.wait_ge(qkT_ready, 8)
            own.link(pool.memset(vbd[:, :, :, :], 0.0))
            own.tell(pool.memset(hidv[:, :, :, :, :], 0.0), hid_zero)
            low_parts(G["if"].chunks[-1].n)
            pool.wait_ge(h_ready, 12)
            own.link(pool.memset(qkc[:, :, 0:2], 0.0))
            own.tell(pool.memset(qkc[:, :, S + 2:S + 4], 0.0), b2_const)
            low_parts(G["memkv"].chunks[-1].n)
            group_used(pool, "memkv")
            own.tell(pool.memset(vext[:, :, :, LV:LV + 1], 1.0), b2_const)
            low_parts(G["navq"].chunks[-1].n)
            for it in range(2 * LH):
                d = it // LH
                off = 0
                for si in range(ST):
                    pool.wait_ge(l_mul, ST * it + si + 1)
                    n = (ST - si) * P if d == 0 else (si + 1) * P
                    dg = off if d == 0 else off + si * P
                    blk = decay[:, it % 2, dg:dg + P]
                    own.tell(pool.affine_select(out=blk, in_=blk, compare_op=ALU.is_ge, fill=0.0, base=0,
                                                pattern=[[1 if d == 0 else -1, P]],
                                                channel_multiplier=-1 if d == 0 else 1), l_mask)
                    off += n
            for hd in range(NH):
                pool.wait_ge(bias_in[hd % 2], 32 * (hd // 2 + 1))
                for rr in range(2):
                    ps = slice(64 - 64 * rr, P - 64 * rr)
                    t = bias2[ps, hd % 2, rr:rr + ROFF, :]
                    lo, hi = t[:, :, 0:GW - NWIN], t[:, :, NWIN:GW]
                    own.link(pool.affine_select(out=lo, in_=lo, compare_op=ALU.is_ge, fill=NEG,
                                                base=NWIN // 2 - (GW - 1),
                                                pattern=[[0, ROFF], [1, GW - NWIN]], channel_multiplier=1))
                    own.tell(pool.affine_select(out=hi, in_=hi, compare_op=ALU.is_ge, fill=NEG,
                                                base=NWIN // 2 - 1 - NWIN + GW - 1,
                                                pattern=[[0, ROFF], [-1, GW - NWIN]], channel_multiplier=-1), b_masked)
            low_parts(len(plan.chunks))

        STATS = [("x", j) for j in range(4)] + [("mem", j) for j in range(2)] + [("att", j) for j in range(4)]
        for ph, nx in (("yo", "hx"), ("yx", "hf"), ("yf", "h2")):
            for j in range(4):
                STATS += [(ph, j), (nx, j)]
        STATS += [("mem2", j) for j in range(2)] + [("h4", j) for j in range(4)]

        SOURCES = {"x": h, "hx": h, "hf": h, "h2": h, "h4": h, "mem": mem_nat, "mem2": mem_nat2, "att": yatt}
        TURNED = {"mem": (memTh, memTl), "mem2": (mem2Th, mem2Tl), "hm": (hmTh, hmTl), "hna": (hmTh, hmTl)}

        FREE = {"hx": "out", "hf": "ox", "h2": "gu2", "mem2": "down2", "h4": "gate2_3"}

        def turned(i, b, low):
            phase, j, banks, first, kt0, gain = NT[i]
            t = TURNED.get(phase, (xTh, xTl))[low]
            blocks = 2 if phase == "hna" else 4
            return t[:, kt0 + 4 * b:kt0 + 4 * b + blocks, j * P:(j + 1) * P], blocks

        ITEMS = [(qt, g, t) for qt in range(ST) for g in range(GROUPS) for t in range(PER_GROUP)]
        LSPAN = {0: [(ST - si) * P for si in range(ST)], 1: [(si + 1) * P for si in range(ST)]}

        def span(d, si):
            return sum(LSPAN[d][:si]), LSPAN[d][si], si * P if d == 0 else 0

        @block.scalar
        def _(act):
            own = Own(act, act_chain)
            done = [0]

            def high(upto):
                while done[0] < len(splits) and splits[done[0]].n <= upto:
                    r = done[0]
                    c = splits[r]
                    done[0] += 1
                    act.wait_ge(raw_in[c.n % RAW], loaded[c.n])
                    if r >= HL:
                        used(act, splits[r - HL])
                    if c.group.mode == "I":
                        act.wait_ge(spread_zero, 1)
                    own.tell(act.copy(split_slot(c, wh), split_slot(c, raw)), wh_done)

            def stat(key, src, width):
                i = STATS.index(key)
                r = rms[:, i:i + 1]
                own.link(act.activation(junk[:, 0:width], src, ACT.Square, accum_out=r))
                own.tell(act.activation(r, r, ACT.Sqrt, bias=eps_col[:, 0:1], scale=1.0 / width), rms_done)

            def hi(i):
                if NT[i][0] in FREE:
                    group_used(act, FREE[NT[i][0]])
                for b in range(NT[i][2]):
                    r = NT[i][3] + b
                    dst, n = turned(i, b, 0)
                    act.wait_ge(q_ready, r + 1)
                    own.tell(act.copy(dst, qbuf[:, r % 2, 0:n * P].rearrange("p (k t) -> p k t", k=n)), hi_done)

            def norm(phase, ntok, width):
                for j in range(ntok):
                    src = SOURCES[phase]
                    stat((phase, j), src[:, j, :], width)
                    if j:
                        hi(ntile[phase, j - 1])
                hi(ntile[phase, ntok - 1])

            def evac(group, write, between=None):
                g = G[group]
                for c in g.chunks:
                    high(c.n + 1)
                    for n, first, last, m, ks in c.tiles:
                        if last and "A" in plan.tiles[n][2]:
                            act.wait_ge(dense_done, n + 1)
                            write(g.tiles.index(n), tile_bank(n))
                    if between:
                        between(c)

            act.wait_ge(const_ready, 1)
            act.wait_ge(x_in, 16)
            norm("x", ST, D)
            act.wait_ge(rope_ang, 1)
            own.link(act.activation(sinT[:, :, 32:64], ang[:, :, :], ACT.Sin))
            own.tell(act.activation(angk[:, :, :], ang[:, :, :], ACT.Sin, scale=0.5), rope_sin)

            def q_out(t, src):
                if t >= 2:
                    act.wait_ge(rot_ready, t - 1)
                own.tell(act.copy(qn[:, t % 2, :], src[:, :]), dense_a)
            evac("q", q_out)
            evac("kv", lambda t, src: own.tell(act.copy(kvn[:, t, :], src[:, :]), dense_a))
            evac("kcvc", None)
            evac("gates", lambda t, src: own.tell(
                act.activation(gates[:, :, :], src[:, 0:4 * 24].rearrange("p (j c) -> p j c", j=4), ACT.Sigmoid),
                dense_a))
            evac("bg", lambda t, src: own.tell(act.copy(bgT[:, t, :], src[:, :]), dense_a))
            evac("cg", lambda t, src: own.tell(act.copy(zT[:, t, 2:S + 2], src[:, :]), dense_a))
            evac("xin", None)

            act.wait_ge(qkT_ready, 8)
            act.wait_ge(hid_zero, 1)
            evac("cmp_kc", lambda m, src: own.tell(
                act.activation(hidk[:, m, :], src[:, 0:GROUPS * NCMP], ACT.Silu), dense_a))

            def hidv_out(m, src):
                v = src[:, 0:GROUPS * NCMP].rearrange("p (g j) -> p g j", g=GROUPS)
                for g in range(GROUPS):
                    ins = act.activation(hidv[:, m, g, :, 0:NCMP], bc(v[:, g, None, :], [P, 4, NCMP]), ACT.Silu)
                    own.tell(ins, dense_a) if g == GROUPS - 1 else own.link(ins)
            evac("cmp_vc", hidv_out)

            for ct in range(4):
                act.wait_ge(conv_y, ct + 1)
                own.tell(act.activation(stage[:, ct // 2, (ct % 2) * S:(ct % 2) * S + S], bgT[:, ct, :], ACT.Square),
                         conv_sq)
            act.wait_ge(conv_ss, 1)
            own.tell(act.activation(stage[:, 0, 0:S], SB[1][:, :], ACT.Sqrt, bias=eps_col[:, 0:1],
                                    scale=1.0 / 512), conv_rms)
            group_used(act, "xin")
            for ct in range(4):
                act.wait_ge(conv_q, ct + 1)
                own.tell(act.copy(xTh[:, ct, :], qbuf[:, ct % 2, :]), conv_hi)

            act.wait_ge(mem_in, 16)
            act.wait_ge(conv_lo, 4)
            norm("mem", MT, D)

            for c in range(ST):
                act.wait_ge(c_shift, c + 1)
                if c >= 2:
                    act.wait_ge(c_tr, c - 1)
                own.tell(act.activation(pc[:, c % 2, :, 0:NCMP], scb[:, :, :], ACT.Exp, scale=HD ** -0.5), c_exp)

            for s in range(len(ITEMS) + 1):
                if s < len(ITEMS):
                    n = (ITEMS[s][0] + 1) * P
                    act.wait_ge(s_max, s + 1)
                    for br in range(2):
                        own.tell(act.activation(prob[:, s % 2, br, 0:n], prob[:, s % 2, br, 0:n], ACT.Exp,
                                                bias=small[:, 4 * (s % 2) + br:4 * (s % 2) + br + 1],
                                                scale=HD ** -0.5,
                                                accum_out=small[:, 8 + 2 * (s % 4) + br:9 + 2 * (s % 4) + br]), s_exp)
                if s >= 1:
                    i = s - 1
                    k = ITEMS[i][0] + 1
                    act.wait_ge(pt_done, 2 * i + 1)
                    if i >= 2:
                        act.wait_ge(pv_done, i - 1)
                    own.tell(act.copy(probT[:, i % 2, 0, 0:k, :],
                                      TB[0][:, 0:k * P].rearrange("p (k q) -> p k q", k=k)), pt_a)
            act.wait_ge(o_taken, len(ITEMS))
            norm("att", ST, 512)

            def post(group, yname, hname, src_ready, filler=None):
                g = G[group]
                last = g.tiles[-4:]
                for c in g.chunks:
                    high(c.n + 1)
                    for n, first, lastc, j, ks in c.tiles:
                        if not lastc:
                            continue
                        half = g.tiles.index(n) // 4
                        if "A" in plan.tiles[n][2]:
                            act.wait_ge(dense_done, n + 1)
                            own.tell(act.copy(ynat[:, j, 512 * half:512 * half + 512], tile_bank(n)[:, :]), dense_a)
                        if half == 1:
                            if "V" in plan.tiles[n][2]:
                                evacuated(act, n)
                            stat((yname, j), ynat[:, j, :], D)
                            act.wait_ge(h_ready, src_ready + j + 1)
                            stat((hname, j), h[:, j, :], D)
                            if j and not filler:
                                hi(ntile[hname, j - 1])
                if filler:
                    filler()
                else:
                    hi(ntile[hname, 3])

            def fill_kv():
                evac("kx", lambda t, src: own.tell(act.copy(kxT[:, t, :], src[:, 0:MEM]), dense_a))
                hi(ntile["hx", 0])
                hi(ntile["hx", 1])
                evac("vx", lambda t, src: own.tell(
                    act.copy(vx[:, t % 2, 512 * (t // 2):512 * (t // 2) + 512], src[:, :]), dense_a))
                hi(ntile["hx", 2])
                hi(ntile["hx", 3])
            post("out", "yo", "hx", 0, fill_kv)
            evac("qx", lambda t, src: own.tell(act.copy(qxT[:, t, :], src[:, :]), dense_a))

            def x_high(hd):
                for dt in range(2):
                    act.wait_ge(x_out, 2 * hd + dt + 1)
                    own.tell(act.copy(xTh[:, 2 * hd + dt, :], bank[2 + dt][:, :]), x_hi)

            def x_pt(hd):
                act.wait_ge(x_tr, ST * (hd + 1))
                if hd:
                    act.wait_ge(x_out, 2 * hd)
                own.tell(act.copy(xprobT[:, 0, :], TB[0][:, :]), x_pta)
            group_used(act, "qx")
            for it in range(XH * ST):
                act.wait_ge(x_max, it + 1)
                if it >= 2:
                    act.wait_ge(x_tr, it - 1)
                own.tell(act.activation(xprob[:, it % 2, :], SB[it % 2][:, 0:MEM], ACT.Exp,
                                        bias=small[:, it % 2:it % 2 + 1], scale=XD ** -0.5,
                                        accum_out=small[:, 2 + it % 2:3 + it % 2]), x_exp)
                if it % 4 == 0 and it:
                    x_pt(it // 4 - 1)
                if it % 4 == 2 and it > 4:
                    x_high(it // 4 - 1)
            x_pt(XH - 1)
            x_high(XH - 1)
            post("ox", "yx", "hf", 4)

            ht = 0
            for s in range(3):
                for c in G[f"gu{s}"].chunks:
                    high(c.n + 1)
                    n = c.tiles[0][0]
                    act.wait_ge(dense_done, n + 1)
                    if ht >= 2:
                        act.wait_ge(hid_q, ht - 1)
                    own.tell(act.activation(silu[:, ht % 2, :], tile_bank(n)[:, :], ACT.Silu), dense_a)
                    act.wait_ge(hid_q, ht + 1)
                    if s and c is G[f"gu{s}"].chunks[0]:
                        group_used(act, f"down{s - 1}")
                    own.tell(act.copy(hidh[:, ht % 8, :], qbuf[:, ht % 2, :]), hid_hi)
                    ht += 1
                if s == 0:
                    evac("down0", lambda t, src: own.tell(
                        act.copy(ynat[:, t % 4, 512 * (t // 4):512 * (t // 4) + 512], src[:, :]), dense_a))
                elif s == 1:
                    evac("down1", None)
                else:
                    post("down2", "yf", "h2", 8)

            act.wait_ge(mem2_in, 16)
            norm("mem2", MT, D)

            def if_out(t, src):
                own.link(act.copy(gate_rows[:, 0, :], src[0:36, :]))
                own.tell(act.copy(gate_rows[:, 1, :], src[64:100, :]), dense_a)
            evac("if", if_out)
            act.wait_ge(b2_const, 1)
            evac("qk2", lambda t, src: own.tell(act.copy(qkc[:, t, 2:S + 2], src[:, :]), dense_a))
            act.wait_ge(gr_lin, 1)
            own.link(act.activation(gate_rows[:, 2, :], gate_rows[:, 2, :], ACT.Exp, scale=-1.0))
            own.tell(act.activation(gate_rows[:, 2, :], gate_rows[:, 2, :], ACT.Ln, bias=ones[0:36, 0:1]), gr_ln)
            for ct in range(4):
                act.wait_ge(qk_conv, ct + 1)
                own.tell(act.activation(qkT[:, ct, :], qkT[:, ct, :], ACT.Silu), qk_ready)
            act.wait_ge(gr_max, 1)
            own.tell(act.activation(gate_rows[:, 5, :], gate_rows[:, 5, :], ACT.Exp, scale=-1.0), gr_em)
            evac("memkv", lambda t, src: own.tell(act.copy(memkv[:, t, :], src[:, :]), dense_a))
            act.wait_ge(b2_const, 2)
            evac("v2", lambda t, src: own.tell(
                act.copy(vext[:, t, :, 0:LV], src[:, :].rearrange("p (h v) -> p h v", h=LH)), dense_a))
            evac("o2", lambda t, src: own.tell(act.activation(og[:, t, :], src[:, :], ACT.Sigmoid), dense_a))

            def naqk_out(t, src):
                if t >= 2:
                    act.wait_ge(n_tr, t - 1)
                own.tell(act.copy(stage[:, t % 2, 0:S], src[:, :]), dense_a)
                n_root(t)

            def n_root(t):
                act.wait_ge(n_raw, t + 1)
                w = 16 if t < 4 else 4
                own.tell(act.activation(small[:, 16:16 + w], small[:, 16:16 + w], ACT.Sqrt, bias=eps_col[:, 0:1],
                                        scale=1.0 / (ND if t < 4 else MD)), n_norm)
            evac("naqk", naqk_out)
            evac("navq", lambda t, src: own.tell(act.copy(navq[:, t, :], src[:, :]), dense_a))
            for t in range(4, 10):
                n_root(t)

            for it in range(2 * LH):
                d = it // LH
                act.wait_ge(l_bc, it + 1)
                if it >= 2:
                    act.wait_ge(l_shift, ST * (it - 1))
                own.tell(act.copy(maxb[:, it % 2, :], bank[4][:, :]), l_bcin)
                for si in range(ST):
                    off, n, t0 = span(d, si)
                    act.wait_ge(l_shift, ST * it + si + 1)
                    own.tell(act.activation(decay[:, it % 2, off:off + n], decay[:, it % 2, off:off + n], ACT.Exp), l_exp)

            for s in range(NH * ST + 1):
                if s < NH * ST:
                    act.wait_ge(a_max, s + 1)
                    own.tell(act.activation(nprob[:, s % 2, :], nprob[:, s % 2, :], ACT.Exp,
                                            bias=small[:, s % 2:s % 2 + 1],
                                            accum_out=small[:, 32 + s:33 + s]), a_exp)
                if s >= 1 and (s - 1) % 2 == 0:
                    i = s - 1
                    act.wait_ge(a_tr, i + 1)
                    if i >= 2:
                        act.wait_ge(a_out, i - 1)
                    own.tell(act.copy(nprobT[:, i % 2, :, ::-1], TB[i % 2][:, :].rearrange("p (k q) -> p k q", k=ST)),
                             a_pta)
            for j in range(ST):
                act.wait_ge(n_raw, 10 + j + 1)
                own.tell(act.activation(small[:, 16:20], small[:, 16:20], ACT.Sqrt, bias=eps_col[:, 0:1],
                                        scale=1.0 / LV), n_norm)
                if j:
                    hi(ntile["hm", j - 1])
            hi(ntile["hm", 3])
            for j in range(ST):
                hi(ntile["hna", j])

            def m_pt(hd):
                act.wait_ge(m_tr, ST * (hd + 1))
                if hd:
                    act.wait_ge(m_out, hd)
                own.tell(act.copy(mprobT[:, 0, :], TB[0][:, :]), m_pta)
            for it in range(MH * ST):
                act.wait_ge(m_max, it + 1)
                if it >= 2:
                    act.wait_ge(m_tr, it - 1)
                own.tell(act.activation(mprob[:, it % 2, :], SB[it % 2][:, 0:MEM], ACT.Exp,
                                        bias=small[:, it % 2:it % 2 + 1],
                                        accum_out=small[:, 2 + it % 2:3 + it % 2]), m_exp)
                if it % 4 == 0 and it:
                    m_pt(it // 4 - 1)
            m_pt(MH - 1)
            for t in range(2):
                act.wait_ge(m_out, 2 * t + 2)
                own.tell(act.copy(hmTh[:, 6 + t, :], bank[2 + t][:, :]), m_hi)

            for cp in range(4):
                def gate_out(t, src, cp=cp):
                    if cp:
                        act.wait_ge(y_q, 2 * cp)
                    own.tell(act.activation(sg[:, t // 2, t % 2, :], src[:, :], ACT.Sigmoid), dense_a)
                evac(f"gate2_{cp}", gate_out)
                high(G[f"proj2_{cp}"].chunks[-1].n + 1)
                for m in range(2):
                    act.wait_ge(y_q, 2 * cp + m + 1)
                    own.tell(act.copy(yTh[:, 2 * cp + m, :], qbuf[:, m, :]), y_hi)
            for c in G["out2"].chunks:
                high(c.n + 1)
            for j in range(ST):
                evacuated(act, G["out2"].tiles[4 + j])
                stat(("h4", j), h[:, j, :], D)
                if j:
                    hi(ntile["h4", j - 1])
            hi(ntile["h4", 3])
            for s in range(4):
                for c in G[f"up{s}"].chunks:
                    high(c.n + 1)
                    for n, *_ in c.tiles:
                        act.wait_ge(dense_done, n + 1)
                        if ht >= 2:
                            act.wait_ge(hid_q, ht - 1)
                        own.tell(act.activation(silu[:, ht % 2, :], tile_bank(n)[:, :], ACT.Relu), dense_a)
                        act.wait_ge(hid_q, ht + 1)
                        if s and n == G[f"up{s}"].tiles[0]:
                            group_used(act, f"dn{s - 1}")
                        own.tell(act.copy(hidh[:, (ht - 22) % 8, :], qbuf[:, ht % 2, :]), hid_hi)
                        ht += 1
                for c in G[f"dn{s}"].chunks:
                    high(c.n + 1)

        @block.vector
        def _(dve):
            own = Own(dve, dve_chain)

            def xn(phase, j, width):
                i = ntile[phase, j]
                k = STATS.index((phase, j))
                dve.wait_ge(rms_done, k + 1)
                own.link(dve.reciprocal(rms[:, k:k + 1], rms[:, k:k + 1]))
                if i >= 2:
                    dve.wait_ge(tr_done, NT[i - 2][3] + NT[i - 2][2])
                own.tell(dve.tensor_scalar(stage[:, i % 2, 0:width], SOURCES[phase][:, j, :], rms[:, k:k + 1], None,
                                           ALU.mult), xn_ready)

            def ql(phase, j):
                i = ntile[phase, j]
                first, gain = NT[i][3], NT[i][5]
                for b in range(NT[i][2]):
                    r = first + b
                    _, n = turned(i, b, 1)
                    dve.wait_ge(tr_done, r + 1)
                    src = TB[r % 2][:, 0:n * P].rearrange("p (k t) -> p k t", k=n)
                    q = qbuf[:, r % 2, 0:n * P].rearrange("p (k t) -> p k t", k=n)
                    if gain is None:
                        own.tell(dve.tensor_copy(q, src), q_ready)
                    else:
                        gv = gcol[:, gain + 4 * b:gain + 4 * b + n]
                        own.tell(dve.tensor_tensor(q, src, bc(gv[:, :, None], [P, n, P]), ALU.mult), q_ready)
                for b in range(NT[i][2]):
                    r = first + b
                    dst, n = turned(i, b, 1)
                    top, _ = turned(i, b, 0)
                    dve.wait_ge(hi_done, r + 1)
                    q = qbuf[:, r % 2, 0:n * P].rearrange("p (k t) -> p k t", k=n)
                    own.tell(dve.tensor_tensor(dst, q, top.bitcast(F32), ALU.subtract), lo_done)

            def norm(phase, ntok, width):
                for j in range(ntok):
                    xn(phase, j, width)
                    if j:
                        ql(phase, j - 1)
                ql(phase, ntok - 1)

            def tile_in(name, t):
                n = G[name].tiles[t]
                dve.wait_ge(dense_done, n + 1)
                return tile_bank(n)

            dve.wait_ge(const_ready, 3)
            dve.wait_ge(pos_in, 16 * (ST + 1))
            own.link(dve.tensor_copy(posf[:, :], posi[:, :]))
            own.link(dve.tensor_tensor(ang[:, :, :], bc(posf[:, :, None], [P, 5, 32]), bc(invf[:, None, :], [P, 5, 32]),
                                       ALU.mult))
            own.link(dve.tensor_scalar(angk[:, :, :], ang[:, :, :], float(1 / (2 * np.pi)), MAGIC, ALU.mult, ALU.add))
            own.link(dve.tensor_scalar(angk[:, :, :], angk[:, :, :], -MAGIC, None, ALU.add))
            for part in TWO_PI:
                own.link(dve.scalar_tensor_tensor(out=ang[:, :, :], in0=angk[:, :, :], scalar=-part, in1=ang[:, :, :],
                                                  op0=ALU.mult, op1=ALU.add))
            own.tell(dve.tensor_scalar(ang[:, :, :], ang[:, :, :], 3.1415925, -3.1415925, ALU.min, ALU.max), rope_ang)
            dve.wait_ge(vec_tr, 1)
            own.link(dve.tensor_copy(gcol[:, :], SB[1][:, 0:NCOL]))
            own.tell(dve.tensor_copy(peT[:, :, :], SB[1][:, P:P + 2 * CMP].rearrange("p (i c) -> p i c", i=2)), vec_col)

            dve.wait_ge(x_in, 16)
            norm("x", ST, D)
            dve.wait_ge(rope_sin, 1)
            own.link(dve.tensor_scalar(sinT[:, :, 0:32], sinT[:, :, 32:64], -1.0, None, ALU.mult))
            own.link(dve.tensor_tensor(angk[:, :, :], angk[:, :, :], angk[:, :, :], ALU.mult))
            for o in (0, 32):
                own.link(dve.tensor_scalar(cosT[:, :, o:o + 32], angk[:, :, :], -2.0, 1.0, ALU.mult, ALU.add))

            def rotate(dst, src, heads, t, np_=P):
                pr, sw = rtmp[0:np_, 0, 0:heads * HD], rtmp[0:np_, 1, 0:heads * HD]
                v = lambda z: z.rearrange("p (h d) -> p h d", h=heads)
                w = lambda z: z.rearrange("p (h a d) -> p h a d", h=heads, a=2)
                own.link(dve.tensor_tensor(v(pr), src, bc(cosT[0:np_, t, None, :], [np_, heads, HD]), ALU.mult))
                own.link(dve.tensor_tensor(
                    w(sw), src.rearrange("p h (a d) -> p h a d", a=2)[:, :, ::-1, :],
                    bc(sinT[0:np_, t, None, :].rearrange("p h (a d) -> p h a d", a=2), [np_, heads, 2, 32]), ALU.mult))
                return dst(dve.tensor_tensor, v(pr), v(sw))

            def rope_q(j):
                n = G["q"].tiles[j]
                evacuated(dve, n)
                if j >= 2:
                    dve.wait_ge(rot_tr, j - 1)
                src = qn[:, j % 2, :].rearrange("p (h d) -> p h d", d=HD)
                out_v = qrot[:, j % 2, :].rearrange("p (t g d) -> p g t d", t=PER_GROUP, g=GROUPS)

                def add(tt, x, y):
                    s4 = lambda z: z.rearrange("p (g t) d -> p g t d", g=GROUPS)
                    own.tell(tt(out_v, s4(x), s4(y), ALU.add), rot_ready)
                rotate(add, src, 8, j)

            def rope_k(j):
                evacuated(dve, G["kv"].tiles[j])
                dve.wait_ge(rot_tr, 4 + j - 1)
                for br in range(2):
                    src = kvn[:, j, 256 * br:256 * br + P].rearrange("p (g d) -> p g d", g=GROUPS)
                    dst = qrot[:, j % 2, br * P:br * P + P].rearrange("p (g d) -> p g d", g=GROUPS)

                    def add(tt, x, y, dst=dst, br=br):
                        ins = tt(dst, x, y, ALU.add)
                        own.tell(ins, rot_ready) if br else own.link(ins)
                    rotate(add, src, GROUPS, j)

            def rot_copy(r):
                dve.wait_ge(rot_tr, r + 1)
                n = 4 if r < 4 else 2
                dst = qT if r < 4 else kT
                j = r % 4
                own.tell(dve.tensor_copy(dst[:, :, j * P:(j + 1) * P],
                                         TB[r % 2][:, 0:n * P].rearrange("p (k t) -> p k t", k=n)), qkT_ready)
            rope_q(0), rope_q(1), rot_copy(0), rot_copy(1), rope_q(2), rope_q(3)
            for i, f in enumerate((fk, fv)):
                src = tile_in("kcvc", i)
                for g in range(GROUPS):
                    ps = slice(HD * g, HD * g + HD)
                    s = src[ps, 0:1]
                    tokens = bass.AP(s.tensor, s.offset, [[s.ap[0][0], HD], [1, CMP], [CSTRIDE, NCMP]])
                    ins = dve.tensor_tensor(f[:, :, g * NCMP:(g + 1) * NCMP], tokens,
                                            bc(peT[ps, i, :, None], [HD, CMP, NCMP]), ALU.add)
                    own.tell(ins, dense_v) if g == 1 else own.link(ins)
            rot_copy(2), rot_copy(3), rope_k(0), rope_k(1), rot_copy(4), rot_copy(5), rope_k(2), rope_k(3)
            rot_copy(6), rot_copy(7)

            for ct in range(4):
                src = tile_in("xin", ct)
                evacuated(dve, G["cg"].tiles[ct])
                own.tell(dve.tensor_tensor(zT[:, ct, 2:S + 2], zT[:, ct, 2:S + 2], src[:, :], ALU.mult), dense_v)
            for ct in range(4):
                w = lambda k: gcol[:, COL["conv_w"] + 4 * k + ct:COL["conv_w"] + 4 * k + ct + 1]
                own.link(dve.tensor_scalar(qbuf[:, 0, :], zT[:, ct, 0:S], w(0), None, ALU.mult))
                for k in (1, 2):
                    own.link(dve.scalar_tensor_tensor(out=qbuf[:, 0, :], in0=zT[:, ct, k:S + k], scalar=w(k),
                                                      in1=qbuf[:, 0, :], op0=ALU.mult, op1=ALU.add))
                evacuated(dve, G["bg"].tiles[ct])
                own.tell(dve.tensor_tensor(bgT[:, ct, :], qbuf[:, 0, :], bgT[:, ct, :], ALU.mult), conv_y)
            dve.wait_ge(conv_rms, 1)
            inv = stage[:, 0, 0:S]
            own.link(dve.reciprocal(inv, inv))

            def conv_scale(ct):
                g = gcol[:, COL["norm_conv_out"] + ct:COL["norm_conv_out"] + ct + 1]
                own.tell(dve.scalar_tensor_tensor(out=qbuf[:, ct % 2, :], in0=bgT[:, ct, :], scalar=g, in1=inv,
                                                  op0=ALU.mult, op1=ALU.mult), conv_q)
            conv_scale(0)
            for ct in range(4):
                if ct < 3:
                    conv_scale(ct + 1)
                dve.wait_ge(conv_hi, ct + 1)
                own.tell(dve.tensor_tensor(xTl[:, ct, :], qbuf[:, ct % 2, :], xTh[:, ct, :].bitcast(F32),
                                           ALU.subtract), conv_lo)
            norm("mem", MT, D)

            dve.wait_ge(cmp_kv, 1)
            own.link(dve.tensor_copy(kcn[0:NCMP, :], TB[0][0:NCMP, 0:P]))
            for hh in range(4):
                ps = slice(32 * hh, 32 * hh + 32)
                own.tell(dve.tensor_copy(vbd[ps, :, hh, :], TB[1][ps, 0:P].rearrange("p (g d) -> p g d", g=GROUPS)),
                         cmp_kv_in)

            def kc_add(tt, x, y):
                own.tell(tt(kcr[0:NCMP, :].rearrange("p (g d) -> p g d", g=GROUPS), x, y, ALU.add), kc_rot)
            krp, krs = qbuf[0:NCMP, 0, 0:P], qbuf[0:NCMP, 1, 0:P]
            v2 = lambda z: z.rearrange("p (g d) -> p g d", g=GROUPS)
            v3 = lambda z: z.rearrange("p (g a d) -> p g a d", g=GROUPS, a=2)
            own.link(dve.tensor_tensor(v2(krp), v2(kcn[0:NCMP, :]), bc(cosT[0:NCMP, 4, None, :], [NCMP, GROUPS, HD]),
                                       ALU.mult))
            own.link(dve.tensor_tensor(v3(krs), v3(kcn[0:NCMP, :])[:, :, ::-1, :],
                                       bc(sinT[0:NCMP, 4, None, :].rearrange("p h (a d) -> p h a d", a=2),
                                          [NCMP, GROUPS, 2, 32]), ALU.mult))
            kc_add(dve.tensor_tensor, v2(krp), v2(krs))
            dve.wait_ge(kc_tr, 1)
            own.tell(dve.tensor_copy(kcT[:, 0:NCMP], TB[0][:, 0:NCMP]), kcT_ready)

            evacuated(dve, G["gates"].tiles[0])
            for c in range(ST):
                dve.wait_ge(c_scores, 2 * c + 2)
                if c:
                    dve.wait_ge(c_exp, c)
                for g in range(GROUPS):
                    own.link(dve.tensor_tensor(scb[:, 4 * g:4 * g + 4, :],
                                               SB[g][:, 0:4 * NCMP].rearrange("p (h j) -> p h j", h=4),
                                               bc(cmask[:, c, None, :], [P, 4, NCMP]), ALU.add))
                own.link(dve.tensor_reduce(small[:, 16:24], scb[:, :, :], X, ALU.max))
                own.tell(dve.tensor_tensor(scb[:, :, :], scb[:, :, :], bc(small[:, 16:24, None], [P, 8, NCMP]),
                                           ALU.subtract), c_shift)
                dve.wait_ge(c_exp, c + 1)
                own.link(dve.tensor_reduce(small[:, 24:32], pc[:, c % 2, :, 0:NCMP], X, ALU.add))
                own.link(dve.reciprocal(small[:, 24:32], small[:, 24:32]))
                own.link(dve.tensor_tensor(small[:, 32:40], small[:, 24:32], gates[:, c, 0:24:3], ALU.mult))
                if c == 0:
                    own.link(dve.tensor_scalar(small[:, 32:40], small[:, 32:40], small[:, 95:96], None, ALU.mult))
                dve.wait_ge(c_tr, c + 1)
                if c:
                    dve.wait_ge(c_out, c)
                own.tell(dve.tensor_copy(pcT[:, :, :], TB[0][:, 0:2 * P].rearrange("p (g q) -> p g q", g=2)), c_trin)
                dve.wait_ge(c_out, c + 1)
                own.tell(dve.tensor_tensor(yatt[:, c, :].rearrange("p (h d) -> p h d", h=8),
                                           bank[3][:, :].rearrange("p (h d) -> p h d", h=8),
                                           bc(small[:, 32:40, None], [P, 8, HD]), ALU.mult), c_used)

            for s in range(len(ITEMS) + 2):
                if s < len(ITEMS):
                    qt = ITEMS[s][0]
                    n = (qt + 1) * P
                    if s >= 2:
                        dve.wait_ge(pt_done, 2 * s - 2)
                    for br in range(2):
                        dve.wait_ge(s_done, 2 * s + br + 1)
                        own.tell(dve.tensor_tensor_reduce(
                            out=prob[:, s % 2, br, 0:n], in0=SB[br][:, 0:n], in1=causal[:, 512 - n:512], scale=1.0,
                            scalar=-3e38, op0=ALU.add, op1=ALU.max, accum_out=small[:, 44 + br:45 + br]), s_taken)
                    own.tell(dve.tensor_scalar(small[:, 4 * (s % 2):4 * (s % 2) + 2], small[:, 44:46], -HD ** -0.5,
                                               None, ALU.mult), s_max)
                if 1 <= s <= len(ITEMS):
                    i = s - 1
                    k = ITEMS[i][0] + 1
                    dve.wait_ge(pt_done, 2 * i + 2)
                    if i >= 2:
                        dve.wait_ge(pv_done, i - 1)
                    own.tell(dve.tensor_copy(probT[:, i % 2, 1, 0:k, :],
                                             TB[1][:, 0:k * P].rearrange("p (k q) -> p k q", k=k)), pt_v)
                if s >= 2:
                    i = s - 2
                    qt, g, t = ITEMS[i]
                    hd = PER_GROUP * g + t
                    den = small[:, 8 + 2 * (i % 4):10 + 2 * (i % 4)]
                    dve.wait_ge(s_exp, 2 * i + 2)
                    own.link(dve.reciprocal(small[:, 46:48], den))
                    own.link(dve.tensor_tensor(small[:, 48:50], small[:, 46:48], gates[:, qt, 3 * hd + 1:3 * hd + 3],
                                               ALU.mult))
                    dve.wait_ge(pv_done, i + 1)
                    y = yatt[:, qt, hd * HD:(hd + 1) * HD]
                    for br in range(2):
                        ins = dve.scalar_tensor_tensor(out=y, in0=bank[3][:, br * HD:(br + 1) * HD],
                                                       scalar=small[:, 48 + br:49 + br], in1=y,
                                                       op0=ALU.mult, op1=ALU.add)
                        own.tell(ins, o_taken) if br else own.link(ins)
            norm("att", ST, 512)

            def post(yname, j, gains):
                k = STATS.index((yname, j))
                dve.wait_ge(rms_done, k + 1)
                dve.wait_ge(gpost_in, 16 * gains)
                own.link(dve.reciprocal(rms[:, k:k + 1], rms[:, k:k + 1]))
                own.link(dve.scalar_tensor_tensor(out=ynat[:, j, :], in0=ynat[:, j, :], scalar=rms[:, k:k + 1],
                                                  in1=gpost[:, :], op0=ALU.mult, op1=ALU.mult))
                own.tell(dve.tensor_tensor(h[:, j, :], h[:, j, :], ynat[:, j, :], ALU.add), h_ready)

            for j in range(2):
                post("yo", j, 1)
                xn("hx", j, D)
            post("yo", 2, 1)
            post("yo", 3, 1)
            ql("hx", 0)
            xn("hx", 2, D)
            ql("hx", 1)
            xn("hx", 3, D)
            ql("hx", 2)
            ql("hx", 3)

            def attention(scores, mx, exp_, normed, tr, pts, outs, prob_, probT_, scale, items, final):
                for it in range(items):
                    c = it % 2
                    dve.wait_ge(scores, it + 1)
                    own.link(dve.tensor_reduce(small[:, 6:7], SB[c][:, 0:MEM], X, ALU.max))
                    if it >= 2:
                        dve.wait_ge(exp_, it - 1)
                    own.tell(dve.tensor_scalar(small[:, c:c + 1], small[:, 6:7], -scale, None, ALU.mult), mx)
                    dve.wait_ge(exp_, it + 1)
                    own.link(dve.reciprocal(small[:, 4 + c:5 + c], small[:, 2 + c:3 + c]))
                    own.tell(dve.tensor_scalar(prob_[:, c, :], prob_[:, c, :], small[:, 4 + c:5 + c], None, ALU.mult),
                             normed)
                    if it % 4 == 0 and it:
                        copy_t(it // 4 - 1, tr, pts, outs, probT_)
                    if it % 4 == 2 and it > 4:
                        final(it // 4 - 1)
                copy_t(items // 4 - 1, tr, pts, outs, probT_)
                final(items // 4 - 1)

            def copy_t(hd, tr, pts, outs, probT_):
                sem_out, per_head = outs
                dve.wait_ge(tr, ST * (hd + 1))
                if hd:
                    dve.wait_ge(sem_out, per_head * hd)
                own.tell(dve.tensor_copy(probT_[:, 1, :], TB[1][:, :]), pts)

            def x_low(hd):
                for dt in range(2):
                    dve.wait_ge(x_hi, 2 * hd + dt + 1)
                    own.tell(dve.tensor_tensor(xTl[:, 2 * hd + dt, :], bank[2 + dt][:, :],
                                               xTh[:, 2 * hd + dt, :].bitcast(F32), ALU.subtract), x_lo)
            attention(x_scores, x_max, x_exp, x_norm, x_tr, x_ptv, (x_out, 2), xprob, xprobT, XD ** -0.5, XH * ST,
                      x_low)
            for j in range(ST):
                post("yx", j, 2)
                if j:
                    ql("hf", j - 1)
                xn("hf", j, D)
            ql("hf", 3)

            ht = 0

            def hid_low():
                dve.wait_ge(hid_hi, ht + 1)
                k = ht % 8 if ht < 22 else (ht - 22) % 8
                own.tell(dve.tensor_tensor(hidl[:, k, :], qbuf[:, ht % 2, :], hidh[:, k, :].bitcast(F32),
                                           ALU.subtract), hid_lo)

            for s in range(3):
                for c in G[f"gu{s}"].chunks:
                    evacuated(dve, c.tiles[0][0])
                    n = c.tiles[1][0]
                    dve.wait_ge(dense_done, n + 1)
                    own.tell(dve.tensor_tensor(qbuf[:, ht % 2, :], silu[:, ht % 2, :], tile_bank(n)[:, :], ALU.mult),
                             hid_q)
                    hid_low()
                    ht += 1
                if s == 0:
                    continue
                for t in range(8):
                    if s == 1 and t == 0:
                        evacuated(dve, G["down0"].tiles[7])
                    half, j = t // 4, t % 4
                    src = tile_in(f"down{s}", t)
                    y = ynat[:, j, 512 * half:512 * half + 512]
                    own.tell(dve.tensor_tensor(y, y, src[:, :], ALU.add), dense_v)
                    if s == 2 and half:
                        post("yf", j, 3)
                        if j:
                            ql("h2", j - 1)
                        xn("h2", j, D)
            ql("h2", 3)

            norm("mem2", MT, D)
            R = gate_rows
            evacuated(dve, G["if"].tiles[0])
            dve.wait_ge(ifb_in, 64)
            own.link(dve.tensor_scalar(R[:, 0, :], R[:, 0, :], small[0:36, 88:89], None, ALU.add))
            own.link(dve.tensor_scalar(R[:, 1, :], R[:, 1, :], small[0:36, 89:90], None, ALU.add))
            own.tell(dve.scalar_tensor_tensor(out=R[:, 2, :], in0=R[:, 1, :], scalar=-1.0, in1=R[:, 1, :],
                                              op0=ALU.mult, op1=ALU.max), gr_lin)
            own.link(dve.memset(R[:, 3:5, :], 0.0))
            for ct in range(4):
                w = lambda k: gcol[:, COL["conv_w_2"] + 4 * k + ct:COL["conv_w_2"] + 4 * k + ct + 1]
                cb = gcol[:, COL["conv_b_2"] + ct:COL["conv_b_2"] + ct + 1]
                evacuated(dve, G["qk2"].tiles[ct])
                own.link(dve.tensor_scalar(qkT[:, ct, :], qkc[:, ct, 0:S], w(0), cb, ALU.mult, ALU.add))
                for k in range(1, 5):
                    ins = dve.scalar_tensor_tensor(out=qkT[:, ct, :], in0=qkc[:, ct, k:S + k], scalar=w(k),
                                                   in1=qkT[:, ct, :], op0=ALU.mult, op1=ALU.add)
                    own.tell(ins, qk_conv) if k == 4 else own.link(ins)
            dve.wait_ge(gr_ln, 1)
            own.link(dve.scalar_tensor_tensor(out=R[:, 1, :], in0=R[:, 1, :], scalar=0.0, in1=R[:, 2, :],
                                              op0=ALU.min, op1=ALU.subtract))
            fw, bw = slice(0, 4), slice(32, 36)
            for ps, step in ((fw, 1), (bw, -1)):
                own.link(dve.tensor_tensor_scan(R[ps, 3, ::step], bc(ones[ps, 0:1], [4, S]), R[ps, 1, ::step], 0.0,
                                                ALU.mult, ALU.add))
            own.link(dve.tensor_tensor(R[:, 0, :], R[:, 0, :], R[:, 3, :], ALU.subtract))
            for ps, step in ((fw, 1), (bw, -1)):
                own.link(dve.tensor_tensor_scan(R[ps, 4, ::step], R[ps, 0, ::step], R[ps, 0, ::step], -3e38,
                                                ALU.max, ALU.max))
            own.tell(dve.tensor_scalar(neg_max, R[:, 4, :], -1.0, None, ALU.mult), gr_neg)
            own.tell(dve.tensor_tensor(R[:, 5, :], R[:, 3, :], R[:, 4, :], ALU.add), gr_max)
            dve.wait_ge(gr_tr, 1)
            own.tell(dve.tensor_copy(acol[:, :, :, :], TB[0][:, 0:8 * 36].rearrange("p (a t r) -> p a t r", a=2, t=ST)),
                     gr_col)

            dve.wait_ge(gain2_in, 64)

            def head_norm(t):
                if t < 4:
                    evacuated(dve, G["naqk"].tiles[t])
                    src, heads, d, gain, scaled = stage[:, t % 2, 0:S], 16, ND, na_gain, 8
                elif t < 8:
                    evacuated(dve, G["navq"].tiles[t - 4])
                    src, heads, d, gain, scaled = navq[:, t - 4, 256:512], 4, MD, mem_gain[:, 0:4, :], 4
                else:
                    evacuated(dve, G["memkv"].tiles[t - 8])
                    src, heads, d, gain, scaled = memkv[:, t - 8, 0:256], 4, MD, mem_gain[:, 4:8, :], 0
                if t >= 2:
                    dve.wait_ge(n_tr, t - 1)
                v = lambda z: z.rearrange("p (h d) -> p h d", h=heads)
                dst = stage[:, t % 2, S:S + heads * d]
                r = small[:, 16:16 + heads]
                own.link(dve.tensor_tensor(dst, src, src, ALU.mult))
                own.tell(dve.tensor_reduce(r, v(dst), X, ALU.add), n_raw)
                dve.wait_ge(n_norm, t + 1)
                own.link(dve.reciprocal(r, r))
                if scaled:
                    own.link(dve.tensor_scalar(small[:, 16:16 + scaled], small[:, 16:16 + scaled], d ** -0.5, None,
                                               ALU.mult))
                own.link(dve.tensor_tensor(v(dst), v(src), bc(r[:, :, None], [P, heads, d]), ALU.mult))
                own.tell(dve.tensor_tensor(v(dst), v(dst), gain, ALU.mult), n_in)

            def head_copy(t):
                dve.wait_ge(n_tr, t + 1)
                dst, j, n = (naT, t, 4) if t < 4 else (qmT, t - 4, 2) if t < 8 else (kmT, t - 8, 2)
                src = TB[t % 2][:, 0:n * P].rearrange("p (k t) -> p k t", k=n)
                to = dst[:, :, j * P:(j + 1) * P]
                if t < 4:
                    own.link(dve.tensor_copy(to[:, 0:2, ::-1], src[:, 0:2, :]))
                    to, src = to[:, 2:4, :], src[:, 2:4, :]
                own.tell(dve.tensor_copy(to, src), n_copied)
            for t in range(10):
                head_norm(t)
                if t:
                    head_copy(t - 1)
            head_copy(9)

            def l_result(it):
                d, hd = it // LH, it % LH
                lo = bank[2], bank[3]
                if it % 2:
                    lo = bank[0], bank[1]
                dve.wait_ge(l_out, it + 1)
                den, tmp = small[:, 52:56], small[:, 56:60]
                for b in range(2):
                    own.link(dve.tensor_copy(tmp[:, 2 * b:2 * b + 2], lo[b][:, 0:2 * (LV + 1)].rearrange(
                        "p (t v) -> p t v", t=2)[:, :, LV]))
                own.link(dve.scalar_tensor_tensor(out=den, in0=tmp, scalar=-1.0, in1=tmp, op0=ALU.mult, op1=ALU.max))
                own.link(dve.tensor_tensor(den, den, acol[:, 1, :, 32 * d + hd], ALU.max))
                own.link(dve.reciprocal(den, den))
                for tt in range(ST):
                    o = lo[tt // 2][:, (tt % 2) * (LV + 1):(tt % 2) * (LV + 1) + LV]
                    y = hsum[:, tt, hd * LV:(hd + 1) * LV]
                    r = den[:, tt:tt + 1]
                    if d == 0:
                        ins = dve.tensor_scalar(y, o, r, None, ALU.mult)
                    else:
                        ins = dve.scalar_tensor_tensor(out=y, in0=o, scalar=r, in1=y, op0=ALU.mult, op1=ALU.add)
                    own.tell(ins, l_used) if tt == ST - 1 else own.link(ins)

            for it in range(2 * LH + 1):
                if it < 2 * LH:
                    d, hd = it // LH, it % LH
                    dve.wait_ge(l_bcin, it + 1)
                    if it >= 2:
                        dve.wait_ge(l_out, it - 1)
                    for si in range(ST):
                        off, n, t0 = span(d, si)
                        a_s = acol[:, 0, si, 32 * d + hd:32 * d + hd + 1]
                        own.tell(dve.tensor_scalar(decay[:, it % 2, off:off + n], maxb[:, it % 2, t0:t0 + n], a_s, 0.0,
                                                   ALU.add, ALU.min), l_shift)
                    for si in range(ST):
                        off, n, t0 = span(d, si)
                        k = ST * it + si
                        dve.wait_ge(l_scores, k + 1)
                        dve.wait_ge(l_exp, k + 1)
                        own.tell(dve.scalar_tensor_tensor(out=decay[:, it % 2, off:off + n], in0=SB[k % 2][:, 0:n],
                                                          scalar=LQ ** -0.5, in1=decay[:, it % 2, off:off + n],
                                                          op0=ALU.mult, op1=ALU.mult), l_mul)
                if it:
                    l_result(it - 1)

            for s in range(NH * ST + 1):
                if s < NH * ST:
                    hd, qt = s // ST, s % ST
                    dve.wait_ge(b_masked, 2 * (hd + 1))
                    dve.wait_ge(a_scores, s + 1)
                    if s >= 2:
                        dve.wait_ge(a_tr, s - 1)
                    own.tell(dve.tensor_tensor_reduce(
                        out=nprob[:, s % 2, :], in0=SB[s % 2][:, :],
                        in1=bias2[:, hd % 2, 7 - 2 * qt:15 - 2 * qt, :].rearrange("p k c -> p (k c)"), scale=1.0,
                        scalar=-3e38, op0=ALU.add, op1=ALU.max, accum_out=small[:, 4:5]), a_taken)
                    own.tell(dve.tensor_scalar(small[:, s % 2:s % 2 + 1], small[:, 4:5], -1.0, None, ALU.mult), a_max)
                if s >= 1 and (s - 1) % 2 == 1:
                    i = s - 1
                    dve.wait_ge(a_tr, i + 1)
                    if i >= 2:
                        dve.wait_ge(a_out, i - 1)
                    own.tell(dve.tensor_copy(nprobT[:, 1, :, ::-1], TB[1][:, :].rearrange("p (k q) -> p k q", k=ST)),
                             a_ptv)
            for j in range(ST):
                i = ntile["hm", j]
                y = hsum[:, j, :]
                v = lambda z: z.rearrange("p (h d) -> p h d", h=LH)
                dve.wait_ge(tr_done, NT[i - 2][3] + NT[i - 2][2])
                own.link(dve.tensor_tensor(stage[:, i % 2, S:2 * S], y, y, ALU.mult))
                own.tell(dve.tensor_reduce(small[:, 16:20], v(stage[:, i % 2, S:2 * S]), X, ALU.add), n_raw)
                dve.wait_ge(n_norm, 10 + j + 1)
                own.link(dve.reciprocal(small[:, 16:20], small[:, 16:20]))
                own.link(dve.tensor_tensor(v(stage[:, i % 2, 0:S]), v(y), bc(small[:, 16:20, None], [P, LH, LV]),
                                           ALU.mult))
                own.tell(dve.tensor_tensor(stage[:, i % 2, 0:S], stage[:, i % 2, 0:S], og[:, j, :], ALU.mult), xn_ready)
                if j:
                    ql("hm", j - 1)
            ql("hm", 3)
            dve.wait_ge(a_den, 1)
            own.link(dve.reciprocal(small[:, 32:64], SB[0][:, 0:NH * ST]))
            for qt in range(ST):
                o = bank[2 + qt // 2][:, (qt % 2) * 256:(qt % 2) * 256 + 256].rearrange("p (h d) -> p h d", h=NH)
                r = small[:, 32:64].rearrange("p (h q) -> p h q", q=ST)[:, :, qt:qt + 1]
                own.tell(dve.tensor_tensor(hna[:, qt, :].rearrange("p (h d) -> p h d", h=NH), o, bc(r, [P, NH, ND]),
                                           ALU.mult), xn_ready)
            for j in range(ST):
                ql("hna", j)

            attention(m_scores, m_max, m_exp, m_norm, m_tr, m_ptv, (m_out, 1), mprob, mprobT, 1.0, MH * ST,
                      lambda hd: None)
            for t in range(2):
                dve.wait_ge(m_hi, t + 1)
                own.tell(dve.tensor_tensor(hmTl[:, 6 + t, :], bank[2 + t][:, :], hmTh[:, 6 + t, :].bitcast(F32),
                                           ALU.subtract), m_lo)

            for cp in range(4):
                g = G[f"proj2_{cp}"]
                for m in range(2):
                    for b in range(3):
                        evacuated(dve, G[f"gate2_{cp}"].tiles[2 * b + m])
                        src = tile_in(f"proj2_{cp}", 3 * m + b)
                        dst = qbuf[:, m, :] if b == 0 else stage[:, 0, (b - 1) * S:b * S]
                        own.tell(dve.tensor_tensor(dst, sg[:, b, m, :], src[:, :], ALU.mult), dense_v)
                    own.link(dve.tensor_tensor(qbuf[:, m, :], qbuf[:, m, :], stage[:, 0, 0:S], ALU.add))
                    own.tell(dve.tensor_tensor(qbuf[:, m, :], qbuf[:, m, :], stage[:, 0, S:2 * S], ALU.add), y_q)
                for m in range(2):
                    dve.wait_ge(y_hi, 2 * cp + m + 1)
                    own.tell(dve.tensor_tensor(yTl[:, 2 * cp + m, :], qbuf[:, m, :],
                                               yTh[:, 2 * cp + m, :].bitcast(F32), ALU.subtract), y_lo)

            def onto_h(name, t):
                half, j = t // 4, t % 4
                src = tile_in(name, t)
                y = h[:, j, 512 * half:512 * half + 512]
                own.tell(dve.tensor_tensor(y, y, src[:, :], ALU.add), dense_v)
            for t in range(4):
                onto_h("out2", t)
            for j in range(ST):
                onto_h("out2", 4 + j)
                if j:
                    ql("h4", j - 1)
                xn("h4", j, D)
            ql("h4", 3)
            for s in range(4):
                for n in G[f"up{s}"].tiles:
                    evacuated(dve, n)
                    own.tell(dve.tensor_tensor(qbuf[:, ht % 2, :], silu[:, ht % 2, :], silu[:, ht % 2, :], ALU.mult),
                             hid_q)
                    hid_low()
                    ht += 1
                for t in range(8):
                    onto_h(f"dn{s}", t)

        @block.tensor
        def _(pe):
            def transpose_blocks(dst, src, n, width=P):
                for b in range(n):
                    mm = pe.transpose(dst[:, b * P:b * P + P], src[:, b * width:(b + 1) * width], ident[:, :])
                return mm

            def turn(phase, j):
                i = ntile[phase, j]
                pe.wait_ge(xn_ready, i + 1)
                for b in range(NT[i][2]):
                    r = NT[i][3] + b
                    if r >= 2:
                        pe.wait_ge(q_ready, r - 1)
                    src = hna[:, j, :] if phase == "hna" else stage[:, i % 2, 512 * b:512 * b + 512]
                    transpose_blocks(TB[r % 2], src, 2 if phase == "hna" else 4).then_inc(tr_done, 1)

            def three(ps, ah, al, bh, bl, first, last):
                pe.matmul(ps, ah, bh, start=first, stop=False)
                pe.matmul(ps, ah, bl, start=False, stop=False)
                return pe.matmul(ps, al, bh, start=False, stop=last)

            def dense(name, xh, xl, ntok=S):
                g = G[name]
                for c in g.chunks:
                    if c.split:
                        pe.wait_ge(wh_done, split_rank[c.n])
                        pe.wait_ge(wl_done, split_rank[c.n])
                        r = (split_rank[c.n] - 1) % HL
                        width = len(c.kts) * c.cols
                        ch = wh[:, r, 0:width].rearrange("p (k n) -> p k n", k=len(c.kts))
                        cl = wl[:, r, 0:width].rearrange("p (k n) -> p k n", k=len(c.kts))
                    else:
                        pe.wait_ge(raw_in[c.n % RAW], loaded[c.n])
                        craw = raw[0:HD, c.n % RAW, :].rearrange("p (i n) -> p i n", n=CHID)
                    mm = None
                    for n, first, last, m, ks in c.tiles:
                        if first and plan.tiles[n][1] is not None:
                            evacuated(pe, plan.tiles[n][1])
                        ps = tile_bank(n)
                        if g.mode == "G":
                            for j in range(ST):
                                for k in range(8):
                                    js = slice(j * P, (j + 1) * P)
                                    mm = three(ps[:, j * 24:(j + 1) * 24], xh[:, k, js], xl[:, k, js], ch[:, k, :],
                                               cl[:, k, :], k == 0, k == 7)
                        elif g.mode == "C":
                            f = xh
                            for k, i in enumerate(ks):
                                mm = pe.matmul(ps[:, 0:GROUPS * NCMP], craw[:, k, m * P:(m + 1) * P], f[:, i, :],
                                               start=first and k == 0, stop=last and k == len(ks) - 1)
                        elif g.mode == "N":
                            for q, k in enumerate(ks):
                                js = slice(m * P, (m + 1) * P)
                                mm = three(ps[:, :], xh[:, k, js], xl[:, k, js], ch[:, q, :], cl[:, q, :],
                                           first and q == 0, last and q == len(ks) - 1)
                        else:
                            for q, k in enumerate(ks):
                                cs = slice(m * P, (m + 1) * P)
                                mm = three(ps[:, 0:ntok], ch[:, k, cs], cl[:, k, cs], xh[:, k, 0:ntok],
                                           xl[:, k, 0:ntok], q == 0, q == len(ks) - 1)
                        if last and n != c.tiles[-1][0]:
                            mm.then_inc(dense_done, 1)
                    mm.then_inc(dense_done if c.ends else chunk_used, 1)

            def turned_ready(phase, ntok):
                i = ntile[phase, ntok - 1]
                pe.wait_ge(lo_done, NT[i][3] + NT[i][2])

            def low_all(phase):
                turned_ready(phase, ST if phase not in ("mem", "mem2") else MT)

            pe.wait_ge(const_ready, 2)
            pe.wait_ge(rows_in_s, 16 * len(VECS))
            pe.wait_ge(pe_in_s, 64)
            pe.transpose(SB[1][:, 0:NCOL], rows_in[:, :], ident[0:NCOL, 0:NCOL])
            for i in range(2):
                mm = pe.transpose(SB[1][:, P + CMP * i:P + CMP * (i + 1)], pe_in[:, i, :, :].rearrange(
                    "p g d -> p (g d)"), ident[0:CMP, 0:CMP])
            mm.then_inc(vec_tr, 1)
            for j in range(ST):
                turn("x", j)
            low_all("x")

            def turn_rot(r):
                pe.wait_ge(rot_ready, r + 1)
                if r >= 2:
                    pe.wait_ge(qkT_ready, r - 1)
                transpose_blocks(TB[r % 2], qrot[:, r % 2, :], 4 if r < 4 else 2).then_inc(rot_tr, 1)
            dense("q", xTh, xTl)
            dense("kv", xTh, xTl)
            turn_rot(0), turn_rot(1)
            dense("kcvc", xTh, xTl)
            turn_rot(2), turn_rot(3)
            dense("gates", xTh, xTl)
            dense("bg", xTh, xTl)
            turn_rot(4), turn_rot(5)
            dense("cg", xTh, xTl)
            turn_rot(6), turn_rot(7)
            dense("xin", xTh, xTl)
            for i, (name, f) in enumerate((("cmp_kc", fk), ("cmp_vc", fv))):
                evacuated(pe, G["kcvc"].tiles[i])
                dense(name, f, None)
            for ct in range(4):
                pe.wait_ge(conv_sq, ct + 1)
                mm = pe.matmul(SB[1][:, :], ones[:, :], stage[:, ct // 2, (ct % 2) * S:(ct % 2) * S + S],
                               start=ct == 0, stop=ct == 3)
            mm.then_inc(conv_ss, 1)
            for j in range(MT):
                turn("mem", j)
            pe.wait_ge(w2_in, 32)
            evacuated(pe, G["cmp_vc"].tiles[1])
            low_all("mem")
            for g in range(GROUPS):
                for m in range(2):
                    pe.matmul(TB[0][0:NCMP, g * HD:(g + 1) * HD], hidk[:, m, g * NCMP:(g + 1) * NCMP], w2k[:, m, :],
                              start=m == 0, stop=m == 1)
            for g in range(GROUPS):
                for m in range(2):
                    mm = pe.matmul(TB[1][:, g * HD:(g + 1) * HD], hidv[:, m, g, :, :].rearrange("p r j -> p (r j)"),
                                   w2v[:, m, :], start=m == 0, stop=m == 1)
            mm.then_inc(cmp_kv, 1)
            pe.wait_ge(kc_rot, 1)
            pe.transpose(TB[0][:, 0:NCMP], kcr[0:NCMP, :], ident[0:NCMP, 0:NCMP]).then_inc(kc_tr, 1)
            pe.wait_ge(kcT_ready, 1)
            pe.wait_ge(cmp_kv_in, 4)
            for c in range(ST):
                if c:
                    pe.wait_ge(c_shift, c)
                for g in range(GROUPS):
                    for t in range(PER_GROUP):
                        ps = slice(HD * g, HD * g + HD)
                        o = t * NCMP
                        mm = pe.matmul(SB[g][:, o:o + NCMP], qT[ps, t, c * P:(c + 1) * P], kcT[ps, 0:NCMP],
                                       start=True, stop=True)
                    mm.then_inc(c_scores, 1)
                pe.wait_ge(c_exp, c + 1)
                if c:
                    pe.wait_ge(c_trin, c)
                for g in range(GROUPS):
                    mm = pe.transpose(TB[0][:, g * P:(g + 1) * P],
                                      pc[:, c % 2, 4 * g:4 * g + 4, :].rearrange("p h j -> p (h j)"), ident[:, :])
                mm.then_inc(c_tr, 1)
                pe.wait_ge(c_trin, c + 1)
                if c:
                    pe.wait_ge(c_used, c)
                for g in range(GROUPS):
                    mm = pe.matmul(bank[3][:, g * 256:(g + 1) * 256], pcT[:, g, :],
                                   vbd[:, g, :, :].rearrange("p r d -> p (r d)"), start=True, stop=True)
                mm.then_inc(c_out, 1)
            pe.wait_ge(c_used, ST)

            for s in range(len(ITEMS) + 2):
                if s < len(ITEMS):
                    qt, g, t = ITEMS[s]
                    ps = slice(HD * g, HD * g + HD)
                    for br in range(2):
                        if s:
                            pe.wait_ge(s_taken, 2 * s - 1 + br)
                        n = (qt + 1) * P
                        pe.matmul(SB[br][:, 0:n], qT[ps, t, qt * P:(qt + 1) * P], kT[ps, br, 0:n],
                                  start=True, stop=True).then_inc(s_done, 1)
                if 1 <= s <= len(ITEMS):
                    i = s - 1
                    k = ITEMS[i][0] + 1
                    for br, evac_sem in ((0, pt_a), (1, pt_v)):
                        pe.wait_ge(s_exp, 2 * i + br + 1)
                        if i:
                            pe.wait_ge(evac_sem, i)
                        transpose_blocks(TB[br], prob[:, i % 2, br, :], k).then_inc(pt_done, 1)
                if s >= 2:
                    i = s - 2
                    qt, g, t = ITEMS[i]
                    pe.wait_ge(pt_a, i + 1)
                    pe.wait_ge(pt_v, i + 1)
                    if i:
                        pe.wait_ge(o_taken, i)
                    for br in range(2):
                        for k in range(qt + 1):
                            mm = pe.matmul(bank[3][:, br * HD:(br + 1) * HD], probT[:, i % 2, br, k, :],
                                           kvn[:, k, 256 * br + P + HD * g:256 * br + P + HD * g + HD],
                                           start=k == 0, stop=k == qt)
                    mm.then_inc(pv_done, 1)
            for j in range(ST):
                turn("att", j)
            low_all("att")
            pe.wait_ge(conv_lo, 4)
            dense("out", xTh, xTl)
            dense("kx", memTh, memTl, MEM)
            turn("hx", 0), turn("hx", 1)
            dense("vx", memTh, memTl)
            turn("hx", 2), turn("hx", 3)
            low_all("hx")
            dense("qx", xTh, xTl)

            for n in G["qx"].tiles[-4:] + G["vx"].tiles[-4:]:
                evacuated(pe, n)
            for it in range(XH * ST + 2):
                if it < XH * ST:
                    hd, qt = it // ST, it % ST
                    if it >= 2:
                        pe.wait_ge(x_exp, it - 1)
                    for k in range(2):
                        mm = pe.matmul(SB[it % 2][:, 0:MEM], qxT[:, 2 * hd + k, qt * P:(qt + 1) * P],
                                       kxT[:, 2 * hd + k, :], start=k == 0, stop=k == 1)
                    mm.then_inc(x_scores, 1)
                if 1 <= it <= XH * ST:
                    i = it - 1
                    hd, qt = i // ST, i % ST
                    pe.wait_ge(x_norm, i + 1)
                    if qt == 0 and hd:
                        pe.wait_ge(x_pta, hd)
                        pe.wait_ge(x_ptv, hd)
                    for k in range(2):
                        mm = pe.transpose(TB[k][:, qt * P:(qt + 1) * P], xprob[:, i % 2, k * P:(k + 1) * P], ident[:, :])
                    mm.then_inc(x_tr, 1)
                if it % 4 == 1 and it > 1:
                    hd = it // 4 - 1
                    pe.wait_ge(x_pta, hd + 1)
                    pe.wait_ge(x_ptv, hd + 1)
                    for dt in range(2):
                        if hd:
                            pe.wait_ge(x_lo, 2 * (hd - 1) + dt + 1)
                        for k in range(2):
                            o = hd * XD + dt * P
                            mm = pe.matmul(bank[2 + dt][:, :], vx[:, k, o:o + P], xprobT[:, k, :],
                                           start=k == 0, stop=k == 1)
                        mm.then_inc(x_out, 1)
            pe.wait_ge(x_lo, 8)
            dense("ox", xTh, xTl)
            for j in range(ST):
                turn("hf", j)
            low_all("hf")

            ht = 0
            for s in range(3):
                dense(f"gu{s}", xTh, xTl)
                ht += len(G[f"gu{s}"].chunks)
                pe.wait_ge(hid_lo, ht)
                dense(f"down{s}", hidh, hidl)
            for j in range(ST):
                turn("h2", j)
            for j in range(MT):
                turn("mem2", j)
            low_all("mem2")

            dense("if", xTh, xTl)
            dense("qk2", xTh, xTl)
            dense("memkv", mem2Th, mem2Tl)
            dense("v2", xTh, xTl)
            dense("o2", xTh, xTl)
            pe.wait_ge(gr_em, 1)
            for a_i, row in enumerate((0, 5)):
                for t in range(ST):
                    o = (a_i * ST + t) * 36
                    mm = pe.transpose(TB[0][:, o:o + 36], gate_rows[:, row, t * P:(t + 1) * P], ident[0:36, 0:36])
            mm.then_inc(gr_tr, 1)
            dense("naqk", xTh, xTl)

            def turn_heads(t):
                pe.wait_ge(n_in, t + 1)
                if t >= 2:
                    pe.wait_ge(n_copied, t - 1)
                if t == 0:
                    pe.wait_ge(gr_col, 1)
                transpose_blocks(TB[t % 2], stage[:, t % 2, S:2 * S], 4 if t < 4 else 2).then_inc(n_tr, 1)
            for t in range(4):
                turn_heads(t)
            dense("navq", xTh, xTl)
            for t in range(4, 10):
                turn_heads(t)
            pe.wait_ge(n_copied, 10)

            pe.wait_ge(qk_ready, 4)
            pe.wait_ge(gr_neg, 1)
            for n in G["navq"].tiles:
                evacuated(pe, n)
            for it in range(2 * LH + 1):
                if it < 2 * LH:
                    d, hd = it // LH, it % LH
                    row = 32 * d + hd
                    if it:
                        pe.wait_ge(l_bcin, it)
                    pe.matmul(TB[0][:, :], bc(ident[0:36, row:row + 1], [36, P]), neg_max, start=True, stop=True)\
                        .then_inc(l_bc, 1)
                    ps = slice(LQ * (hd % 2), LQ * (hd % 2) + LQ)
                    for si in range(ST):
                        off, n, t0 = span(d, si)
                        k = ST * it + si
                        if k >= 2:
                            pe.wait_ge(l_mul, k - 1)
                        pe.matmul(SB[k % 2][:, 0:n], qkT[ps, 2 + hd // 2, si * P:(si + 1) * P],
                                  qkT[ps, hd // 2, t0:t0 + n], start=True, stop=True).then_inc(l_scores, 1)
                if it:
                    i = it - 1
                    d, hd = i // LH, i % LH
                    pe.wait_ge(l_mask, ST * (i + 1))
                    if i >= 2:
                        pe.wait_ge(l_used, i - 1)
                    pair = (bank[2], bank[3]) if i % 2 == 0 else (bank[0], bank[1])
                    for tt in range(ST):
                        keys = list(range(tt + 1)) if d == 0 else list(range(tt, ST))
                        for si in keys:
                            off, n, t0 = span(d, si)
                            q0 = off + tt * P - t0
                            mm = pe.matmul(pair[tt // 2][:, (tt % 2) * (LV + 1):(tt % 2 + 1) * (LV + 1)],
                                           decay[:, i % 2, q0:q0 + P], vext[:, si, hd, :],
                                           start=si == keys[0], stop=si == keys[-1])
                    mm.then_inc(l_out, 1)
            pe.wait_ge(l_used, 2 * LH)

            for s in range(NH * ST + 2):
                if s < NH * ST:
                    hd, qt = s // ST, s % ST
                    if s >= 2:
                        pe.wait_ge(a_taken, s - 1)
                    ps = slice(ND * (hd % 4), ND * (hd % 4) + ND)
                    pe.matmul(SB[s % 2][:, :], naT[ps, hd // 4, qt * P:(qt + 1) * P], naT[ps, 2 + hd // 4, :],
                              start=True, stop=True).then_inc(a_scores, 1)
                if 1 <= s <= NH * ST:
                    i = s - 1
                    pe.wait_ge(a_exp, i + 1)
                    if i >= 2:
                        pe.wait_ge((a_pta, a_ptv)[i % 2], i // 2)
                    transpose_blocks(TB[i % 2], nprob[:, i % 2, :], ST).then_inc(a_tr, 1)
                if s >= 2:
                    i = s - 2
                    hd, qt = i // ST, i % ST
                    pe.wait_ge((a_pta, a_ptv)[i % 2], i // 2 + 1)
                    o = (qt % 2) * 256 + hd * ND
                    for k in range(ST):
                        mm = pe.matmul(bank[2 + qt // 2][:, o:o + ND], nprobT[:, i % 2, k, :],
                                       navq[:, k, hd * ND:(hd + 1) * ND], start=k == 0, stop=k == ST - 1)
                    mm.then_inc(a_out, 1)
            pe.wait_ge(a_exp, NH * ST)
            pe.matmul(SB[0][:, 0:NH * ST], antident[:, :], small[:, 32:32 + NH * ST], start=True, stop=True)\
                .then_inc(a_den, 1)
            for j in range(ST):
                turn("hm", j)
            for j in range(ST):
                turn("hna", j)
            low_all("hna")

            for it in range(MH * ST + 2):
                if it < MH * ST:
                    hd, qt = it // ST, it % ST
                    if it >= 2:
                        pe.wait_ge(m_exp, it - 1)
                    ps = slice(MD * (hd % 2), MD * (hd % 2) + MD)
                    pe.matmul(SB[it % 2][:, 0:MEM], qmT[ps, hd // 2, qt * P:(qt + 1) * P], kmT[ps, hd // 2, :],
                              start=True, stop=True).then_inc(m_scores, 1)
                if 1 <= it <= MH * ST:
                    i = it - 1
                    hd, qt = i // ST, i % ST
                    pe.wait_ge(m_norm, i + 1)
                    if qt == 0 and hd:
                        pe.wait_ge(m_pta, hd)
                        pe.wait_ge(m_ptv, hd)
                    for k in range(2):
                        mm = pe.transpose(TB[k][:, qt * P:(qt + 1) * P], mprob[:, i % 2, k * P:(k + 1) * P], ident[:, :])
                    mm.then_inc(m_tr, 1)
                if it % 4 == 1 and it > 1:
                    hd = it // 4 - 1
                    pe.wait_ge(m_pta, hd + 1)
                    pe.wait_ge(m_ptv, hd + 1)
                    for k in range(2):
                        o = 256 + hd * MD
                        ps = slice(MD * (hd % 2), MD * (hd % 2) + MD)
                        mm = pe.matmul(bank[2 + hd // 2][ps, :], memkv[:, k, o:o + MD], mprobT[:, k, :],
                                       start=k == 0, stop=k == 1)
                    mm.then_inc(m_out, 1)
            pe.wait_ge(m_lo, 2)

            for cp in range(4):
                dense(f"gate2_{cp}", xTh, xTl)
                dense(f"proj2_{cp}", hmTh, hmTl)
            pe.wait_ge(y_lo, 8)
            dense("out2", yTh, yTl)
            for j in range(ST):
                turn("h4", j)
            low_all("h4")
            for s in range(4):
                dense(f"up{s}", xTh, xTl)
                ht += 8
                pe.wait_ge(hid_lo, ht)
                dense(f"dn{s}", hidh, hidl)


INPUTS = (
    "x mem positions norm_mix_pre w_in conv_w pe_kc w1_kc w2_kc pe_vc w1_vc w2_vc norm_conv_out norm_attn_out "
    "w_out norm_mix_post norm_x_pre norm_mem w_q_x w_kv_x w_o_x norm_x_post norm_ffn_pre w_gate_up w_down "
    "norm_ffn_post mem_2 g_mix_2 w_in_2 conv_w_2 conv_b_2 b_igate_2 b_fgate_2 g_mlstm_2 w_proj_mlstm_2 g_na_q_2 "
    "g_na_k_2 rpb_2 w_proj_na_2 g_mem_2 w_mem_kv_2 g_mem_q_2 g_mem_k_2 w_proj_mem_2 w_out_2 g_ffn_2 w_up_2 "
    "w_down_2").split()


def kernel(**inputs):
    import concourse.bacc as bacc
    from concourse.bass_utils import run_bass_kernel_spmd

    nc = bacc.Bacc("TRN2", target_bir_lowering=False, num_devices=1)
    arrays, views = {}, {}
    for name in INPUTS:
        v = np.ascontiguousarray(inputs[name])
        if v.shape[0] == 1:
            v = v[0]
        arrays["in_" + name] = v
        views[name] = nc.dram_tensor("in_" + name, v.shape, mybir.dt.from_np(v.dtype), kind="ExternalInput").ap()
    out = nc.dram_tensor("out_0", (1, S, D), F32, kind="ExternalOutput").ap()
    program(nc, views, out[0])
    result = run_bass_kernel_spmd(nc, [arrays], core_ids=[0])
    return result.results[0]["out_0"]
```

```python
from contextlib import ExitStack

import numpy as np

import concourse.bass as bass
from concourse import mybir

F32 = mybir.dt.float32
F32R = mybir.dt.float32r
I32 = mybir.dt.int32
ALU = mybir.AluOpType
ACT = mybir.ActivationFunctionType
X = mybir.AxisListType.X

P = 128
D, S, MEM = 1024, 512, 256
KT, ST, MT = D // P, S // P, MEM // P
EPS = 1e-6
HD = 64
GROUPS, PER_GROUP = 2, 4
CMP, CSTRIDE = 32, 16
NCMP = (S - CMP) // CSTRIDE + 1
CHID = 256
XH, XD = 4, 256
FF1, FF2 = 2816, 4096
THETA = 10000.0
NEG = -1e30
MAGIC = 12582912.0
TWO_PI = (6.28125, 0.0019340515136718750, 0.00000125566500146)
CW = 2048
RAW, HL = 3, 2
NH, ND = 8, 32
GW = 64
NWIN = 16
ROFF, COFF = 15, 31
LH, LQ, LV = 4, 64, 128
MH, MD = 4, 64

VECS = [("norm_mix_pre", 8), ("norm_x_pre", 8), ("norm_mem", 8), ("norm_ffn_pre", 8), ("g_mix_2", 8),
        ("g_mem_2", 8), ("g_ffn_2", 8), ("norm_conv_out", 4), ("norm_attn_out", 4), ("g_mlstm_2", 4),
        ("conv_w", 12), ("conv_w_2", 20), ("conv_b_2", 4)]
COL = {}
_n = 0
for _name, _rows in VECS:
    COL[_name] = _n
    _n += _rows
NCOL = _n


class Chunk:

    def __init__(self, group, srcs, kts, cols, split=True):
        self.group, self.srcs, self.kts, self.cols, self.split = group, srcs, kts, cols, split
        self.tiles = []


class Group:

    def __init__(self, name, mode, readers):
        self.name, self.mode, self.readers = name, mode, readers
        self.chunks, self.tiles = [], []


class Plan:

    def __init__(self):
        self.groups, self.chunks, self.tiles = {}, [], []
        self.bank_owner = {}
        self.banks, self.turn = (0, 1, 2, 3), 0
        self.rank = {"A": 0, "V": 0, "H": 0, "X": 0}

    def use(self, *banks):
        self.banks, self.turn = banks, 0

    def tile(self, g):
        n = len(self.tiles)
        bank = self.banks[self.turn % len(self.banks)]
        self.turn += 1
        before = self.bank_owner.get(bank)
        ranks = {}
        for r in g.readers:
            self.rank[r] += 1
            ranks[r] = self.rank[r]
        self.tiles.append((bank, before, ranks))
        self.bank_owner[bank] = n
        g.tiles.append(n)
        return n

    def chunk(self, g, c):
        c.n = len(self.chunks)
        self.chunks.append(c)
        g.chunks.append(c)

    def group(self, name, mode, readers):
        g = self.groups[name] = Group(name, mode, readers)
        return g

    def columns(self, name, w, cols, readers="A"):
        g = self.group(name, "T", readers)
        for c0 in cols:
            c = Chunk(g, [(0, 8, 0, 256, w[:, c0:c0 + 256])], list(range(8)), 256)
            for m in range(2):
                c.tiles.append((self.tile(g), True, True, m, list(range(8))))
            self.chunk(g, c)

    def rows(self, name, w, c0, halves, ntok, readers="A", k0=0, kts=8):
        g = self.group(name, "N", readers)
        for half in range(halves):
            tiles = [self.tile(g) for _ in range(ntok)]
            ks = list(range(kts))
            parts = [ks[i:i + 4] for i in range(0, kts, 4)]
            for i, part in enumerate(parts):
                r0 = (k0 + part[0]) * P
                src = w[r0:r0 + len(part) * P, c0 + 512 * half:c0 + 512 * half + 512]
                c = Chunk(g, [(0, len(part), 0, 512, src)], part, 512)
                for j, n in enumerate(tiles):
                    c.tiles.append((n, i == 0, i == len(parts) - 1, j, part))
                self.chunk(g, c)


def make_plan(a):
    p = Plan()
    w_in = a["w_in"]
    p.rows("q", w_in, 1536, 1, 4)
    p.rows("kv", w_in, 2304, 1, 4)
    p.columns("kcvc", w_in, [2048], readers="V")
    g = p.group("gates", "G", "A")
    c = Chunk(g, [(0, 8, 0, 24, w_in[:, 2816:2840])], list(range(8)), 24)
    c.tiles.append((p.tile(g), True, True, 0, list(range(8))))
    p.chunk(g, c)
    for name in ("kc", "vc"):
        g = p.group("cmp_" + name, "C", "A")
        tiles = [p.tile(g), p.tile(g)]
        for i in range(2):
            c = Chunk(g, [(0, 8, 0, 256, a["w1_" + name][i * 1024:(i + 1) * 1024, :])], list(range(8)), 256,
                      split=False)
            for m, n in enumerate(tiles):
                c.tiles.append((n, i == 0, i == 1, m, [8 * i + k for k in range(8)]))
            p.chunk(g, c)
    p.use(0, 1)
    p.columns("bg", w_in, [0, 256])
    p.columns("cg", w_in, [512, 768])
    p.columns("xin", w_in, [1024, 1280], readers="V")
    p.columns("kx", a["w_kv_x"], [0, 256, 512, 768])
    p.use(0, 1, 2, 3)
    p.rows("out", a["w_out"], 0, 2, 4)
    p.use(0, 1)
    p.rows("vx", a["w_kv_x"], 1024, 2, 2, readers="X")
    p.columns("qx", a["w_q_x"], [0, 256, 512, 768])
    p.use(0, 1, 2, 3)
    p.rows("ox", a["w_o_x"], 0, 2, 4)
    for s, (k0, n) in enumerate(((0, 8), (8, 8), (16, 6))):
        g = p.group(f"gu{s}", "T", "A")
        for k in range(k0, k0 + n):
            c = Chunk(g, [(0, 8, 0, 128, a["w_gate_up"][:, k * P:(k + 1) * P]),
                          (0, 8, 128, 256, a["w_gate_up"][:, FF1 + k * P:FF1 + (k + 1) * P])],
                      list(range(8)), 256)
            g.readers = "A"
            c.tiles.append((p.tile(g), True, True, 0, list(range(8))))
            g.readers = "H"
            c.tiles.append((p.tile(g), True, True, 1, list(range(8))))
            p.chunk(g, c)
        p.rows(f"down{s}", a["w_down"], 0, 2, 4, k0=k0, kts=n, readers="A" if s == 0 else "V")
    w2 = a["w_in_2"]
    g = p.group("if", "I", "A")
    c = Chunk(g, [(0, 8, 0, 16, w2[:, 1536:1552])], list(range(8)), 128)
    c.tiles.append((p.tile(g), True, True, 0, list(range(8))))
    p.chunk(g, c)
    p.columns("qk2", w2, [0, 256])
    p.rows("memkv", a["w_mem_kv_2"], 0, 1, 2)
    p.rows("v2", w2, 512, 1, 4)
    p.rows("o2", w2, 1024, 1, 4)
    p.rows("naqk", w2, 1552, 1, 4)
    p.rows("navq", w2, 2064, 1, 4)
    p.use(0, 1)
    p.columns("gate2", w2, [2576 + b * D + cp * 256 for cp in range(4) for b in range(3)])
    p.use(0, 1, 2, 3)
    for cp in range(4):
        g = p.group(f"proj2_{cp}", "T", "V")
        cs = slice(cp * 256, cp * 256 + 256)
        c = Chunk(g, [(0, 4, 0, 256, a["w_proj_mlstm_2"][:, cs]), (4, 6, 0, 256, a["w_proj_na_2"][:, cs]),
                      (6, 8, 0, 256, a["w_proj_mem_2"][:, cs])], list(range(8)), 256)
        for m in range(2):
            for ks in ([0, 1, 2, 3], [4, 5], [6, 7]):
                c.tiles.append((p.tile(g), True, True, m, ks))
        p.chunk(g, c)
    p.rows("out2", a["w_out_2"], 0, 2, 4, readers="V")
    for s in range(4):
        p.columns(f"up{s}", a["w_up_2"], [s * 1024 + 256 * i for i in range(4)])
        p.rows(f"dn{s}", a["w_down_2"], 0, 2, 4, k0=8 * s, readers="V")
    rank = 0
    for c in p.chunks:
        c.ends = c.tiles[-1][2]
        if not c.ends:
            rank += 1
            c.rank = rank
    return p


class Own:

    def __init__(self, eng, chain):
        self.eng, self.chain, self.count = eng, chain, {}

    def tell(self, ins, sem):
        self.count[sem.name] = self.count.get(sem.name, 0) + 1
        ins.then_inc(sem, 1)
        self.eng.wait_ge(sem, self.count[sem.name])

    def link(self, ins):
        self.tell(ins, self.chain)


def norm_tiles():
    out, base = [], 0
    for phase, ntok, banks, kt0, gain in (
            ("x", ST, 2, 0, COL["norm_mix_pre"]), ("mem", MT, 2, 0, COL["norm_mem"]),
            ("att", ST, 1, 4, COL["norm_attn_out"]), ("hx", ST, 2, 0, COL["norm_x_pre"]),
            ("hf", ST, 2, 0, COL["norm_ffn_pre"]), ("h2", ST, 2, 0, COL["g_mix_2"]),
            ("mem2", MT, 2, 0, COL["g_mem_2"]), ("hm", ST, 1, 0, COL["g_mlstm_2"]),
            ("hna", ST, 1, 4, None), ("h4", ST, 2, 0, COL["g_ffn_2"])):
        for j in range(ntok):
            out.append((phase, j, banks, base, kt0, gain))
            base += banks
    return out


def program(nc, a, out):
    plan = make_plan(a)
    G = plan.groups
    NT = norm_tiles()
    ntile = {(t[0], t[1]): i for i, t in enumerate(NT)}
    splits = [c for c in plan.chunks if c.split]
    split_rank = {c.n: i + 1 for i, c in enumerate(splits)}

    with ExitStack() as ctx:
        def sb(name, shape, dt=F32):
            return ctx.enter_context(nc.sbuf_tensor(name, shape, dt))

        def sem(name):
            return ctx.enter_context(nc.semaphore(name))

        h = sb("h", [P, ST, D])
        xTh, xTl = sb("xT_high", [P, KT, S], F32R), sb("xT_low", [P, KT, S], F32R)
        raw = sb("raw", [P, RAW, CW])
        wh, wl = sb("w_high", [P, HL, CW], F32R), sb("w_low", [P, HL, CW], F32R)
        stage = sb("stage", [P, 2, D])
        qbuf = sb("qbuf", [P, 2, S])
        junk = sb("junk", [P, D], mybir.dt.bfloat16)
        ident = sb("ident", [P, P])
        ones = sb("ones", [P, P])
        antident = sb("antident", [P, P])
        gcol = sb("gcol", [P, NCOL])
        rms = sb("rms", [P, 64])
        gates = sb("gates", [P, ST, 24])
        cmask = sb("cmask", [P, ST, NCMP])
        small = sb("small", [P, 96])
        share = sb("share", [P, 512])
        share2 = sb("share2", [P, D])
        eps_col = sb("eps_col", [P, 1])

        rpb_zero = sb("rpb_zero", [1, 64])
        acol = sb("acol", [P, 2, ST, 36])
        arena_bytes = 77888
        arena_at = nc.sbuf_base
        sb("arena", [P, arena_bytes // 4])

        def at(name, off, shape, dt=F32):
            size = 4
            for n in shape[1:]:
                size *= n
            assert off + size <= arena_bytes, name
            return nc.alloc_sbuf_tensor_at(name, shape, dt, offset=arena_at + off)

        zT = at("zT", 0, [P, 4, S + 2])
        bgT = at("bgT", 8256, [P, 4, S])
        memTh, memTl = at("memT_high", 0, [P, KT, MEM], F32R), at("memT_low", 8192, [P, KT, MEM], F32R)
        fk, fv = (at("blocks_k", 16448, [P, CMP // 2, GROUPS * NCMP]),
                  at("blocks_v", 20448, [P, CMP // 2, GROUPS * NCMP]))
        prob = at("prob", 16448, [P, 2, 2, S])
        probT = at("probT", 24640, [P, 2, 2, ST, P])
        kxT, vx = at("kxT", 69696, [P, KT, MEM]), at("vx", 61504, [P, MT, D])
        qT = at("qT", 32832, [P, PER_GROUP, S])
        kT = at("kT", 41024, [P, 2, S])
        kvn = at("kvn", 45120, [P, ST, S])
        ynat = at("ynat", 32832, [P, ST, D])
        qxT = at("qxT", 32832, [P, KT, S])
        yatt = at("yatt", 53312, [P, ST, S])
        qn = at("qn", 53312, [P, 2, S])
        qrot = at("qrot", 57408, [P, 2, S])
        mem_nat = at("mem_nat", 61504, [P, MT, D])
        xprob, xprobT = at("xprob", 53312, [P, 2, MEM]), at("xprobT", 55360, [P, MT, S])
        oxTh, oxTl = at("oxT_high", 0, [P, KT, S], F32R), at("oxT_low", 16448, [P, KT, S], F32R)
        silu = at("silu", 53312, [P, 2, S])
        o = 61504
        hidk = at("hidk", o, [P, 2, GROUPS * NCMP])
        hidv = at("hidv", o + 512, [P, 2, GROUPS, 4, 32])
        vbd = at("vbd", o + 2560, [P, GROUPS, 4, HD])
        scb = at("scb", o + 4608, [P, 8, NCMP])
        pc = at("pc", o + 5632, [P, 2, 8, 32])
        pcT = at("pcT", o + 7680, [P, 2, P])
        kcn, kcr = at("kcn", o + 8704, [32, P]), at("kcr", o + 9216, [32, P])
        kcT = at("kcT", o + 9728, [P, 32])
        cosT, sinT = at("cosT", o + 9856, [P, 5, HD]), at("sinT", o + 11136, [P, 5, HD])
        w2k, w2v = at("w2k", o + 12416, [P, 2, HD]), at("w2v", o + 12928, [P, 2, HD])
        peT = at("peT", o + 13440, [P, 2, CMP])
        posf = at("posf", o + 13696, [P, 5])
        posi = at("posi", o + 13728, [P, 5], I32)
        invf = at("invf", o + 13760, [P, 32])
        ang = at("ang", 24640, [P, 5, 32])
        angk = at("angk", 25280, [P, 5, 32])
        rows_in = at("rows_in", 25920, [NCOL, P])
        pe_in = at("pe_in", 26560, [CMP, 2, 2, HD])
        rtmp = at("rtmp", o, [P, 2, S])
        hidh, hidl = at("hid_high", 0, [P, 8, S], F32R), at("hid_low", 16384, [P, 8, S], F32R)
        vext = at("vext", 0, [P, ST, LH, LV + 1])
        og = at("og", 8256, [P, ST, S])
        navq = at("navq", 16448, [P, ST, S])
        naT = at("naT", 24640, [P, 4, S])
        qmT, kmT = at("qmT", 32832, [P, 2, S]), at("kmT", 36928, [P, 2, MEM])
        memkv = at("memkv", 38976, [P, MT, S])
        hsum = at("hsum", 43072, [P, ST, S])
        hna = at("hna", 51264, [P, ST, NH * ND])
        gate_rows = at("gate_rows", 43072, [36, 6, S])
        mem_nat2 = at("mem_nat2", 61504, [P, MT, D])
        qkT = at("qkT", 55360, [P, 4, S])
        qkc = at("qkc", 63552, [P, 4, S + 4])
        mem2Th, mem2Tl = at("mem2T_high", 16448, [P, KT, MEM], F32R), at("mem2T_low", 24640, [P, KT, MEM], F32R)
        decay = at("decay", 63552, [P, 2, 1280])
        maxb = at("maxb", 73792, [P, 2, S])
        bias2 = at("bias_even", 51264, [P, 16, GW]), at("bias_odd", 0, [P, 16, GW])
        nprob, nprobT = at("nprob", 63552, [P, 2, S]), at("nprobT", 67648, [P, 2, ST, P])
        mprob, mprobT = at("mprob", 63552, [P, 2, MEM]), at("mprobT", 65600, [P, MT, S])
        hmTh, hmTl = at("hmT_high", 0, [P, KT, S], F32R), at("hmT_low", 16448, [P, KT, S], F32R)
        yTh, yTl = at("yT_high", 32832, [P, KT, S], F32R), at("yT_low", 49216, [P, KT, S], F32R)
        sg = at("sg", 65600, [P, 2, 3, S])

        causal = share
        na_gain = share[:, :].rearrange("p (h d) -> p h d", d=ND)
        gpost = share2
        mem_gain = share2[:, 0:512].rearrange("p (h d) -> p h d", d=MD)
        neg_max = share2[0:36, 512:1024]

        bank = [ctx.enter_context(nc.psum_tensor(f"bank{i}", [P, S], F32)) for i in range(8)]
        TB, SB = (bank[4], bank[5]), (bank[6], bank[7])

        gate_dram = nc.dram_tensor("gate_dram", [8, 3, P, S], F32, kind="Internal").ap()
        rpb_pad = nc.dram_tensor("rpb_pad", [1, 64 + NH * ROFF * COFF + 64], F32, kind="Internal").ap()

        raw_in = [sem(f"raw_in{i}") for i in range(RAW)]
        wh_done, wl_done, chunk_used = sem("wh_done"), sem("wl_done"), sem("chunk_used")
        dense_done, dense_a, dense_v = sem("dense_done"), sem("dense_evac_act"), sem("dense_evac_dve")
        act_chain, dve_chain, pool_chain = sem("act_chain"), sem("dve_chain"), sem("pool_chain")
        x_in = [sem(f"x_in{j}") for j in range(ST)]
        rows_in_s, pe_in_s, pos_in = sem("vectors_in"), sem("pe_in_done"), sem("pos_in")
        w2_in, gpost_in, mem_in, mem2_in = sem("w2_in"), sem("gpost_in"), sem("mem_in"), sem("mem2_in")
        bias_in = [sem("bias_in0"), sem("bias_in1")]
        pad_in, gain2_in, ifb_in = sem("pad_in"), sem("gain2_in"), sem("gate_bias_in")
        pad_zero, const_ready, b2_const = sem("pad_zero"), sem("const_ready"), sem("b2_const")
        rms_done, xn_ready, tr_done = sem("rms_done"), sem("xn_ready"), sem("tr_done")
        q_ready, hi_done, lo_done, h_ready = sem("q_ready"), sem("hi_done"), sem("lo_done"), sem("h_ready")
        vec_tr, vec_col = sem("vec_transposed"), sem("vec_columns")
        qn_in, rot_ready, rot_tr, qkT_ready = sem("qn_in"), sem("rot_ready"), sem("rot_transposed"), sem("qkT_ready")
        rope_ang, rope_sin, rope_ready = sem("rope_angle"), sem("rope_sine"), sem("rope_ready")
        conv_y, conv_sq, conv_ss, conv_rms, conv_q, conv_hi, conv_lo = (
            sem("conv_y"), sem("conv_square"), sem("conv_sum"), sem("conv_rms"), sem("conv_q"),
            sem("conv_hi"), sem("conv_lo"))
        blocks_ready, hid_zero, cmp_kv, cmp_kv_in, kc_rot, kc_tr, kcT_ready = (
            sem("blocks_ready"), sem("hid_zero"), sem("cmp_kv"), sem("cmp_kv_in"), sem("kc_rot"), sem("kc_tr"),
            sem("kcT_ready"))
        c_scores, c_shift, c_exp, c_tr, c_trin, c_out, c_used = (
            sem("c_scores"), sem("c_shifted"), sem("c_exp"), sem("c_tr"), sem("c_tr_in"), sem("c_out"), sem("c_used"))
        s_done, s_taken, s_max, s_exp, pt_done, pt_a, pt_v, pv_done, o_taken = (
            sem("s_done"), sem("s_taken"), sem("s_max"), sem("s_exp"), sem("pt_done"), sem("pt_act"), sem("pt_dve"),
            sem("pv_done"), sem("o_taken"))
        x_scores, x_max, x_exp, x_norm, x_tr, x_pta, x_ptv, x_out, x_hi, x_lo = (
            sem("x_scores"), sem("x_max"), sem("x_exp"), sem("x_norm"), sem("x_tr"), sem("x_pt_act"),
            sem("x_pt_dve"), sem("x_out"), sem("x_hi"), sem("x_lo"))
        hid_q, hid_hi, hid_lo = sem("hid_q"), sem("hid_hi"), sem("hid_lo")
        spread_zero, vx_taken = sem("spread_zero"), sem("vx_taken")
        n_raw, n_norm, n_tr, n_in, n_copied = sem("n_raw"), sem("n_norm"), sem("n_tr"), sem("n_ready"), sem("n_copied")
        qk_conv, qk_ready = sem("qk_conv"), sem("qk_ready")
        gr_lin, gr_exp, gr_ln, gr_max, gr_em, gr_tr, gr_col, gr_neg = (
            sem("gr_lin"), sem("gr_exp"), sem("gr_ln"), sem("gr_max"), sem("gr_em"), sem("gr_tr"), sem("gr_col"),
            sem("gr_neg"))
        l_bc, l_bcin, l_scores, l_shift, l_exp, l_mul, l_mask, l_out, l_used = (
            sem("l_bc"), sem("l_bc_in"), sem("l_scores"), sem("l_shift"), sem("l_exp"), sem("l_mul"),
            sem("l_mask"), sem("l_out"), sem("l_used"))
        b_masked, a_scores, a_taken, a_max, a_exp, a_tr, a_pta, a_ptv, a_out = (
            sem("b_masked"), sem("a_scores"), sem("a_taken"), sem("a_max"), sem("a_exp"), sem("a_tr"),
            sem("a_pt_act"), sem("a_pt_dve"), sem("a_out"))
        a_den = sem("a_den")
        spill_out, gate_in, gate_ready = (
            [sem("spill_even"), sem("spill_odd")], [sem("gate_in_0"), sem("gate_in_1")], sem("gate_ready"))
        m_scores, m_max, m_exp, m_norm, m_tr, m_pta, m_ptv, m_out, m_hi, m_lo = (
            sem("m_scores"), sem("m_max"), sem("m_exp"), sem("m_norm"), sem("m_tr"), sem("m_pt_act"),
            sem("m_pt_dve"), sem("m_out"), sem("m_hi"), sem("m_lo"))
        y_q, y_hi, y_lo, out_done = sem("y_q"), sem("y_hi"), sem("y_lo"), sem("out_done")

        block = ctx.enter_context(nc.Block())

        def evacuated(eng, n):
            for r, rank in plan.tiles[n][2].items():
                eng.wait_ge({"A": dense_a, "V": dense_v, "H": hid_q, "X": vx_taken}[r], rank)

        def tile_bank(n):
            return bank[plan.tiles[n][0]]

        def used(eng, c):
            if c.ends:
                eng.wait_ge(dense_done, c.tiles[-1][0] + 1)
            else:
                eng.wait_ge(chunk_used, c.rank)

        def group_used(eng, name):
            used(eng, G[name].chunks[-1])

        gate_tiles = [(c, k) for c in G["gate2"].chunks for k in range(2)]
        H_PIECES, L_PIECES, A_PIECES = 4, 13, 2
        assert 6 * H_PIECES + 2 * LH * L_PIECES + NH * ST * A_PIECES == 8 * len(gate_tiles)

        def pieces(*names):
            return [(c, k, q) for name in names for c in G[name].chunks for k in range(2) for q in range(8)]
        early, middle, late = pieces("bg"), pieces("cg", "xin"), pieces("kx")
        CONV_AT, MEM_AT, KX_AT = 17, 20, 24

        def cmp_pieces(c):
            return early[8 * c:8 * c + 8]

        def item_pieces(s):
            return middle[4 * s:4 * s + 4] if s < 16 else late[8 * (s - KX_AT):8 * (s - KX_AT) + 8] if s >= KX_AT else []

        def head_pieces(it):
            return pieces("qx")[16 + 4 * it:20 + 4 * it]

        def na_piece(s):
            return lstm_piece(2 * LH) + s * A_PIECES

        def lstm_piece(it):
            return 6 * H_PIECES + it * L_PIECES

        def bc(ap, shape):
            return ap.broadcast_to(shape)

        @block.sync
        def _(sp):
            xv = a["x"].rearrange("(j p) d -> p j d", p=P)
            for j in range(ST):
                sp.dma_start(h[:, j, :], xv[:, j, :]).then_inc(x_in[j], 16)

            r = 0
            for name, n in VECS:
                src = a[name]
                src = src.rearrange("(r q) -> r q", q=P) if len(src.shape) == 1 else \
                    src.rearrange("k (r q) -> (k r) q", q=P)
                sp.dma_start(rows_in[r:r + n, :], src).then_inc(rows_in_s, 16)
                r += n

            def position_loads():
                sp.wait_ge(const_ready, 1)
                ps = a["positions"]
                for j in range(ST):
                    sp.dma_start(posi[:, j:j + 1], bass.AP(ps.tensor, j * P, [[1, P], [1, 1]])).then_inc(pos_in, 16)
                sp.dma_start(posi[0:NCMP, 4:5], bass.AP(ps.tensor, CMP - 1, [[CSTRIDE, NCMP], [1, 1]]),
                             allow_slow_non_contiguous=True).then_inc(pos_in, 16)

            def small_loads():
                sp.wait_ge(pad_zero, 1)
                for o in (0, 64 + NH * ROFF * COFF):
                    sp.dma_start(rpb_pad[0:1, o:o + 64], rpb_zero[0:1, :]).then_inc(pad_in, 16)
                sp.dma_start(rpb_pad[0:1, 64:64 + NH * ROFF * COFF],
                             a["rpb_2"].rearrange("h r c -> (h r c)").rearrange("(o n) -> o n", o=1))\
                    .then_inc(pad_in, 16)
                for t, n in ((w2k, "w2_kc"), (w2v, "w2_vc")):
                    sp.dma_start(t[:, :, :], a[n].rearrange("(m p) d -> p m d", p=P)).then_inc(w2_in, 16)

            before = {
                "kv": lambda: position_loads(),
                "kcvc": lambda: small_loads(),
                "kx": lambda: late_mem(),
                "out": lambda: post_gain("norm_mix_post", None),
                "ox": lambda: post_gain("norm_x_post", ("h", 4)),
                "gu0": lambda: second_memory(),
                "gu2": lambda: post_gain("norm_ffn_post", ("h", 8)),
                "qk2": lambda: second_block_loads(),
                "proj2_1": lambda: gates_back(0),
                "proj2_2": lambda: gates_back(1),
                "proj2_3": lambda: gates_back(2),
                "out2": lambda: gates_back(3),
            }

            def late_mem():
                sp.wait_ge(c_used, ST)
                sp.dma_start(mem_nat[:, :, :], a["mem"].rearrange("(j p) d -> p j d", p=P)).then_inc(mem_in, 16)

            def second_memory():
                sp.wait_ge(x_out, 2 * XH)
                sp.dma_start(mem_nat2[:, :, :], a["mem_2"].rearrange("(j p) d -> p j d", p=P)).then_inc(mem2_in, 16)

            def post_gain(name, after):
                if after:
                    sp.wait_ge(h_ready, after[1])
                sp.dma_start(gpost[:, :], a[name].rearrange("(o d) -> o d", o=1).broadcast_to([P, D]))\
                    .then_inc(gpost_in, 16)

            def second_block_loads():
                sp.wait_ge(h_ready, 12)
                gq = a["g_na_q_2"].rearrange("(o d) -> o d", o=1)
                gk = a["g_na_k_2"].rearrange("(o d) -> o d", o=1)
                for i, g in enumerate((gq, gk)):
                    sp.dma_start(na_gain[:, 8 * i:8 * i + 8, :], bass.AP(g.tensor, 0, [[0, P], [0, 8], [1, ND]]))\
                        .then_inc(gain2_in, 16)
                for i, n in enumerate(("g_mem_q_2", "g_mem_k_2")):
                    sp.dma_start(mem_gain[:, 4 * i:4 * i + 4, :], bass.AP(a[n].tensor, 0, [[0, P], [0, 4], [1, MD]]))\
                        .then_inc(gain2_in, 16)
                for i, n in enumerate(("b_igate_2", "b_fgate_2")):
                    for d in range(2):
                        sp.dma_start(small[32 * d:32 * d + 4, 88 + i:89 + i], a[n][d, :].rearrange("(h o) -> h o", o=1))\
                            .then_inc(ifb_in, 16)

            def gates_back(cp):
                if cp == 0:
                    sp.wait_ge(m_out, MH)
                    for e in range(2):
                        sp.wait_ge(spill_out[e], 16 * 12)
                for i in (2 * cp, 2 * cp + 1):
                    if i >= 2:
                        sp.wait_ge(y_q, i - 1)
                    sp.dma_start(sg[:, i % 2, :, :], gate_dram[i, :, :, :].rearrange("b p s -> p b s"))\
                        .then_inc(gate_in[i % 2], 16)

            for c in plan.chunks:
                if c is c.group.chunks[0] and c.group.name in before:
                    before[c.group.name]()
                if c.n >= RAW:
                    old = plan.chunks[c.n - RAW]
                    if old.split:
                        sp.wait_ge(wh_done, split_rank[old.n])
                        sp.wait_ge(wl_done, split_rank[old.n])
                    else:
                        used(sp, old)
                slot = raw[:, c.n % RAW, :]
                for k0, k1, c0, c1, src in c.srcs:
                    width = c.cols if c.group.mode != "I" else 16
                    dst = slot[:, 0:len(c.kts) * width].rearrange("p (k n) -> p k n", n=width)
                    sp.dma_start(dst[:, k0:k1, c0:c1], src.rearrange("(k p) n -> p k n", p=P))\
                        .then_inc(raw_in[c.n % RAW], 16)
            ov = out.rearrange("(j p) d -> p j d", p=P)
            for half in range(2):
                for j in range(ST):
                    evacuated(sp, G["dn3"].tiles[4 * half + j])
                    cs = slice(512 * half, 512 * half + 512)
                    sp.dma_start(ov[:, j, cs], h[:, j, cs]).then_inc(out_done, 16)
            sp.wait_ge(out_done, 16 * 8)

        loaded = {}
        count = [0] * RAW
        for c in plan.chunks:
            count[c.n % RAW] += 16 * len(c.srcs)
            loaded[c.n] = count[c.n % RAW]

        def split_slot(c, t):
            if t is raw:
                slot = raw[:, c.n % RAW, :]
                if c.group.mode == "I":
                    return slot[:, 0:P].rearrange("p (k q e) -> p k q e", q=4, e=4)
            else:
                slot = t[:, (split_rank[c.n] - 1) % HL, :]
                if c.group.mode == "I":
                    return slot[:, 0:8 * P].rearrange("p (k q e) -> p k q e", q=4, e=32)[:, :, :, 0:4]
            return slot[:, 0:len(c.kts) * c.cols]

        @block.gpsimd
        def _(pool):
            own = Own(pool, pool_chain)
            own.link(pool.memset(posi[:, :], 0))
            own.link(pool.memset(small[:, :], 0.0))
            own.tell(pool.memset(eps_col[:, :], EPS), const_ready)
            own.link(pool.memset(ident[:, :], 0.0))
            own.tell(pool.affine_select(out=ident[:, :], in_=ident[:, :], compare_op=ALU.not_equal, fill=1.0,
                                        base=0, pattern=[[-1, P]], channel_multiplier=1), const_ready)
            own.link(pool.memset(ones[:, :], 1.0))
            own.link(pool.memset(antident[:, :], 0.0))
            own.link(pool.affine_select(out=antident[:, :], in_=antident[:, :], compare_op=ALU.not_equal, fill=1.0,
                                        base=1 - P, pattern=[[1, P]], channel_multiplier=1))
            own.link(pool.memset(causal[:, :], 0.0))
            own.link(pool.affine_select(out=causal[:, 384:512], in_=causal[:, 384:512], compare_op=ALU.is_ge,
                                        fill=NEG, base=0, pattern=[[-1, P]], channel_multiplier=1))
            own.link(pool.memset(cmask[:, :, :], 0.0))
            own.link(pool.affine_select(out=cmask[:, :, :], in_=cmask[:, :, :], compare_op=ALU.is_ge, fill=NEG,
                                        base=-(CMP - 1), pattern=[[P, ST], [-CSTRIDE, NCMP]], channel_multiplier=1))
            own.link(pool.memset(small[:, 95:96], 1.0))
            own.link(pool.affine_select(out=small[:, 95:96], in_=small[:, 95:96], compare_op=ALU.is_ge, fill=0.0,
                                        base=-(CMP - 1), pattern=[[0, 1]], channel_multiplier=1))
            for j in range(32):
                own.link(pool.memset(invf[:, j:j + 1], float(np.float32(THETA ** (-j / 32.0)))))
            own.link(pool.memset(zT[:, :, 0:2], 0.0))
            own.tell(pool.memset(pc[:, :, :, :], 0.0), const_ready)
            own.tell(pool.memset(rpb_zero[:, :], 0.0), pad_zero)

            done = [0]

            def low_parts(upto):
                while done[0] < len(splits) and splits[done[0]].n <= upto:
                    c = splits[done[0]]
                    done[0] += 1
                    if c.group.mode == "I":
                        r = (split_rank[c.n] - 1) % HL
                        used(pool, splits[done[0] - 1 - HL])
                        own.link(pool.tensor_copy(wh[:, r, 0:8 * P], bc(small[:, 94:95], [P, 8 * P])))
                        own.tell(pool.tensor_copy(wl[:, r, 0:8 * P], bc(small[:, 94:95], [P, 8 * P])), spread_zero)
                    pool.wait_ge(wh_done, split_rank[c.n])
                    own.tell(pool.tensor_tensor(split_slot(c, wl), split_slot(c, raw), split_slot(c, wh).bitcast(F32),
                                                ALU.subtract), wl_done)

            low_parts(G["gates"].chunks[-1].n)
            pool.wait_ge(qkT_ready, 8)
            own.link(pool.memset(vbd[:, :, :, :], 0.0))
            own.tell(pool.memset(hidv[:, :, :, :, :], 0.0), hid_zero)
            low_parts(G["if"].chunks[-1].n)
            pool.wait_ge(h_ready, 12)
            pool.wait_ge(xn_ready, ntile["mem2", 1] + 1)
            own.link(pool.memset(qkc[:, :, 0:2], 0.0))
            own.tell(pool.memset(qkc[:, :, S + 2:S + 4], 0.0), b2_const)
            low_parts(G["memkv"].chunks[-1].n)
            own.tell(pool.memset(vext[:, :, :, LV:LV + 1], 1.0), b2_const)
            low_parts(G["gate2"].chunks[0].n)
            def gate_low(u0, n):
                for u in range(u0, u0 + n):
                    if u % 16 == 0:
                        low_parts(gate_tiles[u // 8][0].n + 1)

            gate_low(0, 6 * H_PIECES)

            for it in range(2 * LH):
                d = it // LH
                off = 0
                gate_low(lstm_piece(it), L_PIECES)
                for si in range(ST):
                    pool.wait_ge(l_mul, ST * it + si + 1)
                    n = (ST - si) * P if d == 0 else (si + 1) * P
                    dg = off if d == 0 else off + si * P
                    blk = decay[:, it % 2, dg:dg + P]
                    own.tell(pool.affine_select(out=blk, in_=blk, compare_op=ALU.is_ge, fill=0.0, base=0,
                                                pattern=[[1 if d == 0 else -1, P]],
                                                channel_multiplier=-1 if d == 0 else 1), l_mask)
                    off += n

            def mask_bias(hd):
                pool.wait_ge(bias_in[hd % 2], 32 * (hd // 2 + 1))
                for rr in range(2):
                    ps = slice(64 - 64 * rr, P - 64 * rr)
                    t = bias2[hd % 2][ps, rr:rr + ROFF, :]
                    lo, hi = t[:, :, 0:GW - NWIN], t[:, :, NWIN:GW]
                    own.link(pool.affine_select(out=lo, in_=lo, compare_op=ALU.is_ge, fill=NEG,
                                                base=NWIN // 2 - (GW - 1),
                                                pattern=[[0, ROFF], [1, GW - NWIN]], channel_multiplier=1))
                    own.tell(pool.affine_select(out=hi, in_=hi, compare_op=ALU.is_ge, fill=NEG,
                                                base=NWIN // 2 - 1 - NWIN + GW - 1,
                                                pattern=[[0, ROFF], [-1, GW - NWIN]], channel_multiplier=-1), b_masked)
            mask_bias(0)
            for s in range(NH * ST):
                if s % ST == 0 and s < NH * ST - ST:
                    mask_bias(s // ST + 1)
                gate_low(na_piece(s), A_PIECES)
            low_parts(len(plan.chunks))

        STATS = [("x", j) for j in range(4)] + [("mem", j) for j in range(2)] + [("att", j) for j in range(4)]
        for ph, nx in (("yo", "hx"), ("yx", "hf"), ("yf", "h2")):
            STATS += [(ph, 0), (ph, 1), (nx, 0), (ph, 2), (nx, 1), (ph, 3), (nx, 2), (nx, 3)]
        STATS += [("mem2", j) for j in range(2)] + [("h4", j) for j in range(4)]

        SOURCES = {"x": h, "hx": h, "hf": h, "h2": h, "h4": h, "mem": mem_nat, "mem2": mem_nat2, "att": yatt}
        TURNED = {"mem": (memTh, memTl), "mem2": (mem2Th, mem2Tl), "hm": (hmTh, hmTl), "hna": (hmTh, hmTl)}

        FREE = {"hx": "out", "hf": "ox", "h2": "gu2", "mem2": "down2", "h4": "gate2"}

        def turned(i, b, low):
            phase, j, banks, first, kt0, gain = NT[i]
            t = TURNED.get(phase, (xTh, xTl))[low]
            blocks = 2 if phase == "hna" else 4
            return t[:, kt0 + 4 * b:kt0 + 4 * b + blocks, j * P:(j + 1) * P], blocks

        ITEMS = [(qt, g, t) for qt in range(ST) for g in range(GROUPS) for t in range(PER_GROUP)]
        LSPAN = {0: [(ST - si) * P for si in range(ST)], 1: [(si + 1) * P for si in range(ST)]}

        def span(d, si):
            return sum(LSPAN[d][:si]), LSPAN[d][si], si * P if d == 0 else 0

        @block.scalar
        def _(act):
            own = Own(act, act_chain)
            done = [0]

            def high(upto):
                while done[0] < len(splits) and splits[done[0]].n <= upto:
                    r = done[0]
                    c = splits[r]
                    done[0] += 1
                    act.wait_ge(raw_in[c.n % RAW], loaded[c.n])
                    if r >= HL:
                        used(act, splits[r - HL])
                    if c.group.mode == "I":
                        act.wait_ge(spread_zero, 1)
                    own.tell(act.copy(split_slot(c, wh), split_slot(c, raw)), wh_done)

            def stat(key, src, width):
                i = STATS.index(key)
                if key[0] == "x":
                    act.wait_ge(x_in[key[1]], 16)
                r = rms[:, i:i + 1]
                own.link(act.activation(junk[:, 0:width], src, ACT.Square, accum_out=r))
                own.tell(act.activation(r, r, ACT.Sqrt, bias=eps_col[:, 0:1], scale=1.0 / width), rms_done)

            def hi(i):
                if NT[i][0] in FREE:
                    group_used(act, FREE[NT[i][0]])
                for b in range(NT[i][2]):
                    r = NT[i][3] + b
                    dst, n = turned(i, b, 0)
                    act.wait_ge(q_ready, r + 1)
                    own.tell(act.copy(dst, qbuf[:, r % 2, 0:n * P].rearrange("p (k t) -> p k t", k=n)), hi_done)

            def norm(phase, ntok, width):
                for j in range(ntok):
                    src = SOURCES[phase]
                    stat((phase, j), src[:, j, :], width)
                    if j:
                        hi(ntile[phase, j - 1])
                hi(ntile[phase, ntok - 1])

            def evac(group, write, between=None):
                g = G[group]
                for c in g.chunks:
                    high(c.n + 1)
                    for n, first, last, m, ks in c.tiles:
                        if last and "A" in plan.tiles[n][2]:
                            act.wait_ge(dense_done, n + 1)
                            write(g.tiles.index(n), tile_bank(n))
                    if between:
                        between(c)

            for i, n in enumerate(("pe_kc", "pe_vc")):
                for g in range(2):
                    act.dma_start(pe_in[:, i, g, :], a[n]).then_inc(pe_in_s, 16)
            act.wait_ge(const_ready, 1)
            for j in range(ST):
                stat(("x", j), h[:, j, :], D)
                if j:
                    hi(ntile["x", j - 1])
                if j >= 2:
                    high(j - 2)
            hi(ntile["x", 3])
            act.wait_ge(rope_ang, 1)
            own.link(act.activation(sinT[:, :, 32:64], ang[:, :, :], ACT.Sin))
            own.tell(act.activation(angk[:, :, :], ang[:, :, :], ACT.Sin, scale=0.5), rope_sin)

            def q_out(t, src):
                if t >= 2:
                    act.wait_ge(rot_ready, t - 1)
                own.tell(act.copy(qn[:, t % 2, :], src[:, :]), dense_a)
            evac("q", q_out)
            evac("kv", lambda t, src: own.tell(act.copy(kvn[:, t, :], src[:, :]), dense_a))
            evac("kcvc", None)
            evac("gates", lambda t, src: own.tell(
                act.activation(gates[:, :, :], src[:, 0:4 * 24].rearrange("p (j c) -> p j c", j=4), ACT.Sigmoid),
                dense_a))

            act.wait_ge(qkT_ready, 8)
            act.wait_ge(hid_zero, 1)
            evac("cmp_kc", lambda m, src: own.tell(
                act.activation(hidk[:, m, :], src[:, 0:GROUPS * NCMP], ACT.Silu), dense_a))

            def hidv_out(m, src):
                v = src[:, 0:GROUPS * NCMP].rearrange("p (g j) -> p g j", g=GROUPS)
                for g in range(GROUPS):
                    ins = act.activation(hidv[:, m, g, :, 0:NCMP], bc(v[:, g, None, :], [P, 4, NCMP]), ACT.Silu)
                    own.tell(ins, dense_a) if g == GROUPS - 1 else own.link(ins)
            evac("cmp_vc", hidv_out)

            copy_out = {"bg": lambda t, src: act.copy(bgT[:, t, :], src[:, :]),
                        "cg": lambda t, src: act.copy(zT[:, t, 2:S + 2], src[:, :]),
                        "kx": lambda t, src: act.copy(kxT[:, t, :], src[:, 0:MEM]),
                        "qx": lambda t, src: act.copy(qxT[:, t, :], src[:, :])}

            def pieces_out(ps):
                for c, k, q in ps:
                    if k == q == 0:
                        high(c.n + 1)
                    if q == 7 and c.group.name in copy_out:
                        n = c.tiles[k][0]
                        act.wait_ge(dense_done, n + 1)
                        own.tell(copy_out[c.group.name](c.group.tiles.index(n), tile_bank(n)), dense_a)

            def conv_square(ct):
                act.wait_ge(conv_y, ct + 1)
                own.tell(act.activation(stage[:, ct // 2, (ct % 2) * S:(ct % 2) * S + S], bgT[:, ct, :], ACT.Square),
                         conv_sq)

            def conv_root():
                act.wait_ge(conv_ss, 1)
                own.tell(act.activation(stage[:, 0, 0:S], bank[2][:, :], ACT.Sqrt, bias=eps_col[:, 0:1],
                                        scale=1.0 / 512), conv_rms)

            def conv_high():
                group_used(act, "xin")
                for ct in range(4):
                    act.wait_ge(conv_q, ct + 1)
                    own.tell(act.copy(xTh[:, ct, :], qbuf[:, ct % 2, :]), conv_hi)

            for c in range(ST):
                act.wait_ge(c_shift, c + 1)
                if c >= 2:
                    act.wait_ge(c_tr, c - 1)
                own.tell(act.activation(pc[:, c % 2, :, 0:NCMP], scb[:, :, :], ACT.Exp, scale=HD ** -0.5), c_exp)
                pieces_out(cmp_pieces(c))

            for s in range(len(ITEMS) + 1):
                if s < len(ITEMS):
                    n = (ITEMS[s][0] + 1) * P
                    act.wait_ge(s_max, s + 1)
                    for br in range(2):
                        own.tell(act.activation(prob[:, s % 2, br, 0:n], prob[:, s % 2, br, 0:n], ACT.Exp,
                                                bias=small[:, 4 * (s % 2) + br:4 * (s % 2) + br + 1],
                                                scale=HD ** -0.5,
                                                accum_out=small[:, 8 + 2 * (s % 4) + br:9 + 2 * (s % 4) + br]), s_exp)
                if s >= 1:
                    i = s - 1
                    k = ITEMS[i][0] + 1
                    act.wait_ge(pt_done, 2 * i + 1)
                    if i >= 2:
                        act.wait_ge(pv_done, i - 1)
                    own.tell(act.copy(probT[:, i % 2, 0, 0:k, :],
                                      TB[0][:, 0:k * P].rearrange("p (k q) -> p k q", k=k)), pt_a)
                pieces_out(item_pieces(s))
                if s >= 10 and s % 2 == 0 and s < 18:
                    conv_square((s - 10) // 2)
                if s == CONV_AT:
                    conv_root()
                if s == CONV_AT + 1:
                    conv_high()
                if s == MEM_AT:
                    act.wait_ge(mem_in, 16)
                    stat(("mem", 0), mem_nat[:, 0, :], D)
                    stat(("mem", 1), mem_nat[:, 1, :], D)
                if s == MEM_AT + 2:
                    hi(ntile["mem", 0])
                    hi(ntile["mem", 1])
            act.wait_ge(o_taken, len(ITEMS))
            norm("att", ST, 512)

            def residual_stat(hname, j, src_ready):
                act.wait_ge(h_ready, src_ready + j + 1)
                stat((hname, j), h[:, j, :], D)

            def post(group, yname, hname, src_ready, filler=None):
                g = G[group]
                last = g.tiles[-4:]
                for c in g.chunks:
                    high(c.n + 1)
                    for n, first, lastc, j, ks in c.tiles:
                        if not lastc:
                            continue
                        half = g.tiles.index(n) // 4
                        if "A" in plan.tiles[n][2]:
                            act.wait_ge(dense_done, n + 1)
                            own.tell(act.copy(ynat[:, j, 512 * half:512 * half + 512], tile_bank(n)[:, :]), dense_a)
                        if half == 1:
                            if "V" in plan.tiles[n][2]:
                                evacuated(act, n)
                            stat((yname, j), ynat[:, j, :], D)
                            if j:
                                residual_stat(hname, j - 1, src_ready)
                            if filler:
                                filler(j)
                            if j >= 2:
                                hi(ntile[hname, j - 2])
                residual_stat(hname, 3, src_ready)
                hi(ntile[hname, 2])
                hi(ntile[hname, 3])

            def vx_out(j):
                g = G["vx"]
                high(g.chunks[j].n + 1)
                if j % 2:
                    for t in (j - 1, j):
                        n = g.tiles[t]
                        act.wait_ge(dense_done, n + 1)
                        own.tell(act.copy(vx[:, t % 2, 512 * (t // 2):512 * (t // 2) + 512], tile_bank(n)[:, :]),
                                 vx_taken)
            post("out", "yo", "hx", 0, vx_out)
            pieces_out(pieces("qx")[0:16])

            def x_high(hd):
                for dt in range(2):
                    act.wait_ge(x_out, 2 * hd + dt + 1)
                    own.tell(act.copy(oxTh[:, 2 * hd + dt, :], bank[2 + dt][:, :]), x_hi)

            def x_pt(hd):
                act.wait_ge(x_tr, ST * (hd + 1))
                if hd:
                    act.wait_ge(x_out, 2 * hd)
                own.tell(act.copy(xprobT[:, 0, :], TB[0][:, :]), x_pta)
            for it in range(XH * ST):
                act.wait_ge(x_max, it + 1)
                if it >= 2:
                    act.wait_ge(x_tr, it - 1)
                own.tell(act.activation(xprob[:, it % 2, :], SB[it % 2][:, 0:MEM], ACT.Exp,
                                        bias=small[:, it % 2:it % 2 + 1], scale=XD ** -0.5,
                                        accum_out=small[:, 2 + it % 2:3 + it % 2]), x_exp)
                pieces_out(head_pieces(it))
                if it % 4 == 0 and it:
                    x_pt(it // 4 - 1)
                if it % 4 == 2 and it > 4:
                    x_high(it // 4 - 1)
            x_pt(XH - 1)
            x_high(XH - 1)
            post("ox", "yx", "hf", 4)

            ht = 0
            for s in range(3):
                for c in G[f"gu{s}"].chunks:
                    high(c.n + 1)
                    n = c.tiles[0][0]
                    act.wait_ge(dense_done, n + 1)
                    if ht >= 2:
                        act.wait_ge(hid_q, ht - 1)
                    own.tell(act.activation(silu[:, ht % 2, :], tile_bank(n)[:, :], ACT.Silu), dense_a)
                    act.wait_ge(hid_q, ht + 1)
                    if s and c is G[f"gu{s}"].chunks[0]:
                        group_used(act, f"down{s - 1}")
                    own.tell(act.copy(hidh[:, ht % 8, :], qbuf[:, ht % 2, :]), hid_hi)
                    ht += 1
                if s == 0:
                    evac("down0", lambda t, src: own.tell(
                        act.copy(ynat[:, t % 4, 512 * (t // 4):512 * (t // 4) + 512], src[:, :]), dense_a))
                elif s == 1:
                    evac("down1", None)
                else:
                    post("down2", "yf", "h2", 8)

            act.wait_ge(mem2_in, 16)
            stat(("mem2", 0), mem_nat2[:, 0, :], D)
            stat(("mem2", 1), mem_nat2[:, 1, :], D)

            def if_out(t, src):
                own.link(act.copy(gate_rows[:, 0, :], src[0:36, :]))
                own.tell(act.copy(gate_rows[:, 1, :], src[64:100, :]), dense_a)
            evac("if", if_out)
            hi(ntile["mem2", 0])
            hi(ntile["mem2", 1])
            act.wait_ge(b2_const, 1)
            evac("qk2", lambda t, src: own.tell(act.copy(qkc[:, t, 2:S + 2], src[:, :]), dense_a))
            evac("memkv", lambda t, src: own.tell(act.copy(memkv[:, t, :], src[:, :]), dense_a))
            act.wait_ge(gr_lin, 1)
            own.link(act.activation(gate_rows[:, 2, :], gate_rows[:, 2, :], ACT.Exp, scale=-1.0))
            own.tell(act.activation(gate_rows[:, 2, :], gate_rows[:, 2, :], ACT.Ln, bias=ones[0:36, 0:1]), gr_ln)
            for ct in range(4):
                act.wait_ge(qk_conv, ct + 1)
                own.tell(act.activation(qkT[:, ct, :], qkT[:, ct, :], ACT.Silu), qk_ready)
            act.wait_ge(gr_max, 1)
            own.tell(act.activation(gate_rows[:, 5, :], gate_rows[:, 5, :], ACT.Exp, scale=-1.0), gr_em)
            act.wait_ge(b2_const, 2)
            evac("v2", lambda t, src: own.tell(
                act.copy(vext[:, t, :, 0:LV], src[:, :].rearrange("p (h v) -> p h v", h=LH)), dense_a))
            evac("o2", lambda t, src: own.tell(act.activation(og[:, t, :], src[:, :], ACT.Sigmoid), dense_a))

            def naqk_out(t, src):
                if t >= 2:
                    act.wait_ge(n_tr, t - 1)
                own.tell(act.copy(stage[:, t % 2, 0:S], src[:, :]), dense_a)
                n_root(t)

            def n_root(t):
                act.wait_ge(n_raw, t + 1)
                w = 16 if t < 4 else 4
                own.tell(act.activation(small[:, 16:16 + w], small[:, 16:16 + w], ACT.Sqrt, bias=eps_col[:, 0:1],
                                        scale=1.0 / (ND if t < 4 else MD)), n_norm)
            evac("naqk", naqk_out)
            evac("navq", lambda t, src: own.tell(act.copy(navq[:, t, :], src[:, :]), dense_a))

            def window_bias(hd):
                src = bass.AP(rpb_pad.tensor, 64 + hd * ROFF * COFF + NWIN - GW, [[1, GW], [COFF, ROFF], [1, GW]])
                for rr in range(2):
                    act.dma_start(bias2[hd % 2][64 - 64 * rr:P - 64 * rr, rr:rr + ROFF, :], src)\
                        .then_inc(bias_in[hd % 2], 16)

            def gate_high(u0, n):
                for u in range(u0, u0 + n):
                    if u % 16 == 0:
                        high(gate_tiles[u // 8][0].n + 1)

            def gate_out(u0, n):
                for u in range(u0, u0 + n):
                    if u % 8 == 7:
                        spill(u // 8)

            def spill(e):
                c, k = gate_tiles[e]
                n = c.tiles[k][0]
                act.wait_ge(dense_done, n + 1)
                if e >= 2:
                    act.wait_ge(spill_out[e % 2], 16 * (e // 2))
                own.tell(act.copy(qbuf[:, e % 2, :], tile_bank(n)[:, :]), dense_a)
                act.dma_start(gate_dram[2 * (e // 6) + k, (e % 6) // 2, :, :], qbuf[:, e % 2, :])\
                    .then_inc(spill_out[e % 2], 16)

            for t in range(4, 10):
                n_root(t)
                gate_high((t - 4) * H_PIECES, H_PIECES)
                gate_out((t - 4) * H_PIECES, H_PIECES)

            act.wait_ge(pad_in, 48)
            for it in range(2 * LH):
                d = it // LH
                act.wait_ge(l_bc, it + 1)
                if it >= 2:
                    act.wait_ge(l_shift, ST * (it - 1))
                own.tell(act.copy(maxb[:, it % 2, :], bank[4][:, :]), l_bcin)
                for si in range(ST):
                    off, n, t0 = span(d, si)
                    act.wait_ge(l_shift, ST * it + si + 1)
                    own.tell(act.activation(decay[:, it % 2, off:off + n], decay[:, it % 2, off:off + n], ACT.Exp), l_exp)
                if it == LH:
                    window_bias(0)
                gate_high(lstm_piece(it), L_PIECES)
                gate_out(lstm_piece(it), L_PIECES)

            for s in range(NH * ST + 1):
                if s == 0:
                    act.wait_ge(l_used, 2 * LH)
                    window_bias(1)
                if s < NH * ST:
                    act.wait_ge(a_max, s + 1)
                    if s % ST == 0 and ST <= s < NH * ST - ST:
                        window_bias(s // ST + 1)
                    own.tell(act.activation(nprob[:, s % 2, :], nprob[:, s % 2, :], ACT.Exp,
                                            bias=small[:, s % 2:s % 2 + 1],
                                            accum_out=small[:, 32 + s:33 + s]), a_exp)
                if s >= 1 and (s - 1) % 2 == 0:
                    i = s - 1
                    act.wait_ge(a_tr, i + 1)
                    if i >= 2:
                        act.wait_ge(a_out, i - 1)
                    own.tell(act.copy(nprobT[:, i % 2, :, ::-1], TB[i % 2][:, :].rearrange("p (k q) -> p k q", k=ST)),
                             a_pta)
                if s < NH * ST:
                    gate_high(na_piece(s), A_PIECES)
                    gate_out(na_piece(s), A_PIECES)
            for j in range(ST):
                act.wait_ge(n_raw, 10 + j + 1)
                own.tell(act.activation(small[:, 16:20], small[:, 16:20], ACT.Sqrt, bias=eps_col[:, 0:1],
                                        scale=1.0 / LV), n_norm)
                if j:
                    hi(ntile["hm", j - 1])
            hi(ntile["hm", 3])
            for j in range(ST):
                hi(ntile["hna", j])

            def m_pt(hd):
                act.wait_ge(m_tr, ST * (hd + 1))
                if hd:
                    act.wait_ge(m_out, hd)
                own.tell(act.copy(mprobT[:, 0, :], TB[0][:, :]), m_pta)
            for it in range(MH * ST):
                act.wait_ge(m_max, it + 1)
                if it >= 2:
                    act.wait_ge(m_tr, it - 1)
                own.tell(act.activation(mprob[:, it % 2, :], SB[it % 2][:, 0:MEM], ACT.Exp,
                                        bias=small[:, it % 2:it % 2 + 1],
                                        accum_out=small[:, 2 + it % 2:3 + it % 2]), m_exp)
                if it % 4 == 0 and it:
                    m_pt(it // 4 - 1)
            m_pt(MH - 1)
            for t in range(2):
                act.wait_ge(m_out, 2 * t + 2)
                own.tell(act.copy(hmTh[:, 6 + t, :], bank[2 + t][:, :]), m_hi)

            for i in range(8):
                high(G[f"proj2_{i // 2}"].chunks[-1].n + i % 2)
                act.wait_ge(gate_in[i % 2], 16 * (i // 2 + 1))
                own.tell(act.activation(sg[:, i % 2, :, :], sg[:, i % 2, :, :], ACT.Sigmoid), gate_ready)
                if i:
                    act.wait_ge(y_q, i)
                    own.tell(act.copy(yTh[:, i - 1, :], qbuf[:, (i - 1) % 2, :]), y_hi)
            act.wait_ge(y_q, 8)
            own.tell(act.copy(yTh[:, 7, :], qbuf[:, 1, :]), y_hi)
            for c in G["out2"].chunks:
                high(c.n + 1)
            for j in range(ST):
                evacuated(act, G["out2"].tiles[4 + j])
                stat(("h4", j), h[:, j, :], D)
                if j:
                    hi(ntile["h4", j - 1])
            hi(ntile["h4", 3])
            for s in range(4):
                for c in G[f"up{s}"].chunks:
                    high(c.n + 1)
                    for n, *_ in c.tiles:
                        act.wait_ge(dense_done, n + 1)
                        if ht >= 2:
                            act.wait_ge(hid_q, ht - 1)
                        own.tell(act.activation(silu[:, ht % 2, :], tile_bank(n)[:, :], ACT.Relu), dense_a)
                        act.wait_ge(hid_q, ht + 1)
                        if s and n == G[f"up{s}"].tiles[0]:
                            group_used(act, f"dn{s - 1}")
                        own.tell(act.copy(hidh[:, (ht - 22) % 8, :], qbuf[:, ht % 2, :]), hid_hi)
                        ht += 1
                for c in G[f"dn{s}"].chunks:
                    high(c.n + 1)

        @block.vector
        def _(dve):
            own = Own(dve, dve_chain)

            def xn(phase, j, width):
                i = ntile[phase, j]
                k = STATS.index((phase, j))
                dve.wait_ge(rms_done, k + 1)
                own.link(dve.reciprocal(rms[:, k:k + 1], rms[:, k:k + 1]))
                if i >= 2:
                    dve.wait_ge(tr_done, NT[i - 2][3] + NT[i - 2][2])
                own.tell(dve.tensor_scalar(stage[:, i % 2, 0:width], SOURCES[phase][:, j, :], rms[:, k:k + 1], None,
                                           ALU.mult), xn_ready)

            def ql(phase, j):
                i = ntile[phase, j]
                first, gain = NT[i][3], NT[i][5]
                for b in range(NT[i][2]):
                    r = first + b
                    _, n = turned(i, b, 1)
                    dve.wait_ge(tr_done, r + 1)
                    src = TB[r % 2][:, 0:n * P].rearrange("p (k t) -> p k t", k=n)
                    q = qbuf[:, r % 2, 0:n * P].rearrange("p (k t) -> p k t", k=n)
                    if gain is None:
                        own.tell(dve.tensor_copy(q, src), q_ready)
                    else:
                        gv = gcol[:, gain + 4 * b:gain + 4 * b + n]
                        own.tell(dve.tensor_tensor(q, src, bc(gv[:, :, None], [P, n, P]), ALU.mult), q_ready)
                for b in range(NT[i][2]):
                    r = first + b
                    dst, n = turned(i, b, 1)
                    top, _ = turned(i, b, 0)
                    dve.wait_ge(hi_done, r + 1)
                    q = qbuf[:, r % 2, 0:n * P].rearrange("p (k t) -> p k t", k=n)
                    own.tell(dve.tensor_tensor(dst, q, top.bitcast(F32), ALU.subtract), lo_done)

            def norm(phase, ntok, width):
                for j in range(ntok):
                    xn(phase, j, width)
                    if j:
                        ql(phase, j - 1)
                ql(phase, ntok - 1)

            def tile_in(name, t):
                n = G[name].tiles[t]
                dve.wait_ge(dense_done, n + 1)
                return tile_bank(n)

            dve.wait_ge(vec_tr, 1)
            own.link(dve.tensor_copy(gcol[:, :], SB[1][:, 0:NCOL]))
            own.tell(dve.tensor_copy(peT[:, :, :], SB[1][:, P:P + 2 * CMP].rearrange("p (i c) -> p i c", i=2)), vec_col)

            norm("x", ST, D)
            dve.wait_ge(const_ready, 3)
            dve.wait_ge(pos_in, 16 * (ST + 1))
            own.link(dve.tensor_copy(posf[:, :], posi[:, :]))
            own.link(dve.tensor_tensor(ang[:, :, :], bc(posf[:, :, None], [P, 5, 32]), bc(invf[:, None, :], [P, 5, 32]),
                                       ALU.mult))
            own.link(dve.tensor_scalar(angk[:, :, :], ang[:, :, :], float(1 / (2 * np.pi)), MAGIC, ALU.mult, ALU.add))
            own.link(dve.tensor_scalar(angk[:, :, :], angk[:, :, :], -MAGIC, None, ALU.add))
            for part in TWO_PI:
                own.link(dve.scalar_tensor_tensor(out=ang[:, :, :], in0=angk[:, :, :], scalar=-part, in1=ang[:, :, :],
                                                  op0=ALU.mult, op1=ALU.add))
            own.tell(dve.tensor_scalar(ang[:, :, :], ang[:, :, :], 3.1415925, -3.1415925, ALU.min, ALU.max), rope_ang)
            dve.wait_ge(rope_sin, 1)
            own.link(dve.tensor_scalar(sinT[:, :, 0:32], sinT[:, :, 32:64], -1.0, None, ALU.mult))
            own.link(dve.tensor_tensor(angk[:, :, :], angk[:, :, :], angk[:, :, :], ALU.mult))
            for o in (0, 32):
                own.link(dve.tensor_scalar(cosT[:, :, o:o + 32], angk[:, :, :], -2.0, 1.0, ALU.mult, ALU.add))

            def rotate(dst, src, heads, t, np_=P):
                pr, sw = rtmp[0:np_, 0, 0:heads * HD], rtmp[0:np_, 1, 0:heads * HD]
                v = lambda z: z.rearrange("p (h d) -> p h d", h=heads)
                w = lambda z: z.rearrange("p (h a d) -> p h a d", h=heads, a=2)
                own.link(dve.tensor_tensor(v(pr), src, bc(cosT[0:np_, t, None, :], [np_, heads, HD]), ALU.mult))
                own.link(dve.tensor_tensor(
                    w(sw), src.rearrange("p h (a d) -> p h a d", a=2)[:, :, ::-1, :],
                    bc(sinT[0:np_, t, None, :].rearrange("p h (a d) -> p h a d", a=2), [np_, heads, 2, 32]), ALU.mult))
                return dst(dve.tensor_tensor, v(pr), v(sw))

            def rope_q(j):
                n = G["q"].tiles[j]
                evacuated(dve, n)
                if j >= 2:
                    dve.wait_ge(rot_tr, j - 1)
                src = qn[:, j % 2, :].rearrange("p (h d) -> p h d", d=HD)
                out_v = qrot[:, j % 2, :].rearrange("p (t g d) -> p g t d", t=PER_GROUP, g=GROUPS)

                def add(tt, x, y):
                    s4 = lambda z: z.rearrange("p (g t) d -> p g t d", g=GROUPS)
                    own.tell(tt(out_v, s4(x), s4(y), ALU.add), rot_ready)
                rotate(add, src, 8, j)

            def rope_k(j):
                evacuated(dve, G["kv"].tiles[j])
                dve.wait_ge(rot_tr, 4 + j - 1)
                for br in range(2):
                    src = kvn[:, j, 256 * br:256 * br + P].rearrange("p (g d) -> p g d", g=GROUPS)
                    dst = qrot[:, j % 2, br * P:br * P + P].rearrange("p (g d) -> p g d", g=GROUPS)

                    def add(tt, x, y, dst=dst, br=br):
                        ins = tt(dst, x, y, ALU.add)
                        own.tell(ins, rot_ready) if br else own.link(ins)
                    rotate(add, src, GROUPS, j)

            def rot_copy(r):
                dve.wait_ge(rot_tr, r + 1)
                n = 4 if r < 4 else 2
                dst = qT if r < 4 else kT
                j = r % 4
                own.tell(dve.tensor_copy(dst[:, :, j * P:(j + 1) * P],
                                         TB[r % 2][:, 0:n * P].rearrange("p (k t) -> p k t", k=n)), qkT_ready)
            rope_q(0), rope_q(1), rot_copy(0), rot_copy(1), rope_q(2), rope_q(3)
            for i, f in enumerate((fk, fv)):
                src = tile_in("kcvc", i)
                for g in range(GROUPS):
                    ps = slice(HD * g, HD * g + HD)
                    for odd in range(2):
                        s = src[ps, odd:odd + 1]
                        tokens = bass.AP(s.tensor, s.offset, [[s.ap[0][0], HD], [2, CMP // 2], [CSTRIDE, NCMP]])
                        ins = dve.tensor_tensor(f[HD * odd:HD * odd + HD, :, g * NCMP:(g + 1) * NCMP], tokens,
                                                bc(peT[ps, i, odd::2, None], [HD, CMP // 2, NCMP]), ALU.add)
                        own.tell(ins, dense_v) if g == odd == 1 else own.link(ins)
            rot_copy(2), rot_copy(3), rope_k(0), rope_k(1), rot_copy(4), rot_copy(5), rope_k(2), rope_k(3)
            rot_copy(6), rot_copy(7)


            dve.wait_ge(cmp_kv, 1)
            own.link(dve.tensor_copy(kcn[0:NCMP, :], TB[0][0:NCMP, 0:P]))
            for hh in range(4):
                ps = slice(32 * hh, 32 * hh + 32)
                own.tell(dve.tensor_copy(vbd[ps, :, hh, :], TB[1][ps, 0:P].rearrange("p (g d) -> p g d", g=GROUPS)),
                         cmp_kv_in)

            def kc_add(tt, x, y):
                own.tell(tt(kcr[0:NCMP, :].rearrange("p (g d) -> p g d", g=GROUPS), x, y, ALU.add), kc_rot)
            krp, krs = qbuf[0:NCMP, 0, 0:P], qbuf[0:NCMP, 1, 0:P]
            v2 = lambda z: z.rearrange("p (g d) -> p g d", g=GROUPS)
            v3 = lambda z: z.rearrange("p (g a d) -> p g a d", g=GROUPS, a=2)
            own.link(dve.tensor_tensor(v2(krp), v2(kcn[0:NCMP, :]), bc(cosT[0:NCMP, 4, None, :], [NCMP, GROUPS, HD]),
                                       ALU.mult))
            own.link(dve.tensor_tensor(v3(krs), v3(kcn[0:NCMP, :])[:, :, ::-1, :],
                                       bc(sinT[0:NCMP, 4, None, :].rearrange("p h (a d) -> p h a d", a=2),
                                          [NCMP, GROUPS, 2, 32]), ALU.mult))
            kc_add(dve.tensor_tensor, v2(krp), v2(krs))
            dve.wait_ge(kc_tr, 1)
            own.tell(dve.tensor_copy(kcT[:, 0:NCMP], TB[0][:, 0:NCMP]), kcT_ready)

            def conv(ct):
                src = tile_in("xin", ct)
                evacuated(dve, G["cg"].tiles[ct])
                own.tell(dve.tensor_tensor(zT[:, ct, 2:S + 2], zT[:, ct, 2:S + 2], src[:, :], ALU.mult), dense_v)
                w = lambda k: gcol[:, COL["conv_w"] + 4 * k + ct:COL["conv_w"] + 4 * k + ct + 1]
                own.link(dve.tensor_scalar(qbuf[:, 0, :], zT[:, ct, 0:S], w(0), None, ALU.mult))
                for k in (1, 2):
                    own.link(dve.scalar_tensor_tensor(out=qbuf[:, 0, :], in0=zT[:, ct, k:S + k], scalar=w(k),
                                                      in1=qbuf[:, 0, :], op0=ALU.mult, op1=ALU.add))
                evacuated(dve, G["bg"].tiles[ct])
                own.tell(dve.tensor_tensor(bgT[:, ct, :], qbuf[:, 0, :], bgT[:, ct, :], ALU.mult), conv_y)

            def conv_norm():
                dve.wait_ge(conv_rms, 1)
                inv = stage[:, 0, 0:S]
                own.link(dve.reciprocal(inv, inv))

                def scaled(ct):
                    g = gcol[:, COL["norm_conv_out"] + ct:COL["norm_conv_out"] + ct + 1]
                    own.tell(dve.scalar_tensor_tensor(out=qbuf[:, ct % 2, :], in0=bgT[:, ct, :], scalar=g, in1=inv,
                                                      op0=ALU.mult, op1=ALU.mult), conv_q)
                scaled(0)
                for ct in range(4):
                    if ct < 3:
                        scaled(ct + 1)
                    dve.wait_ge(conv_hi, ct + 1)
                    own.tell(dve.tensor_tensor(xTl[:, ct, :], qbuf[:, ct % 2, :], xTh[:, ct, :].bitcast(F32),
                                               ALU.subtract), conv_lo)

            evacuated(dve, G["gates"].tiles[0])
            for c in range(ST):
                dve.wait_ge(c_scores, 2 * c + 2)
                if c:
                    dve.wait_ge(c_exp, c)
                for g in range(GROUPS):
                    own.link(dve.tensor_tensor(scb[:, 4 * g:4 * g + 4, :],
                                               SB[g][:, 0:4 * NCMP].rearrange("p (h j) -> p h j", h=4),
                                               bc(cmask[:, c, None, :], [P, 4, NCMP]), ALU.add))
                own.link(dve.tensor_reduce(small[:, 16:24], scb[:, :, :], X, ALU.max))
                own.tell(dve.tensor_tensor(scb[:, :, :], scb[:, :, :], bc(small[:, 16:24, None], [P, 8, NCMP]),
                                           ALU.subtract), c_shift)
                dve.wait_ge(c_exp, c + 1)
                own.link(dve.tensor_reduce(small[:, 24:32], pc[:, c % 2, :, 0:NCMP], X, ALU.add))
                own.link(dve.reciprocal(small[:, 24:32], small[:, 24:32]))
                own.link(dve.tensor_tensor(small[:, 32:40], small[:, 24:32], gates[:, c, 0:24:3], ALU.mult))
                if c == 0:
                    own.link(dve.tensor_scalar(small[:, 32:40], small[:, 32:40], small[:, 95:96], None, ALU.mult))
                dve.wait_ge(c_tr, c + 1)
                if c:
                    dve.wait_ge(c_out, c)
                own.tell(dve.tensor_copy(pcT[:, :, :], TB[0][:, 0:2 * P].rearrange("p (g q) -> p g q", g=2)), c_trin)
                dve.wait_ge(c_out, c + 1)
                own.tell(dve.tensor_tensor(yatt[:, c, :].rearrange("p (h d) -> p h d", h=8),
                                           bank[3][:, :].rearrange("p (h d) -> p h d", h=8),
                                           bc(small[:, 32:40, None], [P, 8, HD]), ALU.mult), c_used)

            for s in range(len(ITEMS) + 2):
                if s < len(ITEMS):
                    qt = ITEMS[s][0]
                    n = (qt + 1) * P
                    if s >= 2:
                        dve.wait_ge(pt_done, 2 * s - 2)
                    for br in range(2):
                        dve.wait_ge(s_done, 2 * s + br + 1)
                        own.tell(dve.tensor_tensor_reduce(
                            out=prob[:, s % 2, br, 0:n], in0=SB[br][:, 0:n], in1=causal[:, 512 - n:512], scale=1.0,
                            scalar=-3e38, op0=ALU.add, op1=ALU.max, accum_out=small[:, 44 + br:45 + br]), s_taken)
                    own.tell(dve.tensor_scalar(small[:, 4 * (s % 2):4 * (s % 2) + 2], small[:, 44:46], -HD ** -0.5,
                                               None, ALU.mult), s_max)
                if 1 <= s <= len(ITEMS):
                    i = s - 1
                    k = ITEMS[i][0] + 1
                    dve.wait_ge(pt_done, 2 * i + 2)
                    if i >= 2:
                        dve.wait_ge(pv_done, i - 1)
                    own.tell(dve.tensor_copy(probT[:, i % 2, 1, 0:k, :],
                                             TB[1][:, 0:k * P].rearrange("p (k q) -> p k q", k=k)), pt_v)
                if s >= 2:
                    i = s - 2
                    qt, g, t = ITEMS[i]
                    hd = PER_GROUP * g + t
                    den = small[:, 8 + 2 * (i % 4):10 + 2 * (i % 4)]
                    dve.wait_ge(s_exp, 2 * i + 2)
                    own.link(dve.reciprocal(small[:, 46:48], den))
                    own.link(dve.tensor_tensor(small[:, 48:50], small[:, 46:48], gates[:, qt, 3 * hd + 1:3 * hd + 3],
                                               ALU.mult))
                    dve.wait_ge(pv_done, i + 1)
                    y = yatt[:, qt, hd * HD:(hd + 1) * HD]
                    for br in range(2):
                        ins = dve.scalar_tensor_tensor(out=y, in0=bank[3][:, br * HD:(br + 1) * HD],
                                                       scalar=small[:, 48 + br:49 + br], in1=y,
                                                       op0=ALU.mult, op1=ALU.add)
                        own.tell(ins, o_taken) if br else own.link(ins)
                if s >= 9 and s % 2 and s < 17:
                    conv((s - 9) // 2)
                if s == CONV_AT + 1:
                    conv_norm()
                if s == MEM_AT + 1:
                    xn("mem", 0, D)
                    xn("mem", 1, D)
                if s == MEM_AT + 2:
                    ql("mem", 0)
                    ql("mem", 1)
            norm("att", ST, 512)

            def post(yname, j, gains):
                k = STATS.index((yname, j))
                dve.wait_ge(rms_done, k + 1)
                dve.wait_ge(gpost_in, 16 * gains)
                own.link(dve.reciprocal(rms[:, k:k + 1], rms[:, k:k + 1]))
                own.link(dve.scalar_tensor_tensor(out=ynat[:, j, :], in0=ynat[:, j, :], scalar=rms[:, k:k + 1],
                                                  in1=gpost[:, :], op0=ALU.mult, op1=ALU.mult))
                own.tell(dve.tensor_tensor(h[:, j, :], h[:, j, :], ynat[:, j, :], ALU.add), h_ready)

            def staggered(name, j):
                if j:
                    xn(name, j - 1, D)
                if j >= 2:
                    ql(name, j - 2)
                if j == 3:
                    xn(name, 3, D)
                    ql(name, 2)
                    ql(name, 3)

            for j in range(ST):
                post("yo", j, 1)
                staggered("hx", j)

            def attention(scores, mx, exp_, normed, tr, pts, outs, prob_, probT_, scale, items, final):
                for it in range(items):
                    c = it % 2
                    dve.wait_ge(scores, it + 1)
                    own.link(dve.tensor_reduce(small[:, 6:7], SB[c][:, 0:MEM], X, ALU.max))
                    if it >= 2:
                        dve.wait_ge(exp_, it - 1)
                    own.tell(dve.tensor_scalar(small[:, c:c + 1], small[:, 6:7], -scale, None, ALU.mult), mx)
                    dve.wait_ge(exp_, it + 1)
                    own.link(dve.reciprocal(small[:, 4 + c:5 + c], small[:, 2 + c:3 + c]))
                    own.tell(dve.tensor_scalar(prob_[:, c, :], prob_[:, c, :], small[:, 4 + c:5 + c], None, ALU.mult),
                             normed)
                    if it % 4 == 0 and it:
                        copy_t(it // 4 - 1, tr, pts, outs, probT_)
                    if it % 4 == 2 and it > 4:
                        final(it // 4 - 1)
                copy_t(items // 4 - 1, tr, pts, outs, probT_)
                final(items // 4 - 1)

            def copy_t(hd, tr, pts, outs, probT_):
                sem_out, per_head = outs
                dve.wait_ge(tr, ST * (hd + 1))
                if hd:
                    dve.wait_ge(sem_out, per_head * hd)
                own.tell(dve.tensor_copy(probT_[:, 1, :], TB[1][:, :]), pts)

            def x_low(hd):
                for dt in range(2):
                    dve.wait_ge(x_hi, 2 * hd + dt + 1)
                    own.tell(dve.tensor_tensor(oxTl[:, 2 * hd + dt, :], bank[2 + dt][:, :],
                                               oxTh[:, 2 * hd + dt, :].bitcast(F32), ALU.subtract), x_lo)
            attention(x_scores, x_max, x_exp, x_norm, x_tr, x_ptv, (x_out, 2), xprob, xprobT, XD ** -0.5, XH * ST,
                      x_low)
            for j in range(ST):
                post("yx", j, 2)
                staggered("hf", j)

            ht = 0

            def hid_low():
                dve.wait_ge(hid_hi, ht + 1)
                k = ht % 8 if ht < 22 else (ht - 22) % 8
                own.tell(dve.tensor_tensor(hidl[:, k, :], qbuf[:, ht % 2, :], hidh[:, k, :].bitcast(F32),
                                           ALU.subtract), hid_lo)

            for s in range(3):
                for c in G[f"gu{s}"].chunks:
                    evacuated(dve, c.tiles[0][0])
                    n = c.tiles[1][0]
                    dve.wait_ge(dense_done, n + 1)
                    own.tell(dve.tensor_tensor(qbuf[:, ht % 2, :], silu[:, ht % 2, :], tile_bank(n)[:, :], ALU.mult),
                             hid_q)
                    hid_low()
                    ht += 1
                if s == 0:
                    continue
                for t in range(8):
                    if s == 1 and t == 0:
                        evacuated(dve, G["down0"].tiles[7])
                    half, j = t // 4, t % 4
                    src = tile_in(f"down{s}", t)
                    y = ynat[:, j, 512 * half:512 * half + 512]
                    own.tell(dve.tensor_tensor(y, y, src[:, :], ALU.add), dense_v)
                    if s == 2 and half and j:
                        post("yf", j - 1, 3)
                        staggered("h2", j - 1)

            post("yf", 3, 3)
            staggered("h2", 3)

            xn("mem2", 0, D)
            xn("mem2", 1, D)
            ql("mem2", 0)
            ql("mem2", 1)
            R = gate_rows
            evacuated(dve, G["if"].tiles[0])
            dve.wait_ge(ifb_in, 64)
            own.link(dve.tensor_scalar(R[:, 0, :], R[:, 0, :], small[0:36, 88:89], None, ALU.add))
            own.link(dve.tensor_scalar(R[:, 1, :], R[:, 1, :], small[0:36, 89:90], None, ALU.add))
            own.tell(dve.scalar_tensor_tensor(out=R[:, 2, :], in0=R[:, 1, :], scalar=-1.0, in1=R[:, 1, :],
                                              op0=ALU.mult, op1=ALU.max), gr_lin)
            own.link(dve.memset(R[:, 3:5, :], 0.0))
            for ct in range(4):
                w = lambda k: gcol[:, COL["conv_w_2"] + 4 * k + ct:COL["conv_w_2"] + 4 * k + ct + 1]
                cb = gcol[:, COL["conv_b_2"] + ct:COL["conv_b_2"] + ct + 1]
                evacuated(dve, G["qk2"].tiles[ct])
                own.link(dve.tensor_scalar(qkT[:, ct, :], qkc[:, ct, 0:S], w(0), cb, ALU.mult, ALU.add))
                for k in range(1, 5):
                    ins = dve.scalar_tensor_tensor(out=qkT[:, ct, :], in0=qkc[:, ct, k:S + k], scalar=w(k),
                                                   in1=qkT[:, ct, :], op0=ALU.mult, op1=ALU.add)
                    own.tell(ins, qk_conv) if k == 4 else own.link(ins)
            dve.wait_ge(gr_ln, 1)
            own.link(dve.scalar_tensor_tensor(out=R[:, 1, :], in0=R[:, 1, :], scalar=0.0, in1=R[:, 2, :],
                                              op0=ALU.min, op1=ALU.subtract))
            fw, bw = slice(0, 4), slice(32, 36)
            for ps, step in ((fw, 1), (bw, -1)):
                own.link(dve.tensor_tensor_scan(R[ps, 3, ::step], bc(ones[ps, 0:1], [4, S]), R[ps, 1, ::step], 0.0,
                                                ALU.mult, ALU.add))
            own.link(dve.tensor_tensor(R[:, 0, :], R[:, 0, :], R[:, 3, :], ALU.subtract))
            for ps, step in ((fw, 1), (bw, -1)):
                own.link(dve.tensor_tensor_scan(R[ps, 4, ::step], R[ps, 0, ::step], R[ps, 0, ::step], -3e38,
                                                ALU.max, ALU.max))
            own.tell(dve.tensor_scalar(neg_max, R[:, 4, :], -1.0, None, ALU.mult), gr_neg)
            own.tell(dve.tensor_tensor(R[:, 5, :], R[:, 3, :], R[:, 4, :], ALU.add), gr_max)
            dve.wait_ge(gr_tr, 1)
            own.tell(dve.tensor_copy(acol[:, :, :, :], TB[0][:, 0:8 * 36].rearrange("p (a t r) -> p a t r", a=2, t=ST)),
                     gr_col)

            dve.wait_ge(gain2_in, 64)

            def head_norm(t):
                if t < 4:
                    evacuated(dve, G["naqk"].tiles[t])
                    src, heads, d, gain, scaled = stage[:, t % 2, 0:S], 16, ND, na_gain, 8
                elif t < 8:
                    evacuated(dve, G["navq"].tiles[t - 4])
                    src, heads, d, gain, scaled = navq[:, t - 4, 256:512], 4, MD, mem_gain[:, 0:4, :], 4
                else:
                    evacuated(dve, G["memkv"].tiles[t - 8])
                    src, heads, d, gain, scaled = memkv[:, t - 8, 0:256], 4, MD, mem_gain[:, 4:8, :], 0
                if t >= 2:
                    dve.wait_ge(n_tr, t - 1)
                v = lambda z: z.rearrange("p (h d) -> p h d", h=heads)
                dst = stage[:, t % 2, S:S + heads * d]
                r = small[:, 16:16 + heads]
                own.link(dve.tensor_tensor(dst, src, src, ALU.mult))
                own.tell(dve.tensor_reduce(r, v(dst), X, ALU.add), n_raw)
                dve.wait_ge(n_norm, t + 1)
                own.link(dve.reciprocal(r, r))
                if scaled:
                    own.link(dve.tensor_scalar(small[:, 16:16 + scaled], small[:, 16:16 + scaled], d ** -0.5, None,
                                               ALU.mult))
                own.link(dve.tensor_tensor(v(dst), v(src), bc(r[:, :, None], [P, heads, d]), ALU.mult))
                own.tell(dve.tensor_tensor(v(dst), v(dst), gain, ALU.mult), n_in)

            def head_copy(t):
                dve.wait_ge(n_tr, t + 1)
                dst, j, n = (naT, t, 4) if t < 4 else (qmT, t - 4, 2) if t < 8 else (kmT, t - 8, 2)
                src = TB[t % 2][:, 0:n * P].rearrange("p (k t) -> p k t", k=n)
                to = dst[:, :, j * P:(j + 1) * P]
                if t < 4:
                    own.link(dve.tensor_copy(to[:, 0:2, ::-1], src[:, 0:2, :]))
                    to, src = to[:, 2:4, :], src[:, 2:4, :]
                own.tell(dve.tensor_copy(to, src), n_copied)
            for t in range(10):
                head_norm(t)
                if t:
                    head_copy(t - 1)
            head_copy(9)

            def l_result(it):
                d, hd = it // LH, it % LH
                lo = bank[2], bank[3]
                dve.wait_ge(l_out, it + 1)
                den, tmp = small[:, 52:56], small[:, 56:60]
                for b in range(2):
                    own.link(dve.tensor_copy(tmp[:, 2 * b:2 * b + 2], lo[b][:, 0:2 * (LV + 1)].rearrange(
                        "p (t v) -> p t v", t=2)[:, :, LV]))
                own.link(dve.scalar_tensor_tensor(out=den, in0=tmp, scalar=-1.0, in1=tmp, op0=ALU.mult, op1=ALU.max))
                own.link(dve.tensor_tensor(den, den, acol[:, 1, :, 32 * d + hd], ALU.max))
                own.link(dve.reciprocal(den, den))
                for tt in range(ST):
                    o = lo[tt // 2][:, (tt % 2) * (LV + 1):(tt % 2) * (LV + 1) + LV]
                    y = hsum[:, tt, hd * LV:(hd + 1) * LV]
                    r = den[:, tt:tt + 1]
                    if d == 0:
                        ins = dve.tensor_scalar(y, o, r, None, ALU.mult)
                    else:
                        ins = dve.scalar_tensor_tensor(out=y, in0=o, scalar=r, in1=y, op0=ALU.mult, op1=ALU.add)
                    own.tell(ins, l_used) if tt == ST - 1 else own.link(ins)

            for it in range(2 * LH + 1):
                if it < 2 * LH:
                    d, hd = it // LH, it % LH
                    dve.wait_ge(l_bcin, it + 1)
                    if it >= 2:
                        dve.wait_ge(l_out, it - 1)
                    for si in range(ST):
                        off, n, t0 = span(d, si)
                        a_s = acol[:, 0, si, 32 * d + hd:32 * d + hd + 1]
                        own.tell(dve.tensor_scalar(decay[:, it % 2, off:off + n], maxb[:, it % 2, t0:t0 + n], a_s, 0.0,
                                                   ALU.add, ALU.min), l_shift)
                    for si in range(ST):
                        off, n, t0 = span(d, si)
                        k = ST * it + si
                        dve.wait_ge(l_scores, k + 1)
                        dve.wait_ge(l_exp, k + 1)
                        own.tell(dve.scalar_tensor_tensor(out=decay[:, it % 2, off:off + n], in0=SB[k % 2][:, 0:n],
                                                          scalar=LQ ** -0.5, in1=decay[:, it % 2, off:off + n],
                                                          op0=ALU.mult, op1=ALU.mult), l_mul)
                if it:
                    l_result(it - 1)

            for s in range(NH * ST + 1):
                if s < NH * ST:
                    hd, qt = s // ST, s % ST
                    dve.wait_ge(b_masked, 2 * (hd + 1))
                    dve.wait_ge(a_scores, s + 1)
                    if s >= 2:
                        dve.wait_ge(a_tr, s - 1)
                    own.tell(dve.tensor_tensor_reduce(
                        out=nprob[:, s % 2, :], in0=SB[s % 2][:, :],
                        in1=bias2[hd % 2][:, 7 - 2 * qt:15 - 2 * qt, :].rearrange("p k c -> p (k c)"), scale=1.0,
                        scalar=-3e38, op0=ALU.add, op1=ALU.max, accum_out=small[:, 4:5]), a_taken)
                    own.tell(dve.tensor_scalar(small[:, s % 2:s % 2 + 1], small[:, 4:5], -1.0, None, ALU.mult), a_max)
                if s >= 1 and (s - 1) % 2 == 1:
                    i = s - 1
                    dve.wait_ge(a_tr, i + 1)
                    if i >= 2:
                        dve.wait_ge(a_out, i - 1)
                    own.tell(dve.tensor_copy(nprobT[:, 1, :, ::-1], TB[1][:, :].rearrange("p (k q) -> p k q", k=ST)),
                             a_ptv)
            for e in range(2):
                dve.wait_ge(spill_out[e], 16 * 12)
            for j in range(ST):
                i = ntile["hm", j]
                y = hsum[:, j, :]
                v = lambda z: z.rearrange("p (h d) -> p h d", h=LH)
                dve.wait_ge(tr_done, NT[i - 2][3] + NT[i - 2][2])
                own.link(dve.tensor_tensor(stage[:, i % 2, S:2 * S], y, y, ALU.mult))
                own.tell(dve.tensor_reduce(small[:, 16:20], v(stage[:, i % 2, S:2 * S]), X, ALU.add), n_raw)
                dve.wait_ge(n_norm, 10 + j + 1)
                own.link(dve.reciprocal(small[:, 16:20], small[:, 16:20]))
                own.link(dve.tensor_tensor(v(stage[:, i % 2, 0:S]), v(y), bc(small[:, 16:20, None], [P, LH, LV]),
                                           ALU.mult))
                own.tell(dve.tensor_tensor(stage[:, i % 2, 0:S], stage[:, i % 2, 0:S], og[:, j, :], ALU.mult), xn_ready)
                if j:
                    ql("hm", j - 1)
            ql("hm", 3)
            dve.wait_ge(a_den, 1)
            own.link(dve.reciprocal(small[:, 32:64], SB[0][:, 0:NH * ST]))
            for qt in range(ST):
                o = bank[2 + qt // 2][:, (qt % 2) * 256:(qt % 2) * 256 + 256].rearrange("p (h d) -> p h d", h=NH)
                r = small[:, 32:64].rearrange("p (h q) -> p h q", q=ST)[:, :, qt:qt + 1]
                own.tell(dve.tensor_tensor(hna[:, qt, :].rearrange("p (h d) -> p h d", h=NH), o, bc(r, [P, NH, ND]),
                                           ALU.mult), xn_ready)
            for j in range(ST):
                ql("hna", j)

            attention(m_scores, m_max, m_exp, m_norm, m_tr, m_ptv, (m_out, 1), mprob, mprobT, 1.0, MH * ST,
                      lambda hd: None)
            for t in range(2):
                dve.wait_ge(m_hi, t + 1)
                own.tell(dve.tensor_tensor(hmTl[:, 6 + t, :], bank[2 + t][:, :], hmTh[:, 6 + t, :].bitcast(F32),
                                           ALU.subtract), m_lo)

            def y_low(i):
                dve.wait_ge(y_hi, i + 1)
                own.tell(dve.tensor_tensor(yTl[:, i, :], qbuf[:, i % 2, :], yTh[:, i, :].bitcast(F32), ALU.subtract),
                         y_lo)

            for cp in range(4):
                for m in range(2):
                    dve.wait_ge(gate_ready, 2 * cp + m + 1)
                    for b in range(3):
                        src = tile_in(f"proj2_{cp}", 3 * m + b)
                        dst = qbuf[:, m, :] if b == 0 else stage[:, 0, (b - 1) * S:b * S]
                        own.tell(dve.tensor_tensor(dst, sg[:, m, b, :], src[:, :], ALU.mult), dense_v)
                    own.link(dve.tensor_tensor(qbuf[:, m, :], qbuf[:, m, :], stage[:, 0, 0:S], ALU.add))
                    own.tell(dve.tensor_tensor(qbuf[:, m, :], qbuf[:, m, :], stage[:, 0, S:2 * S], ALU.add), y_q)
                    if 2 * cp + m:
                        y_low(2 * cp + m - 1)
            y_low(7)

            def onto_h(name, t):
                half, j = t // 4, t % 4
                src = tile_in(name, t)
                y = h[:, j, 512 * half:512 * half + 512]
                own.tell(dve.tensor_tensor(y, y, src[:, :], ALU.add), dense_v)
            for t in range(4):
                onto_h("out2", t)
            for j in range(ST):
                onto_h("out2", 4 + j)
                staggered("h4", j)
            for s in range(4):
                for n in G[f"up{s}"].tiles:
                    evacuated(dve, n)
                    own.tell(dve.tensor_tensor(qbuf[:, ht % 2, :], silu[:, ht % 2, :], silu[:, ht % 2, :], ALU.mult),
                             hid_q)
                    hid_low()
                    ht += 1
                for t in range(8):
                    onto_h(f"dn{s}", t)

        @block.tensor
        def _(pe):
            def transpose_blocks(dst, src, n, width=P):
                for b in range(n):
                    mm = pe.transpose(dst[:, b * P:b * P + P], src[:, b * width:(b + 1) * width], ident[:, :])
                return mm

            def turn(phase, j):
                i = ntile[phase, j]
                pe.wait_ge(xn_ready, i + 1)
                for b in range(NT[i][2]):
                    r = NT[i][3] + b
                    if r >= 2:
                        pe.wait_ge(q_ready, r - 1)
                    src = hna[:, j, :] if phase == "hna" else stage[:, i % 2, 512 * b:512 * b + 512]
                    transpose_blocks(TB[r % 2], src, 2 if phase == "hna" else 4).then_inc(tr_done, 1)

            def three(ps, ah, al, bh, bl, first, last):
                pe.matmul(ps, ah, bh, start=first, stop=False)
                pe.matmul(ps, ah, bl, start=False, stop=False)
                return pe.matmul(ps, al, bh, start=False, stop=last)

            def dense(name, xh, xl, ntok=S, low=None, base=0):
                for c in G[name].chunks:
                    if low:
                        pe.wait_ge(low, base + c.kts[-1] + 1)
                    for k in range(len(c.tiles)):
                        product(c, k, xh, xl, ntok)

            def product(c, k_tile, xh, xl, ntok=S, piece=None):
                g = c.group
                if k_tile == 0 and not piece and c.split:
                    pe.wait_ge(wh_done, split_rank[c.n])
                    pe.wait_ge(wl_done, split_rank[c.n])
                elif k_tile == 0 and not piece:
                    pe.wait_ge(raw_in[c.n % RAW], loaded[c.n])
                if c.split:
                    r = (split_rank[c.n] - 1) % HL
                    width = len(c.kts) * c.cols
                    ch = wh[:, r, 0:width].rearrange("p (k n) -> p k n", k=len(c.kts))
                    cl = wl[:, r, 0:width].rearrange("p (k n) -> p k n", k=len(c.kts))
                else:
                    craw = raw[:, c.n % RAW, :].rearrange("p (i n) -> p i n", n=CHID)
                n, first, last, m, ks = c.tiles[k_tile]
                if first and not piece and plan.tiles[n][1] is not None:
                    evacuated(pe, plan.tiles[n][1])
                ps = tile_bank(n)
                if g.mode == "G":
                    for j in range(ST):
                        for k in range(8):
                            js = slice(j * P, (j + 1) * P)
                            mm = three(ps[:, j * 24:(j + 1) * 24], xh[:, k, js], xl[:, k, js], ch[:, k, :],
                                       cl[:, k, :], k == 0, k == 7)
                elif g.mode == "C":
                    f = xh
                    for k, i in enumerate(ks):
                        mm = pe.matmul(ps[:, 0:GROUPS * NCMP], craw[:, k, m * P:(m + 1) * P], f[:, i, :],
                                       start=first and k == 0, stop=last and k == len(ks) - 1)
                elif g.mode == "N":
                    for q, k in enumerate(ks):
                        js = slice(m * P, (m + 1) * P)
                        mm = three(ps[:, :], xh[:, k, js], xl[:, k, js], ch[:, q, :], cl[:, q, :],
                                   first and q == 0, last and q == len(ks) - 1)
                else:
                    for q, k in enumerate(ks):
                        if piece not in (None, q):
                            continue
                        cs = slice(m * P, (m + 1) * P)
                        mm = three(ps[:, 0:ntok], ch[:, k, cs], cl[:, k, cs], xh[:, k, 0:ntok],
                                   xl[:, k, 0:ntok], q == 0, q == len(ks) - 1)
                if piece not in (None, len(ks) - 1):
                    return
                if last:
                    mm.then_inc(dense_done, 1)
                elif k_tile == len(c.tiles) - 1:
                    mm.then_inc(chunk_used, 1)

            def x_pieces(ps):
                for c, k, q in ps:
                    if c.group.name == "kx":
                        product(c, k, memTh, memTl, MEM, piece=q)
                    else:
                        product(c, k, xTh, xTl, piece=q)

            def gate_pieces(u0, n):
                for u in range(u0, u0 + n):
                    product(*gate_tiles[u // 8], xTh, xTl, piece=u % 8)

            def turned_ready(phase, ntok):
                i = ntile[phase, ntok - 1]
                pe.wait_ge(lo_done, NT[i][3] + NT[i][2])

            def low_all(phase):
                turned_ready(phase, ST if phase not in ("mem", "mem2") else MT)

            pe.wait_ge(const_ready, 2)
            pe.wait_ge(rows_in_s, 16 * len(VECS))
            pe.wait_ge(pe_in_s, 64)
            pe.transpose(SB[1][:, 0:NCOL], rows_in[:, :], ident[0:NCOL, 0:NCOL])
            for i in range(2):
                mm = pe.transpose(SB[1][:, P + CMP * i:P + CMP * (i + 1)], pe_in[:, i, :, :].rearrange(
                    "p g d -> p (g d)"), ident[0:CMP, 0:CMP])
            mm.then_inc(vec_tr, 1)
            for j in range(ST):
                turn("x", j)
            low_all("x")

            def turn_rot(r):
                pe.wait_ge(rot_ready, r + 1)
                if r >= 2:
                    pe.wait_ge(qkT_ready, r - 1)
                transpose_blocks(TB[r % 2], qrot[:, r % 2, :], 4 if r < 4 else 2).then_inc(rot_tr, 1)
            dense("q", xTh, xTl)
            dense("kv", xTh, xTl)
            turn_rot(0), turn_rot(1)
            dense("kcvc", xTh, xTl)
            turn_rot(2), turn_rot(3)
            dense("gates", xTh, xTl)
            turn_rot(4), turn_rot(5)
            for i, (name, f) in enumerate((("cmp_kc", fk), ("cmp_vc", fv))):
                evacuated(pe, G["kcvc"].tiles[i])
                dense(name, f, None)
                if i == 0:
                    turn_rot(6), turn_rot(7)
            pe.wait_ge(w2_in, 32)
            evacuated(pe, G["cmp_vc"].tiles[1])
            pe.wait_ge(qkT_ready, 8)
            for g in range(GROUPS):
                for m in range(2):
                    pe.matmul(TB[0][0:NCMP, g * HD:(g + 1) * HD], hidk[:, m, g * NCMP:(g + 1) * NCMP], w2k[:, m, :],
                              start=m == 0, stop=m == 1)
            for g in range(GROUPS):
                for m in range(2):
                    mm = pe.matmul(TB[1][:, g * HD:(g + 1) * HD], hidv[:, m, g, :, :].rearrange("p r j -> p (r j)"),
                                   w2v[:, m, :], start=m == 0, stop=m == 1)
            mm.then_inc(cmp_kv, 1)
            pe.wait_ge(kc_rot, 1)
            pe.transpose(TB[0][:, 0:NCMP], kcr[0:NCMP, :], ident[0:NCMP, 0:NCMP]).then_inc(kc_tr, 1)
            pe.wait_ge(kcT_ready, 1)
            pe.wait_ge(cmp_kv_in, 4)
            for c in range(ST):
                if c:
                    pe.wait_ge(c_shift, c)
                for g in range(GROUPS):
                    for t in range(PER_GROUP):
                        ps = slice(HD * g, HD * g + HD)
                        o = t * NCMP
                        mm = pe.matmul(SB[g][:, o:o + NCMP], qT[ps, t, c * P:(c + 1) * P], kcT[ps, 0:NCMP],
                                       start=True, stop=True)
                    mm.then_inc(c_scores, 1)
                x_pieces(cmp_pieces(c))
                pe.wait_ge(c_exp, c + 1)
                if c:
                    pe.wait_ge(c_trin, c)
                for g in range(GROUPS):
                    mm = pe.transpose(TB[0][:, g * P:(g + 1) * P],
                                      pc[:, c % 2, 4 * g:4 * g + 4, :].rearrange("p h j -> p (h j)"), ident[:, :])
                mm.then_inc(c_tr, 1)
                pe.wait_ge(c_trin, c + 1)
                if c:
                    pe.wait_ge(c_used, c)
                for g in range(GROUPS):
                    mm = pe.matmul(bank[3][:, g * 256:(g + 1) * 256], pcT[:, g, :],
                                   vbd[:, g, :, :].rearrange("p r d -> p (r d)"), start=True, stop=True)
                mm.then_inc(c_out, 1)
            pe.wait_ge(c_used, ST)

            for s in range(len(ITEMS) + 2):
                if s == CONV_AT:
                    for ct in range(4):
                        pe.wait_ge(conv_sq, ct + 1)
                        mm = pe.matmul(bank[2][:, :], ones[:, :], stage[:, ct // 2, (ct % 2) * S:(ct % 2) * S + S],
                                       start=ct == 0, stop=ct == 3)
                    mm.then_inc(conv_ss, 1)
                if s == MEM_AT + 3:
                    pe.wait_ge(pt_a, s - 1)
                    pe.wait_ge(pt_v, s - 1)
                    turn("mem", 0)
                    turn("mem", 1)
                    pe.wait_ge(q_ready, NT[ntile["mem", 1]][3] + 2)
                if s < len(ITEMS):
                    qt, g, t = ITEMS[s]
                    ps = slice(HD * g, HD * g + HD)
                    for br in range(2):
                        if s:
                            pe.wait_ge(s_taken, 2 * s - 1 + br)
                        n = (qt + 1) * P
                        pe.matmul(SB[br][:, 0:n], qT[ps, t, qt * P:(qt + 1) * P], kT[ps, br, 0:n],
                                  start=True, stop=True).then_inc(s_done, 1)
                    if s == KX_AT:
                        low_all("mem")
                    x_pieces(item_pieces(s))
                if 1 <= s <= len(ITEMS):
                    i = s - 1
                    k = ITEMS[i][0] + 1
                    for br, evac_sem in ((0, pt_a), (1, pt_v)):
                        pe.wait_ge(s_exp, 2 * i + br + 1)
                        if i:
                            pe.wait_ge(evac_sem, i)
                        transpose_blocks(TB[br], prob[:, i % 2, br, :], k).then_inc(pt_done, 1)
                if s >= 2:
                    i = s - 2
                    qt, g, t = ITEMS[i]
                    pe.wait_ge(pt_a, i + 1)
                    pe.wait_ge(pt_v, i + 1)
                    if i:
                        pe.wait_ge(o_taken, i)
                    for br in range(2):
                        for k in range(qt + 1):
                            mm = pe.matmul(bank[3][:, br * HD:(br + 1) * HD], probT[:, i % 2, br, k, :],
                                           kvn[:, k, 256 * br + P + HD * g:256 * br + P + HD * g + HD],
                                           start=k == 0, stop=k == qt)
                    mm.then_inc(pv_done, 1)
            pe.wait_ge(conv_lo, 4)
            for i, c in enumerate(G["out"].chunks):
                if i == 1:
                    low_all("att")
                for k in range(ST):
                    if i == 0 and k == 3:
                        pe.wait_ge(o_taken, len(ITEMS))
                    product(c, k, xTh, xTl)
                    if i == 0:
                        turn("att", k)
            for i, c in enumerate(G["vx"].chunks):
                for k in range(2):
                    product(c, k, memTh, memTl)
                if i:
                    turn("hx", i - 1)
            turn("hx", 3)
            low_all("hx")
            x_pieces(pieces("qx")[0:16])

            evacuated(pe, G["out"].tiles[-1])
            evacuated(pe, G["vx"].tiles[-1])
            for it in range(XH * ST + 2):
                if it < XH * ST:
                    hd, qt = it // ST, it % ST
                    if qt == 0:
                        evacuated(pe, G["qx"].tiles[2 * hd + 1])
                    if it >= 2:
                        pe.wait_ge(x_exp, it - 1)
                    for k in range(2):
                        mm = pe.matmul(SB[it % 2][:, 0:MEM], qxT[:, 2 * hd + k, qt * P:(qt + 1) * P],
                                       kxT[:, 2 * hd + k, :], start=k == 0, stop=k == 1)
                    mm.then_inc(x_scores, 1)
                    x_pieces(head_pieces(it))
                    if it in (12, 14):
                        if it == 12:
                            pe.wait_ge(x_lo, 4)
                        product(G["ox"].chunks[0], (it - 12) // 2, oxTh, oxTl)
                if 1 <= it <= XH * ST:
                    i = it - 1
                    hd, qt = i // ST, i % ST
                    pe.wait_ge(x_norm, i + 1)
                    if qt == 0 and hd:
                        pe.wait_ge(x_pta, hd)
                        pe.wait_ge(x_ptv, hd)
                    for k in range(2):
                        mm = pe.transpose(TB[k][:, qt * P:(qt + 1) * P], xprob[:, i % 2, k * P:(k + 1) * P], ident[:, :])
                    mm.then_inc(x_tr, 1)
                if it % 4 == 1 and it > 1:
                    hd = it // 4 - 1
                    pe.wait_ge(x_pta, hd + 1)
                    pe.wait_ge(x_ptv, hd + 1)
                    for dt in range(2):
                        if hd:
                            pe.wait_ge(x_lo, 2 * (hd - 1) + dt + 1)
                        for k in range(2):
                            o = hd * XD + dt * P
                            mm = pe.matmul(bank[2 + dt][:, :], vx[:, k, o:o + P], xprobT[:, k, :],
                                           start=k == 0, stop=k == 1)
                        mm.then_inc(x_out, 1)
            pe.wait_ge(x_lo, 8)
            for i, c in enumerate(G["ox"].chunks):
                for k in range(2 if i == 0 else 0, ST):
                    product(c, k, oxTh, oxTl)
            for j in range(ST):
                turn("hf", j)
            low_all("hf")

            ht = 0
            for s in range(3):
                dense(f"gu{s}", xTh, xTl)
                dense(f"down{s}", hidh, hidl, low=hid_lo, base=ht)
                ht += len(G[f"gu{s}"].chunks)
            for j in range(ST):
                turn("h2", j)
            low_all("h2")

            dense("if", xTh, xTl)
            for j in range(MT):
                turn("mem2", j)
            dense("qk2", xTh, xTl)
            low_all("mem2")
            dense("memkv", mem2Th, mem2Tl)
            dense("v2", xTh, xTl)
            dense("o2", xTh, xTl)
            pe.wait_ge(gr_em, 1)
            for a_i, row in enumerate((0, 5)):
                for t in range(ST):
                    o = (a_i * ST + t) * 36
                    mm = pe.transpose(TB[0][:, o:o + 36], gate_rows[:, row, t * P:(t + 1) * P], ident[0:36, 0:36])
            mm.then_inc(gr_tr, 1)
            dense("naqk", xTh, xTl)

            def turn_heads(t):
                pe.wait_ge(n_in, t + 1)
                if t >= 2:
                    pe.wait_ge(n_copied, t - 1)
                if t == 0:
                    pe.wait_ge(gr_col, 1)
                transpose_blocks(TB[t % 2], stage[:, t % 2, S:2 * S], 4 if t < 4 else 2).then_inc(n_tr, 1)
            for c in G["navq"].chunks:
                for k in range(ST):
                    product(c, k, xTh, xTl)
                    if c is G["navq"].chunks[0]:
                        turn_heads(k)
            for t in range(4, 10):
                turn_heads(t)
                gate_pieces((t - 4) * H_PIECES, H_PIECES)
            pe.wait_ge(n_copied, 10)

            pe.wait_ge(qk_ready, 4)
            pe.wait_ge(gr_neg, 1)
            for n in G["navq"].tiles:
                evacuated(pe, n)
            for it in range(2 * LH + 1):
                if it < 2 * LH:
                    d, hd = it // LH, it % LH
                    row = 32 * d + hd
                    if it:
                        pe.wait_ge(l_bcin, it)
                    pe.matmul(TB[0][:, :], bc(ident[0:36, row:row + 1], [36, P]), neg_max, start=True, stop=True)\
                        .then_inc(l_bc, 1)
                    ps = slice(LQ * (hd % 2), LQ * (hd % 2) + LQ)
                    for si in range(ST):
                        off, n, t0 = span(d, si)
                        k = ST * it + si
                        if k >= 2:
                            pe.wait_ge(l_mul, k - 1)
                        pe.matmul(SB[k % 2][:, 0:n], qkT[ps, 2 + hd // 2, si * P:(si + 1) * P],
                                  qkT[ps, hd // 2, t0:t0 + n], start=True, stop=True).then_inc(l_scores, 1)
                        gate_pieces(lstm_piece(it) + (0, 4, 7, 10)[si], (4, 3, 3, 3)[si])
                if it:
                    i = it - 1
                    d, hd = i // LH, i % LH
                    pe.wait_ge(l_mask, ST * (i + 1))
                    if i:
                        pe.wait_ge(l_used, i)
                    pair = bank[2], bank[3]
                    for tt in range(ST):
                        keys = list(range(tt + 1)) if d == 0 else list(range(tt, ST))
                        for si in keys:
                            off, n, t0 = span(d, si)
                            q0 = off + tt * P - t0
                            mm = pe.matmul(pair[tt // 2][:, (tt % 2) * (LV + 1):(tt % 2 + 1) * (LV + 1)],
                                           decay[:, i % 2, q0:q0 + P], vext[:, si, hd, :],
                                           start=si == keys[0], stop=si == keys[-1])
                    mm.then_inc(l_out, 1)
            pe.wait_ge(l_used, 2 * LH)

            for s in range(NH * ST + 2):
                if s < NH * ST:
                    hd, qt = s // ST, s % ST
                    if s >= 2:
                        pe.wait_ge(a_taken, s - 1)
                    ps = slice(ND * (hd % 4), ND * (hd % 4) + ND)
                    pe.matmul(SB[s % 2][:, :], naT[ps, hd // 4, qt * P:(qt + 1) * P], naT[ps, 2 + hd // 4, :],
                              start=True, stop=True).then_inc(a_scores, 1)
                    gate_pieces(na_piece(s), A_PIECES)
                if 1 <= s <= NH * ST:
                    i = s - 1
                    pe.wait_ge(a_exp, i + 1)
                    if i >= 2:
                        pe.wait_ge((a_pta, a_ptv)[i % 2], i // 2)
                    transpose_blocks(TB[i % 2], nprob[:, i % 2, :], ST).then_inc(a_tr, 1)
                if s >= 2:
                    i = s - 2
                    hd, qt = i // ST, i % ST
                    pe.wait_ge((a_pta, a_ptv)[i % 2], i // 2 + 1)
                    o = (qt % 2) * 256 + hd * ND
                    for k in range(ST):
                        mm = pe.matmul(bank[2 + qt // 2][:, o:o + ND], nprobT[:, i % 2, k, :],
                                       navq[:, k, hd * ND:(hd + 1) * ND], start=k == 0, stop=k == ST - 1)
                    mm.then_inc(a_out, 1)
            pe.wait_ge(a_exp, NH * ST)
            pe.matmul(SB[0][:, 0:NH * ST], antident[:, :], small[:, 32:32 + NH * ST], start=True, stop=True)\
                .then_inc(a_den, 1)
            for j in range(ST):
                turn("hm", j)
            for j in range(ST):
                turn("hna", j)
            low_all("hna")

            for it in range(MH * ST + 2):
                if it < MH * ST:
                    hd, qt = it // ST, it % ST
                    if it >= 2:
                        pe.wait_ge(m_exp, it - 1)
                    ps = slice(MD * (hd % 2), MD * (hd % 2) + MD)
                    pe.matmul(SB[it % 2][:, 0:MEM], qmT[ps, hd // 2, qt * P:(qt + 1) * P], kmT[ps, hd // 2, :],
                              start=True, stop=True).then_inc(m_scores, 1)
                if 1 <= it <= MH * ST:
                    i = it - 1
                    hd, qt = i // ST, i % ST
                    pe.wait_ge(m_norm, i + 1)
                    if qt == 0 and hd:
                        pe.wait_ge(m_pta, hd)
                        pe.wait_ge(m_ptv, hd)
                    for k in range(2):
                        mm = pe.transpose(TB[k][:, qt * P:(qt + 1) * P], mprob[:, i % 2, k * P:(k + 1) * P], ident[:, :])
                    mm.then_inc(m_tr, 1)
                if it % 4 == 1 and it > 1:
                    hd = it // 4 - 1
                    pe.wait_ge(m_pta, hd + 1)
                    pe.wait_ge(m_ptv, hd + 1)
                    for k in range(2):
                        o = 256 + hd * MD
                        ps = slice(MD * (hd % 2), MD * (hd % 2) + MD)
                        mm = pe.matmul(bank[2 + hd // 2][ps, :], memkv[:, k, o:o + MD], mprobT[:, k, :],
                                       start=k == 0, stop=k == 1)
                    mm.then_inc(m_out, 1)
            pe.wait_ge(m_lo, 2)

            for cp in range(4):
                dense(f"proj2_{cp}", hmTh, hmTl)
            dense("out2", yTh, yTl, low=y_lo)
            for j in range(ST):
                turn("h4", j)
            low_all("h4")
            for s in range(4):
                dense(f"up{s}", xTh, xTl)
                dense(f"dn{s}", hidh, hidl, low=hid_lo, base=ht)
                ht += 8


INPUTS = (
    "x mem positions norm_mix_pre w_in conv_w pe_kc w1_kc w2_kc pe_vc w1_vc w2_vc norm_conv_out norm_attn_out "
    "w_out norm_mix_post norm_x_pre norm_mem w_q_x w_kv_x w_o_x norm_x_post norm_ffn_pre w_gate_up w_down "
    "norm_ffn_post mem_2 g_mix_2 w_in_2 conv_w_2 conv_b_2 b_igate_2 b_fgate_2 g_mlstm_2 w_proj_mlstm_2 g_na_q_2 "
    "g_na_k_2 rpb_2 w_proj_na_2 g_mem_2 w_mem_kv_2 g_mem_q_2 g_mem_k_2 w_proj_mem_2 w_out_2 g_ffn_2 w_up_2 "
    "w_down_2").split()


def kernel(**inputs):
    import concourse.bacc as bacc
    from concourse.bass_utils import run_bass_kernel_spmd

    nc = bacc.Bacc("TRN2", target_bir_lowering=False, num_devices=1)
    arrays, views = {}, {}
    for name in INPUTS:
        v = np.ascontiguousarray(inputs[name])
        if v.shape[0] == 1:
            v = v[0]
        arrays["in_" + name] = v
        views[name] = nc.dram_tensor("in_" + name, v.shape, mybir.dt.from_np(v.dtype), kind="ExternalInput").ap()
    out = nc.dram_tensor("out_0", (1, S, D), F32, kind="ExternalOutput").ap()
    program(nc, views, out[0])
    result = run_bass_kernel_spmd(nc, [arrays], core_ids=[0])
    return result.results[0]["out_0"]
```
